# Optimizing a Trainium2 kernel written in Bass

```python
import jax, jax.numpy as jnp
from jax import lax
import numpy as np

D_MODEL = 1024
BATCH = 1
SEQ = 2048
DEPTH = 1

D_MIX = D_MODEL
HEAD_DIM = 64
D_A = D_MIX // 4
D_B = D_MIX // 4
D_C = D_MIX // 4
D_D = D_MIX - D_A - D_B - D_C
H_B = D_B // HEAD_DIM
H_C = D_C // HEAD_DIM
CONF_KERNEL = 31
LRU_CONV = 4
LRU_C = 8.0
SHORT_CONV = 3
LORA_W = 32
LORA_A = 32
LORA_G = 64
C_COLS = 3 * D_C + LORA_W + LORA_A + LORA_G
P_IN = 2 * D_A + 2 * D_B + C_COLS + 3 * D_D
RWKV_GN_EPS = 64e-5
N_EXPERTS = 64
TOP_K = 8
N_GROUPS = 8
TOPK_GROUPS = 4
E_PER_GROUP = N_EXPERTS // N_GROUPS
D_EXPERT = 256
D_SHARED = 256
ROUTED_SCALE = 2.5
MOE_BLOCK = 128
ALPHA = (2.0 * DEPTH) ** 0.25
BETA = (8.0 * DEPTH) ** -0.25
LN_EPS = 1e-5

kernel_name = "hybrid_conv_lru_rwkv7_shortconv_moe_deepnorm"

def _layer_norm(x, g, b, eps=LN_EPS):
    xf = x.astype(jnp.float32)
    mu = jnp.mean(xf, -1, keepdims=True)
    var = jnp.mean(jnp.square(xf - mu), -1, keepdims=True)
    return ((xf - mu) * lax.rsqrt(var + eps)).astype(x.dtype) * g + b

def _causal_dwconv(x, w):
    k = w.shape[0]
    return lax.conv_general_dilated(
        x, w[:, None, :].astype(x.dtype), window_strides=(1,), padding=[(k - 1, 0)],
        dimension_numbers=("NWC", "WIO", "NWC"), feature_group_count=x.shape[-1])

def _conformer_conv(pa, conv_a, conv_a_bias, ln_a_g, ln_a_b):
    val, gate = jnp.split(pa, 2, axis=-1)
    hid = val * jax.nn.sigmoid(gate)
    hid = _causal_dwconv(hid, conv_a) + conv_a_bias
    return jax.nn.silu(_layer_norm(hid, ln_a_g, ln_a_b))

def _linear_scan(a, bx):
    def combine(left, right):
        a_l, b_l = left
        a_r, b_r = right
        return a_l * a_r, a_r * b_l + b_r
    _, h = lax.associative_scan(combine, (a, bx), axis=1)
    return h

def _rg_lru(pb, conv_b, conv_b_bias, w_rg, b_rg, w_ig, b_ig, lru_lambda):
    bsz, s, _ = pb.shape
    xb, gb = jnp.split(pb, 2, axis=-1)
    u = _causal_dwconv(xb, conv_b) + conv_b_bias
    uh = u.reshape(bsz, s, H_B, HEAD_DIM)
    r = jax.nn.sigmoid((jnp.einsum("bshd,hde->bshe", uh, w_rg).reshape(bsz, s, D_B) + b_rg).astype(jnp.float32))
    i = jax.nn.sigmoid((jnp.einsum("bshd,hde->bshe", uh, w_ig).reshape(bsz, s, D_B) + b_ig).astype(jnp.float32))
    log_a = -LRU_C * r * jax.nn.softplus(-lru_lambda.astype(jnp.float32))
    a = jnp.exp(log_a)
    mult = jnp.sqrt(-jnp.expm1(2.0 * log_a))
    h = _linear_scan(a, mult * (i * u.astype(jnp.float32)))
    return h.astype(pb.dtype) * jax.nn.gelu(gb, approximate=True)

def _rwkv7_scan(r, decay, k, v, kk, a):
    bsz, _, h, n = r.shape

    def step(state, inp):
        r_t, w_t, k_t, v_t, kk_t, a_t = inp
        s_kk = jnp.einsum("bhij,bhj->bhi", state, kk_t)
        state = (state * w_t[:, :, None, :]
                 - s_kk[..., None] * (kk_t * a_t)[:, :, None, :]
                 + v_t[..., None] * k_t[:, :, None, :])
        return state, jnp.einsum("bhij,bhj->bhi", state, r_t)

    seq_major = tuple(jnp.moveaxis(t, 1, 0) for t in (r, decay, k, v, kk, a))
    state0 = jnp.zeros((bsz, h, n, n), jnp.float32)
    _, y = lax.scan(step, state0, seq_major)
    return jnp.moveaxis(y, 0, 1)

def _rwkv7_mix(pc, mu_c, w0, w_w2, a0, w_a2, w_g2, k_k, k_a, r_k, gn_g, gn_b):
    bsz, s, _ = pc.shape
    f32 = jnp.float32
    prev = jnp.pad(pc, ((0, 0), (1, 0), (0, 0)))[:, :-1]
    xs = pc + (prev - pc) * mu_c
    r, k, v, xw, xa, xg = jnp.split(
        xs, [D_C, 2 * D_C, 3 * D_C, 3 * D_C + LORA_W, 3 * D_C + LORA_W + LORA_A], axis=-1)
    wlog = -jax.nn.softplus(-(w0 + jnp.tanh(xw) @ w_w2).astype(f32)) - 0.5
    decay = jnp.exp(-jnp.exp(wlog))
    a = jax.nn.sigmoid((a0 + xa @ w_a2).astype(f32))
    g = (jax.nn.sigmoid(xg) @ w_g2).astype(f32)
    kf = k.astype(f32)
    kk = (kf * k_k).reshape(bsz, s, H_C, HEAD_DIM)
    kk = kk * lax.rsqrt(jnp.sum(kk * kk, -1, keepdims=True) + 1e-12)
    kf = kf * (1.0 + (a - 1.0) * k_a)
    rh = r.astype(f32).reshape(bsz, s, H_C, HEAD_DIM)
    kh = kf.reshape(bsz, s, H_C, HEAD_DIM)
    vh = v.astype(f32).reshape(bsz, s, H_C, HEAD_DIM)
    y = _rwkv7_scan(rh, decay.reshape(bsz, s, H_C, HEAD_DIM), kh, vh, kk,
                    a.reshape(bsz, s, H_C, HEAD_DIM))
    mu = jnp.mean(y, -1, keepdims=True)
    var = jnp.mean(jnp.square(y - mu), -1, keepdims=True)
    y = ((y - mu) * lax.rsqrt(var + RWKV_GN_EPS)).reshape(bsz, s, D_C) * gn_g + gn_b
    bonus = jnp.sum(rh * kh * r_k, -1, keepdims=True) * vh
    y = (y + bonus.reshape(bsz, s, D_C)) * g
    return y.astype(pc.dtype)

def _short_conv(pd, conv_d):
    gb, gc, hd = jnp.split(pd, 3, axis=-1)
    return gb * _causal_dwconv(gc * hd, conv_d)

def _token_mixers(u, w_in, w_out, conv_a, conv_a_bias, ln_a_g, ln_a_b, conv_b, conv_b_bias,
                  w_rg, b_rg, w_ig, b_ig, lru_lambda, mu_c, w0, w_w2, a0, w_a2, w_g2,
                  k_k, k_a, r_k, gn_g, gn_b, conv_d):
    proj = u @ w_in
    pa, pb, pc, pd = jnp.split(
        proj, [2 * D_A, 2 * D_A + 2 * D_B, 2 * D_A + 2 * D_B + C_COLS], axis=-1)
    y_a = _conformer_conv(pa, conv_a, conv_a_bias, ln_a_g, ln_a_b)
    y_b = _rg_lru(pb, conv_b, conv_b_bias, w_rg, b_rg, w_ig, b_ig, lru_lambda)
    y_c = _rwkv7_mix(pc, mu_c, w0, w_w2, a0, w_a2, w_g2, k_k, k_a, r_k, gn_g, gn_b)
    y_d = _short_conv(pd, conv_d)
    y = jnp.concatenate([y_a, y_b, y_c, y_d], axis=-1)
    return y @ w_out

def _moe_ffn(u, w_router, e_bias, w13, w2, ws13, ws2):
    bsz, s, d = u.shape
    n = bsz * s
    h = u.reshape(n, d)
    scores = jax.nn.sigmoid((h @ w_router).astype(jnp.float32))
    biased = scores + e_bias.astype(jnp.float32)
    grp = biased.reshape(n, N_GROUPS, E_PER_GROUP)
    grp_score = jnp.sum(lax.top_k(grp, 2)[0], axis=-1)
    _, top_grp = lax.top_k(grp_score, TOPK_GROUPS)
    keep = jnp.sum(jax.nn.one_hot(top_grp, N_GROUPS, dtype=jnp.int32), axis=-2) > 0
    masked = jnp.where(jnp.repeat(keep, E_PER_GROUP, axis=-1), biased, -jnp.inf)
    _, idx = lax.top_k(masked, TOP_K)
    wts = jnp.take_along_axis(scores, idx, axis=-1)
    wts = wts / jnp.sum(wts, -1, keepdims=True) * ROUTED_SCALE
    nk = n * TOP_K
    flat_e = idx.reshape(nk)
    flat_w = wts.reshape(nk)
    flat_tok = jnp.arange(nk, dtype=jnp.int32) // TOP_K
    order = jnp.argsort(flat_e)
    se = flat_e[order]
    counts = jnp.bincount(flat_e, length=N_EXPERTS)
    padded = (counts + MOE_BLOCK - 1) // MOE_BLOCK * MOE_BLOCK
    pad_end = jnp.cumsum(padded)
    pad_start = pad_end - padded
    start = jnp.cumsum(counts) - counts
    dest = pad_start[se] + jnp.arange(nk, dtype=jnp.int32) - start[se]
    n_blocks = (nk + N_EXPERTS * (MOE_BLOCK - 1) + MOE_BLOCK - 1) // MOE_BLOCK
    cap = n_blocks * MOE_BLOCK
    buf_tok = jnp.full((cap,), n, jnp.int32).at[dest].set(flat_tok[order])
    buf_w = jnp.zeros((cap,), jnp.float32).at[dest].set(flat_w[order])
    block_start = jnp.arange(n_blocks, dtype=jnp.int32) * MOE_BLOCK
    block_e = jnp.minimum(jnp.searchsorted(pad_end, block_start, side="right"), N_EXPERTS - 1)
    h_pad = jnp.concatenate([h, jnp.zeros((1, d), h.dtype)], axis=0)

    def body(acc, blk):
        tok, wt, e = blk
        xb = jnp.take(h_pad, tok, axis=0)
        gate, up = jnp.split(xb @ w13[e], 2, axis=-1)
        y = (jax.nn.silu(gate) * up) @ w2[e]
        return acc.at[tok].add(y.astype(jnp.float32) * wt[:, None]), None

    acc0 = jnp.zeros((n + 1, d), jnp.float32)
    acc, _ = lax.scan(body, acc0, (buf_tok.reshape(n_blocks, MOE_BLOCK),
                                   buf_w.reshape(n_blocks, MOE_BLOCK), block_e))
    sg, su = jnp.split(h @ ws13, 2, axis=-1)
    shared = (jax.nn.silu(sg) * su) @ ws2
    return (acc[:n].astype(u.dtype) + shared).reshape(bsz, s, d)

def setup_inputs(seed: int = 0) -> dict:
    key = jax.random.key(seed)
    ks = iter(jax.random.split(key, 64))
    L = DEPTH

    def nrm(shape, scale):
        return jax.random.normal(next(ks), shape, jnp.float32) * scale

    def near_one(shape):
        return 1.0 + nrm(shape, 0.02)

    out = {}
    out["x"] = nrm((BATCH, SEQ, D_MODEL), 1.0)
    out["c"] = nrm((BATCH, D_MODEL), 1.0)
    out["w_mod"] = nrm((L, D_MODEL, 6 * D_MODEL), 0.1 * D_MODEL ** -0.5)
    out["b_mod"] = nrm((L, 6 * D_MODEL), 0.01)
    out["w_in"] = nrm((L, D_MODEL, P_IN), D_MODEL ** -0.5)
    out["w_out"] = nrm((L, D_MIX, D_MODEL), BETA * D_MIX ** -0.5)
    out["conv_a"] = nrm((L, CONF_KERNEL, D_A), CONF_KERNEL ** -0.5)
    out["conv_a_bias"] = nrm((L, D_A), 0.01)
    out["ln_a_g"] = near_one((L, D_A))
    out["ln_a_b"] = nrm((L, D_A), 0.01)
    out["conv_b"] = nrm((L, LRU_CONV, D_B), LRU_CONV ** -0.5)
    out["conv_b_bias"] = nrm((L, D_B), 0.01)
    out["w_rg"] = nrm((L, H_B, HEAD_DIM, HEAD_DIM), HEAD_DIM ** -0.5)
    out["b_rg"] = nrm((L, D_B), 0.01)
    out["w_ig"] = nrm((L, H_B, HEAD_DIM, HEAD_DIM), HEAD_DIM ** -0.5)
    out["b_ig"] = nrm((L, D_B), 0.01)
    ua = jax.random.uniform(next(ks), (L, D_B), jnp.float32, 0.9, 0.999)
    sa = ua ** (1.0 / LRU_C)
    out["lru_lambda"] = jnp.log(sa) - jnp.log1p(-sa)
    out["mu_c"] = jax.random.uniform(next(ks), (L, C_COLS), jnp.float32)
    out["w0"] = jax.random.uniform(next(ks), (L, D_C), jnp.float32, -6.5, -1.5)
    out["w_w2"] = nrm((L, LORA_W, D_C), 0.1 * LORA_W ** -0.5)
    out["a0"] = nrm((L, D_C), 0.1)
    out["w_a2"] = nrm((L, LORA_A, D_C), 0.1 * LORA_A ** -0.5)
    out["w_g2"] = nrm((L, LORA_G, D_C), LORA_G ** -0.5)
    out["k_k"] = 0.85 + nrm((L, D_C), 0.02)
    out["k_a"] = near_one((L, D_C))
    out["r_k"] = nrm((L, H_C, HEAD_DIM), 0.1)
    out["gn_g"] = near_one((L, D_C))
    out["gn_b"] = nrm((L, D_C), 0.01)
    out["conv_d"] = nrm((L, SHORT_CONV, D_D), SHORT_CONV ** -0.5)
    out["ln1_g"] = near_one((L, D_MODEL))
    out["ln1_b"] = nrm((L, D_MODEL), 0.01)
    out["w_router"] = nrm((L, D_MODEL, N_EXPERTS), D_MODEL ** -0.5)
    out["e_bias"] = nrm((L, N_EXPERTS), 0.01)
    out["w13"] = nrm((L, N_EXPERTS, D_MODEL, 2 * D_EXPERT), D_MODEL ** -0.5)
    out["w2"] = nrm((L, N_EXPERTS, D_EXPERT, D_MODEL), BETA * D_EXPERT ** -0.5)
    out["ws13"] = nrm((L, D_MODEL, 2 * D_SHARED), D_MODEL ** -0.5)
    out["ws2"] = nrm((L, D_SHARED, D_MODEL), BETA * D_SHARED ** -0.5)
    out["ln2_g"] = near_one((L, D_MODEL))
    out["ln2_b"] = nrm((L, D_MODEL), 0.01)
    return out

def reference(x, c, w_mod, b_mod, w_in, w_out, conv_a, conv_a_bias, ln_a_g, ln_a_b,
              conv_b, conv_b_bias, w_rg, b_rg, w_ig, b_ig, lru_lambda, mu_c, w0, w_w2,
              a0, w_a2, w_g2, k_k, k_a, r_k, gn_g, gn_b, conv_d, ln1_g, ln1_b,
              w_router, e_bias, w13, w2, ws13, ws2, ln2_g, ln2_b):
    c_act = jax.nn.silu(c)
    for l in range(DEPTH):
        mod = (c_act @ w_mod[l] + b_mod[l])[:, None, :]
        sh1, sc1, g1, sh2, sc2, g2 = jnp.split(mod, 6, axis=-1)
        u = x * (1.0 + sc1) + sh1
        mix = _token_mixers(u, w_in[l], w_out[l], conv_a[l], conv_a_bias[l], ln_a_g[l], ln_a_b[l],
                            conv_b[l], conv_b_bias[l], w_rg[l], b_rg[l], w_ig[l], b_ig[l],
                            lru_lambda[l], mu_c[l], w0[l], w_w2[l], a0[l], w_a2[l], w_g2[l],
                            k_k[l], k_a[l], r_k[l], gn_g[l], gn_b[l], conv_d[l])
        x = _layer_norm(ALPHA * x + (1.0 + g1) * mix, ln1_g[l], ln1_b[l])
        u = x * (1.0 + sc2) + sh2
        ffn = _moe_ffn(u, w_router[l], e_bias[l], w13[l], w2[l], ws13[l], ws2[l])
        x = _layer_norm(ALPHA * x + (1.0 + g2) * ffn, ln2_g[l], ln2_b[l])
    return x


_drawn_inputs = setup_inputs


def setup_inputs(seed=0):
    import zlib

    import numpy as np

    out = dict(_drawn_inputs(seed))
    spreads = {}
    factors = {'conv_a_bias': 3.557,
     'ln_a_g': 3.593,
     'ln_a_b': 4.664,
     'b_rg': 36.141,
     'b_ig': 30.557,
     'w_w2': 8.0,
     'k_k': 4.184,
     'k_a': 4.599,
     'gn_g': 4.183,
     'gn_b': 5.845,
     'ln2_g': 7.426,
     'ln2_b': 15.687}
    for name, (base, spread) in spreads.items():
        noise = np.random.default_rng([zlib.crc32(name.encode()), seed]).standard_normal(out[name].shape)
        drawn = base * np.exp(spread * noise) if base else spread * noise
        out[name] = __import__('jax').numpy.asarray(drawn.astype(out[name].dtype))
    for name, factor in factors.items():
        out[name] = (out[name] * factor).astype(out[name].dtype)
    return out
```

```python
from contextlib import ExitStack

import concourse.bass as bass
from concourse import mybir

P = 128
D = 1024
DC = D // P
SEQ = 2048
TB = 512
NTB = SEQ // TB
NCH = TB // P
NPROJ = 2688
NPT = NPROJ // P
GRP = 3
NGRP = NPT // GRP
HALO_A, HALO_B, HALO_D = 30, 3, 2
NE = 64
TOPK = 8
NGR = 8
DE = 256
NBLK = 192
CAP = SEQ
LEVELS = [1, 2, 4, 8, 16, 32, 64]
ALPHA = 2.0 ** 0.25
LN_EPS = 1e-5
GN_EPS = 64e-5
ROUTED_SCALE = 2.5
EM05 = 0.6065306597126334
NEG = -1.0e30

F32 = mybir.dt.float32
I32 = mybir.dt.int32
U32 = mybir.dt.uint32
ACT = mybir.ActivationFunctionType
ALU = mybir.AluOpType
AX_X = mybir.AxisListType.X

CV = {}
for _n, _w in (("conv_a", 62), ("conv_a_bias", 2), ("ln_a_g", 2), ("ln_a_b", 2), ("conv_b", 8),
               ("conv_b_bias", 2), ("b_rg", 2), ("b_ig", 2), ("lru_lambda", 2), ("mu_c", 7), ("w0", 2),
               ("a0", 2), ("k_k", 2), ("k_a", 2), ("r_k", 2), ("gn_g", 2), ("gn_b", 2), ("conv_d", 6)):
    CV[_n] = sum(w for _, w in CV.values()), _w
NCV = sum(w for _, w in CV.values())


class Count:

    seen = {}

    def __init__(self, sem, part):
        self.sem, self.n, self.part = sem, 0, (part, sem.name)

    def mark(self, key, by=1):
        self.n += by
        Count.seen[self.part, key] = self.n
        return by

    def at(self, key):
        if Count.final:
            return Count.seen[self.part, key]
        return 1

    final = False


def build(nc, t):
    top = ExitStack()

    def dram(name, shape, dt=F32):
        return nc.dram_tensor(name, shape, dt, kind="Internal").ap()

    U2 = dram("u2_rows", (SEQ + P, D))
    X1 = dram("x1_rows", (SEQ, D))
    YACC = dram("y_acc", (SEQ + P, D))
    LISTS = dram("expert_lists", ((NE + 1) * CAP, 2), I32)

    names = ["pe_steps", "act_steps", "dve_steps", "pool_steps", "x_loaded", "w_even_loaded", "w_odd_loaded",
             "params_loaded", "rows0_loaded", "rows1_loaded", "shared_w_loaded", "rows_stored", "shared_stored"]
    handles = [top.enter_context(nc.semaphore(n)) for n in names]
    span = range(min(h.num for h in handles), max(h.num for h in handles) + 1)
    assert len(span) == len(handles)
    lists_written = top.enter_context(nc.semaphore("lists_written"))

    def stage(tag):
        return [Count(h, tag) for h in handles]

    def need(eng, c, key):
        eng.wait_ge(c.sem, c.at(key))

    def stepper(eng, c):
        def do(ins, key=None, wait=True):
            ins.then_inc(c.sem, c.mark(key if key is not None else ("step", c.n)))
            if wait:
                eng.wait_ge(c.sem, c.n)
        return do

    def sb(stack, name, shape, dt=F32):
        return stack.enter_context(nc.sbuf_tensor(name, shape, dt))

    bank = [top.enter_context(nc.psum_tensor(f"bank{i}", [P, 512], F32)) for i in range(8)]

    ident = sb(top, "ident", [P, P])
    ones = sb(top, "ones", [P, P])
    maskf = sb(top, "maskf", [P, 512])
    cum_sel = sb(top, "cum_sel", [P, NE])
    g2p1 = sb(top, "g2p1", [P, D])
    epsc = sb(top, "epsc", [P, 4])

    mix = ExitStack()

    def mb(name, shape, dt=F32):
        return sb(mix, name, shape, dt)

    levm = mb("levm", [P, len(LEVELS), P])
    blk1 = mb("blk1", [P, P])
    scan_keep = mb("scan_keep", [P, TB])
    iota_e = mb("iota_e", [P, TOPK, NE])
    tok_id = mb("tok_id", [P, SEQ // P], I32)
    eye2 = mb("eye2", [P, 64])
    cv = mb("cv", [P, NCV])
    chalf = mb("chalf", [P, 2])
    ebias = mb("ebias", [P, NE])
    shcol = mb("shcol", [P, DC])
    sccol = mb("sccol", [P, DC])
    wout = mb("wout", [P, DC, D])
    wrt = mb("wrt", [P, DC, NE])
    lora = mb("lora", [P, 256])
    wri = mb("wri", [P, 2, 2, P])
    g1p1 = mb("g1p1", [P, D])
    sc2p1 = mb("sc2p1", [P, D])
    sh2r = mb("sh2r", [P, D])
    ln1g = mb("ln1g", [P, D])
    ln1b = mb("ln1b", [P, D])
    hid = mb("hid", [P, 2, HALO_A + TB])
    ya = mb("ya", [P, 2, TB])
    xb = mb("xb", [P, 2, HALO_B + TB])
    yb = mb("yb", [P, 2, TB])
    hlast = mb("hlast", [P, 2])
    pd = mb("pd", [P, 2, HALO_D + TB])
    yd = mb("yd", [P, 2, TB])
    pc = mb("pc", [P, 7, 1 + TB])
    pclast = mb("pclast", [P, 7])
    tmp = [mb(f"tmp{i}", [P, 2, TB]) for i in range(7)]
    kr = mb("kr", [P, 2, NCH, 2, P])
    bh = mb("bh", [P, 2, TB])
    kh = mb("kh", [P, 2, TB])
    state = mb("state", [P, 2, 64])
    s_in = mb("s_in", [P, 2, 64])
    dsc = mb("dsc", [P, 2, NCH, 2])
    small = mb("small", [P, 64])
    rt = mb("rt", [P, 512])
    tw = mb("tw", [P, TOPK, 2], I32)
    slot = mb("slot", [P, TOPK], I32)
    idx8 = mb("idx8", [P, TOPK], U32)
    ARENA = 45 * 256
    arena = mb("arena", [P, ARENA])
    taken = [0]

    def cut(*dims):
        n = 1
        for d in dims:
            n *= d
        a = arena[:, taken[0]:taken[0] + n]
        taken[0] += n
        assert taken[0] <= ARENA, taken
        if len(dims) == 2:
            return a.rearrange("p (a b) -> p a b", a=dims[0])
        if len(dims) == 3:
            return a.rearrange("p (a b c) -> p a b c", a=dims[0], b=dims[1])
        return a

    def cvc(name, i=0):
        o, w = CV[name]
        assert i < w
        return cv[:, o + i:o + i + 1]

    def flat(a):
        return a[:, :, :].rearrange("p a b -> p (a b)")

    PE, AC, DV, PO, XL, WE, WO, PL, R0, R1, SL, ST, SS = stage("setup")
    MC = 6 * D // 512
    taken[0] = 0
    wm = [cut(DC, 512) for _ in range(2)]
    crep = cut(DC, P)
    rows = [flat(kh), flat(bh), g1p1[:, :], sh2r[:, :], sc2p1[:, :], g2p1[:, :]]
    brow = [flat(x) for x in (*tmp[0:5], yd)]
    listpat = kr[0:NE + 1, :, :, :, :].rearrange("p a b c d -> p (a b c d)").bitcast(I32)
    with nc.Block() as block:
        @block.gpsimd
        def _(pool):
            do = stepper(pool, PO)
            for a, v in ((ones, 1.0), (ident, 0.0), (maskf, 1.0), (levm, 0.0), (blk1, 0.0), (scan_keep, 1.0), (wri, 0.0),
                         (hid, 0.0), (xb, 0.0), (pd, 0.0), (pc, 0.0), (hlast, 0.0), (state, 0.0), (cum_sel, 0.0), (eye2, 0.0)):
                do(pool.memset(a[tuple([slice(None)] * len(a.shape))], v), ("set", a.name), wait=False)
            for j, v in enumerate((LN_EPS, 1e-12, GN_EPS, 1.0)):
                do(pool.memset(epsc[:, j:j + 1], v), ("eps", j))
            do(pool.affine_select(out=ident[:, :], in_=ident[:, :], compare_op=ALU.not_equal, fill=1.0, base=0,
                                  pattern=[[-1, P]], channel_multiplier=1))
            for j in range(4):
                m = maskf[:, j * P:(j + 1) * P]
                do(pool.affine_select(out=m, in_=m, compare_op=ALU.is_ge if j % 2 else ALU.is_gt, fill=0.0, base=0,
                                      pattern=[[1, P]], channel_multiplier=-1))
            for j, m in enumerate(LEVELS):
                nb = P // (2 * m)
                v = levm[:, j, :].rearrange("p (n h m) -> p n h m", h=2, m=m)[:, :, 1, :]
                do(pool.memset(v, 1.0))
                do(pool.affine_select(out=v, in_=v, compare_op=ALU.is_ge, fill=0.0, base=0,
                                      pattern=[[-2 * m, nb], [0, m]], channel_multiplier=1))
                do(pool.affine_select(out=v, in_=v, compare_op=ALU.is_ge, fill=0.0, base=m - 1,
                                      pattern=[[2 * m, nb], [0, m]], channel_multiplier=-1))
            for h in range(2):
                do(pool.memset(blk1[64 * h:64 * h + 64, 64 * h:64 * h + 64], 1.0))
                e = eye2[64 * h:64 * h + 64, :]
                do(pool.affine_select(out=e, in_=e, compare_op=ALU.not_equal, fill=1.0, base=0,
                                      pattern=[[-1, 64]], channel_multiplier=1))
            do(pool.memset(scan_keep[:, :].rearrange("p (c n) -> p c n", n=P)[:, :, 0:1], 0.0))
            do(pool.iota(iota_e[:, :, :], pattern=[[0, TOPK], [1, NE]], base=0, channel_multiplier=0,
                         allow_small_or_imprecise_dtypes=True))
            do(pool.iota(tok_id[:, :], pattern=[[P, SEQ // P]], base=0, channel_multiplier=1))
            lp = listpat.rearrange("p (b n c) -> p b n c", n=P, c=2)
            do(pool.memset(lp[:, :, :, 1], 0))
            do(pool.iota(lp[:, :, :, 0], pattern=[[0, CAP // P // 2], [1, P]], base=SEQ, channel_multiplier=0), "list")

        @block.sync
        def _(sp):
            sp.dma_start(small[:, 0:DC], t["c"].rearrange("a (p c) -> p (a c)", c=DC)).then_inc(XL.sem, 16)
            w = t["w_mod"].rearrange("(p c) n -> p c n", c=DC)
            for j in range(MC):
                if j >= 2:
                    need(sp, PE, ("mod", j - 2))
                c = (WE, WO)[j % 2]
                sp.dma_start(wm[j % 2], w[:, :, j * 512:(j + 1) * 512]).then_inc(c.sem, c.mark(j, 16))
            need(sp, PO, "list")
            lv = LISTS.rearrange("(e h n) c -> e h (n c)", h=2, n=CAP // 2)
            for h in range(2):
                sp.dma_start(lv[:, h, :], listpat).then_inc(ST.sem, 16)
            z = flat(hid)[:, 0:D]
            sp.dma_start(U2[SEQ:SEQ + P, :], z).then_inc(ST.sem, 16)
            sp.dma_start(YACC[SEQ:SEQ + P, :], z).then_inc(ST.sem, 16)
            sp.wait_ge(ST.sem, 64)
            sp.drain()

        @block.scalar
        def _(act):
            do = stepper(act, AC)

            def load(dst, src):
                act.dma_start(dst, src).then_inc(PL.sem, PL.mark("all", 16))
            load(cv[:, :], t["chan"])
            for r in range(6):
                load(brow[r], t["b_mod"][0, r * D:(r + 1) * D].partition_broadcast(P))
            load(wout[:, :, :], t["w_out"].rearrange("(t p) n -> p t n", p=P))
            load(wrt[:, :, :], t["w_router"].rearrange("(p c) n -> p c n", c=DC))
            load(lora[:, :], t["lora"])
            need(act, PO, ("set", "wri"))
            for g, nme in enumerate(("w_rg", "w_ig")):
                for h in range(4):
                    o = 64 * (h % 2)
                    load(wri[o:o + 64, g, h // 2, o:o + 64], t[nme][h])
            load(ln1g[:, :], t["ln1_g"][0, :].partition_broadcast(P))
            load(ln1b[:, :], t["ln1_b"][0, :].partition_broadcast(P))
            load(ebias[:, :], t["e_bias"][0, :].partition_broadcast(P))
            act.wait_ge(XL.sem, 16)
            do(act.activation(small[:, 8:8 + DC], small[:, 0:DC], ACT.Silu))
            need(act, PO, ("set", "ones"))
            for k in range(DC):
                do(act.activation(crep[:, k, :], ones[:, :], ACT.Copy, scale=small[:, 8 + k:9 + k]), ("crep", k))
            act.wait_ge(PL.sem, PL.n)
            o = CV["lru_lambda"][0]
            do(act.activation(small[:, 16:18], cv[:, o:o + 2], ACT.Abs))
            do(act.activation(small[:, 16:18], small[:, 16:18], ACT.Exp, scale=-1.0), "ylam")

        @block.tensor
        def _(pe):
            need(pe, AC, ("crep", DC - 1))
            for j in range(MC):
                c = (WE, WO)[j % 2]
                need(pe, c, j)
                if j >= 4:
                    need(pe, DV, ("mod", j - 4))
                for k in range(DC):
                    mm = pe.matmul(bank[j % 4][:, :], crep[:, k, :], wm[j % 2][:, k, :], start=(k == 0), stop=(k == DC - 1))
                mm.then_inc(PE.sem, PE.mark(("mod", j)))
            need(pe, DV, ("row", 1))
            for r in range(2):
                v = rows[r][0:1, :].rearrange("p (n c) -> p n c", c=DC)
                for k in range(DC):
                    mm = pe.matmul(bank[5][:, r * DC + k:r * DC + k + 1], v[:, :, k], ones[0:1, 0:1], start=True, stop=True)
            mm.then_inc(PE.sem, PE.mark("cols"))

        @block.vector
        def _(dve):
            do = stepper(dve, DV)
            need(dve, PL, "all")
            for j in range(MC):
                r, o = j // 2, (j % 2) * 512
                need(dve, PE, ("mod", j))
                do(dve.tensor_tensor(rows[r][:, o:o + 512], bank[j % 4][:, :], brow[r][:, o:o + 512], ALU.add), ("mod", j))
                if j % 2:
                    if r in (1, 2, 4, 5):
                        do(dve.tensor_scalar(rows[r], rows[r], 1.0, None, ALU.add), ("row", r))
            need(dve, PE, "cols")
            do(dve.tensor_copy(shcol[:, :], bank[5][:, 0:DC]))
            do(dve.tensor_copy(sccol[:, :], bank[5][:, DC:2 * DC]))
            need(dve, AC, "ylam")
            y, z, z2, acc = (small[:, 16 + 2 * i:18 + 2 * i] for i in range(4))
            o = CV["lru_lambda"][0]
            do(dve.tensor_scalar(z, y, 2.0, None, ALU.add))
            do(dve.reciprocal(z, z))
            do(dve.tensor_tensor(z, z, y, ALU.mult))
            do(dve.tensor_tensor(z2, z, z, ALU.mult))
            do(dve.memset(acc, 1.0 / 19))
            for n in range(17, 0, -2):
                do(dve.tensor_tensor(acc, acc, z2, ALU.mult))
                do(dve.tensor_scalar(acc, acc, 1.0 / n, None, ALU.add))
            do(dve.tensor_tensor(acc, acc, z, ALU.mult))
            do(dve.tensor_scalar(z, cv[:, o:o + 2], -1.0, 0.0, ALU.mult, ALU.max))
            do(dve.scalar_tensor_tensor(out=acc, in0=acc, scalar=2.0, in1=z, op0=ALU.mult, op1=ALU.add))
            do(dve.tensor_scalar(chalf[:, :], acc, 4.0, None, ALU.mult))
    nc.all_engine_barrier(sems_to_clear=span)

    PE, AC, DV, PO, XL, WE, WO, PL, R0, R1, SL, ST, SS = stage("mix")
    taken[0] = 0
    ut = cut(DC, TB)
    wb = [cut(DC, GRP * P) for _ in range(2)]
    taken[0] = 0
    gm = cut(8, 4 * P)
    em = cut(8, P)
    xi = cut(8, P)
    xt = cut(8, P)
    pm = cut(8, P)
    rb = cut(8, P)
    tk = cut(2, 3, 256)
    rk = cut(4, P)
    phi = cut(4, 64)
    taken[0] = 0
    ws13 = cut(DC, 512)
    ws2 = cut(2, D)
    xr = [cut(D) for _ in range(2)]
    x1 = cut(D)
    u2 = cut(D)
    u2t = cut(DC, P)
    ysh = flat(tmp[2])
    hs = tmp[3][:, 0, 0:256]
    hst = tmp[3][:, 1, 0:256]
    mask_u = maskf[:, :].bitcast(U32)
    TAIL = list(range(7, NPT))
    EVEN = lambda n: WE if n % 2 == 0 else WO

    with nc.Fori(0, NTB) as it:
      with nc.Block() as block:
        @block.sync
        def _(sp):
            sp.dma_start(ut, t["xt"][:, :, bass.ds(it * TB, TB)]).then_inc(XL.sem, 16)
            for g in range(NGRP):
                if g >= 2:
                    need(sp, PE, ("proj", GRP * (g - 1) - 1))
                sp.dma_start(wb[g % 2], t["w_in"][:, g]).then_inc(EVEN(g).sem, EVEN(g).mark(g, 16))
            need(sp, PE, "chunks")
            need(sp, DV, "chunks")
            need(sp, AC, "chunks")
            sp.dma_start(ws13, t["ws13"].rearrange("(p c) n -> p c n", c=DC)).then_inc(SL.sem, 16)
            sp.dma_start(ws2, t["ws2"].rearrange("(p c) n -> p c n", c=2)).then_inc(SL.sem, 16)

            def load_rows(tt):
                c = (R0, R1)[tt % 2]
                sp.dma_start(xr[tt % 2], t["x"][bass.ds(it * TB + tt * P, P), :]).then_inc(c.sem, c.mark(tt, 16))

            for tt in range(2):
                load_rows(tt)
            for tt in range(NCH):
                need(sp, DV, ("x1", tt))
                sp.dma_start(X1[bass.ds(it * TB + tt * P, P), :], x1).then_inc(ST.sem, ST.mark(("x1", tt), 16))
                if tt + 2 < NCH:
                    load_rows(tt + 2)
                need(sp, DV, ("u2", tt))
                sp.dma_start(U2[bass.ds(it * TB + tt * P, P), :], u2).then_inc(ST.sem, ST.mark(("u2", tt), 16))
                need(sp, AC, ("ysh", tt))
                sp.dma_start(YACC[bass.ds(it * TB + tt * P, P), :], ysh).then_inc(SS.sem, SS.mark(tt, 16))
            sp.wait_ge(ST.sem, ST.n)
            sp.wait_ge(SS.sem, SS.n)
            sp.drain()

        @block.tensor
        def _(pe):
            def mark(mm, key):
                mm.then_inc(PE.sem, PE.mark(key))

            for c in range(DC):
                need(pe, DV, ("ut", c))
            for n in range(NPT):
                g = n // GRP
                if n % GRP == 0:
                    need(pe, EVEN(g), g)
                if n >= 4:
                    need(pe, *((DV, ("evac", n - 4)) if n - 4 in (8, 10, 19, 20) else (AC, ("evac", n - 4))))
                for c in range(DC):
                    mm = pe.matmul(bank[n % 4][:, :], wb[g % 2][:, c, (n % GRP) * P:(n % GRP + 1) * P], ut[:, c, :],
                                   start=(c == 0), stop=(c == DC - 1))
                mark(mm, ("proj", n))
                if n == 8:
                    need(pe, AC, "lt")
                    for ct in range(2):
                        mark(pe.matmul(bank[4 + ct][:, :], lora[0:32, ct * P:(ct + 1) * P], tmp[5][0:32, 0, :],
                                       start=True, stop=True), ("lw", ct))
                        mark(pe.matmul(bank[6 + ct][:, :], lora[32:64, ct * P:(ct + 1) * P], tmp[5][32:64, 0, :],
                                       start=True, stop=True), ("la", ct))
                if n == 12:
                    need(pe, DV, "kksq")
                    for ct in range(2):
                        need(pe, AC, ("sig_w", ct))
                        mark(pe.matmul(bank[4 + ct][:, :], blk1[:, :], tmp[6][:, ct, :], start=True, stop=True), ("ss", ct))
                if n == 15:
                    need(pe, DV, "rkk")
                    for ct in range(2):
                        need(pe, AC, ("sig_a", ct))
                        mark(pe.matmul(bank[6 + ct][:, :], blk1[:, :], tmp[6][:, ct, :], start=True, stop=True), ("bonus", ct))
                    for ct in range(2):
                        need(pe, AC, ("knorm", ct))
                        mark(pe.matmul(bank[4 + ct][:, :], lora[64:128, ct * P:(ct + 1) * P], tmp[5][64:128, 0, :],
                                       start=True, stop=True), ("lg", ct))
            need(pe, DV, ("u", 1))
            need(pe, DV, "bonus")
            need(pe, AC, ("g", 1))
            for ct in range(2):
                mark(pe.matmul(bank[4 + ct][:, :], wri[:, 0, ct, :], tmp[2][:, ct, :], start=True, stop=True), ("gr", ct))
                mark(pe.matmul(bank[6 + ct][:, :], wri[:, 1, ct, :], tmp[2][:, ct, :], start=True, stop=True), ("gi", ct))

            need(pe, AC, ("evac", 18))
            need(pe, DV, ("evac", 20))
            need(pe, DV, "rp")
            need(pe, AC, ("gi", 1))
            for w in range(2):
                if w:
                    need(pe, AC, ("y", 0, 1))
                    need(pe, DV, ("st", 0, 1))
                for cc in range(2):
                    ch = 2 * w + cc
                    cs = slice(ch * P, (ch + 1) * P)
                    for ct in range(2):
                        pe.transpose(bank[2 * cc][:, ct * P:(ct + 1) * P], kr[:, ct, ch, 0, :], ident[:, :])
                        pe.transpose(bank[2 * cc][:, (2 + ct) * P:(3 + ct) * P], pc[:, 4 + ct, 1 + ch * P:1 + (ch + 1) * P], ident[:, :])
                        pe.transpose(bank[2 * cc + 1][:, ct * P:(ct + 1) * P], kh[:, ct, cs], ident[:, :])
                        mm = pe.transpose(bank[2 * cc + 1][:, (2 + ct) * P:(3 + ct) * P], bh[:, ct, cs], ident[:, :])
                    mark(mm, ("tok", w, cc))
                for n in range(8):
                    cc, h = n // 4, n % 4
                    ct, o, ch = h // 2, 64 * (h % 2), 2 * w + cc
                    cs = slice(ch * P, (ch + 1) * P)
                    if n >= 4:
                        need(pe, DV, ("gm", w, n - 4))
                    rhs = kr[o:o + 64, ct, ch, :, :].rearrange("p a b -> p (a b)")
                    pe.matmul(bank[4 + h][:, 0:256], bh[o:o + 64, ct, cs], rhs, start=True, stop=True)
                    mark(pe.matmul(bank[4 + h][:, 256:512], kh[o:o + 64, ct, cs], rhs, start=True, stop=True), ("g4", w, n))
                need(pe, AC, ("tok", w, 1))
                for n in range(8):
                    cc, h = n // 4, n % 4
                    need(pe, DV, ("gm", w, n))
                    mm = pe.matmul(bank[0][:, n * 64:(n + 1) * 64], gm[:, n, 256:384], tk[:, cc, 0, h * 64:(h + 1) * 64], start=True, stop=True)
                mark(mm, ("av", w))
                need(pe, PO, ("em", w, 0))
                for cc in range(2):
                    for h in range(4):
                        n = 4 * cc + h
                        mm = pe.matmul(bank[3 + cc][:, h * P:(h + 1) * P], em[:, n, :], ident[:, :], start=True, stop=True)
                    mark(mm, ("q", w, 0, cc))
                for lv in range(1, len(LEVELS)):
                    need(pe, PO, ("em", w, lv))
                    for cc in range(2):
                        need(pe, DV, ("x", w, lv - 1, cc))
                        for h in range(4):
                            n = 4 * cc + h
                            mm = pe.matmul(bank[1 + cc][:, h * P:(h + 1) * P], em[:, n, :], xi[:, n, :], start=True, stop=True)
                        mark(mm, ("p", w, lv, cc))
                    for cc in range(2):
                        need(pe, AC, ("pm", w, lv, cc))
                        need(pe, DV, ("xt", w, lv - 1, cc))
                        if lv < len(LEVELS) - 1:
                            for h in range(4):
                                n = 4 * cc + h
                                mm = pe.matmul(bank[3 + cc][:, h * P:(h + 1) * P], xt[:, n, :], pm[:, n, :], start=True, stop=True)
                            mark(mm, ("q", w, lv, cc))
                        for h in range(4):
                            n = 4 * cc + h
                            mm = pe.matmul(bank[5 + cc][:, h * P:(h + 1) * P], pm[:, n, :], xt[:, n, :], start=True, stop=True)
                        mark(mm, ("qt", w, lv, cc))
                need(pe, AC, ("av", w))
                for cc in range(2):
                    need(pe, DV, ("xt", w, len(LEVELS) - 1, cc))
                    for h in range(4):
                        n = 4 * cc + h
                        mm = pe.matmul(bank[1 + cc][:, h * P:(h + 1) * P], xt[:, n, :], rb[:, n, :], start=True, stop=True)
                    mark(mm, ("wg", w, cc))
                for cc in range(2):
                    need(pe, AC, ("wg", w, cc))
                    for h in range(4):
                        n, o, ct = 4 * cc + h, 64 * (h % 2), h // 2
                        q = 2 * cc + ct
                        pe.matmul(bank[3][o:o + 64, q * P:(q + 1) * P], pm[:, n, 0:64], gm[:, n, 128:256], start=True, stop=True)
                        mm = pe.matmul(bank[4][o:o + 64, q * 64:(q + 1) * 64], pm[:, n, 0:64], tk[:, cc, 2, h * 64:(h + 1) * 64],
                                       start=True, stop=True)
                mark(mm, ("rk", w))
                need(pe, DV, ("rk", w))
                need(pe, DV, ("phi", w))
                for cc in range(2):
                    need(pe, DV, ("sin", w, cc))
                    for h in range(4):
                        n, o, ct = 4 * cc + h, 64 * (h % 2), h // 2
                        q = 2 * cc + ct
                        vt = tk[:, cc, 0, h * 64:(h + 1) * 64]
                        out = bank[5][o:o + 64, ct * 64:(ct + 1) * 64]
                        pe.matmul(out, tk[:, cc, 1, h * 64:(h + 1) * 64], vt, start=True, stop=False)
                        pe.matmul(out, tk[:, cc, 2, h * 64:(h + 1) * 64], pm[:, n, 64:128], start=False, stop=False)
                        mm = pe.matmul(out, phi[o:o + 64, q, :], s_in[o:o + 64, ct, :], start=False, stop=True)
                    mark(mm, ("st", w, cc))
                    for h in range(4):
                        n, o, ct = 4 * cc + h, 64 * (h % 2), h // 2
                        q = 2 * cc + ct
                        vt = tk[:, cc, 0, h * 64:(h + 1) * 64]
                        out = bank[6 + cc][o:o + 64, ct * P:(ct + 1) * P]
                        pe.matmul(out, vt, gm[:, n, 384:512], start=True, stop=False)
                        pe.matmul(out, pm[:, n, 64:128], gm[:, n, 128:256], start=False, stop=False)
                        mm = pe.matmul(out, s_in[o:o + 64, ct, :], rk[o:o + 64, q, :], start=False, stop=True)
                    mark(mm, ("y", w, cc))
            mark(pe.matmul(bank[0][0:1, 0:1], ones[0:1, 0:1], ones[0:1, 0:1], start=True, stop=True), "chunks")

            need(pe, AC, ("y", 1, 1))
            for ct in range(2):
                mark(pe.matmul(bank[1 + ct][:, :], blk1[:, :], tmp[0][:, ct, :], start=True, stop=True), ("gnm", ct))
            need(pe, DV, "conv_a")
            for ct in range(2):
                mm = pe.matmul(bank[3][:, :], ones[:, :], ya[:, ct, :], start=(ct == 0), stop=(ct == 1))
            mark(mm, "lam")
            need(pe, AC, "gnsq")
            for ct in range(2):
                need(pe, DV, ("gnd", ct))
                mark(pe.matmul(bank[1 + ct][:, :], blk1[:, :], tmp[2][:, ct, :], start=True, stop=True), ("gnv", ct))
            need(pe, AC, "lasq")
            for ct in range(2):
                mm = pe.matmul(bank[3][:, :], ones[:, :], tmp[3][:, ct, :], start=(ct == 0), stop=(ct == 1))
            mark(mm, "lav")

            for tt in range(NCH):
                ts = slice(tt * P, (tt + 1) * P)
                if tt == 0:
                    need(pe, DV, "yc")
                    need(pe, AC, "ya")
                else:
                    need(pe, AC, ("ysh", tt - 1))
                mats = [ya[:, 0, ts], ya[:, 1, ts], yb[:, 0, ts], yb[:, 1, ts],
                        pc[:, 0, 1 + tt * P:1 + (tt + 1) * P], pc[:, 1, 1 + tt * P:1 + (tt + 1) * P], yd[:, 0, ts], yd[:, 1, ts]]
                for n in range(2):
                    for k in range(DC):
                        mm = pe.matmul(bank[n][:, :], mats[k], wout[:, k, n * 512:(n + 1) * 512], start=(k == 0), stop=(k == DC - 1))
                    mark(mm, ("out", tt, n))
                need(pe, DV, ("u2", tt))
                v = u2.rearrange("p (n c) -> p n c", c=DC)
                for k in range(DC):
                    mm = pe.transpose(bank[2 + k // 4][:, (k % 4) * P:(k % 4 + 1) * P], v[:, :, k], ident[:, :])
                    if k % 4 == 3:
                        mark(mm, ("u2t", tt, k // 4))
                need(pe, AC, ("u2t", tt))
                if tt:
                    need(pe, AC, ("score", tt - 1))
                for k in range(DC):
                    mm = pe.matmul(bank[4][:, 0:NE], u2t[:, k, :], wrt[:, k, :], start=(k == 0), stop=(k == DC - 1))
                mark(mm, ("score", tt))
                if tt == 0:
                    pe.wait_ge(SL.sem, 32)
                for k in range(DC):
                    mm = pe.matmul(bank[5][:, :], u2t[:, k, :], ws13[:, k, :], start=(k == 0), stop=(k == DC - 1))
                mark(mm, ("sh", tt))
                need(pe, DV, ("hs", tt))
                pe.matmul(bank[7][:, 0:NE], maskf[:, 0:P], rt[:, 128:128 + NE], start=True, stop=False)
                mark(pe.matmul(bank[7][:, 0:NE], ones[:, :], cum_sel[:, :], start=False, stop=True), ("rank", tt))
                v = hs.rearrange("p (n c) -> p n c", c=2)
                for k in range(2):
                    mm = pe.transpose(bank[6][:, k * P:(k + 1) * P], v[:, :, k], ident[:, :])
                mark(mm, ("hst", tt))
                need(pe, AC, ("hst", tt))
                for n in range(2):
                    for k in range(2):
                        mm = pe.matmul(bank[n][:, :], hst[:, k * P:(k + 1) * P], ws2[:, k, n * 512:(n + 1) * 512],
                                       start=(k == 0), stop=(k == 1))
                mark(mm, ("ysh", tt))

        @block.scalar
        def _(act):
            do = stepper(act, AC)

            def evac(n):
                need(act, PE, ("proj", n))
                src = bank[n % 4][:, :]
                if n < 7:
                    do(act.activation(pc[:, n, 1:1 + TB], src, ACT.Copy), ("evac", n), wait=False)
                elif n in (7, 9):
                    do(act.activation(ya[:, (n - 7) // 2, :], src, ACT.Sigmoid), ("evac", n), wait=False)
                elif n in (11, 12):
                    do(act.activation(xb[:, n - 11, HALO_B:], src, ACT.Copy), ("evac", n), wait=False)
                elif n in (13, 14):
                    do(act.activation(yb[:, n - 13, :], src, ACT.Gelu_apprx_tanh), ("evac", n), wait=False)
                elif n in (15, 16):
                    do(act.activation(yd[:, n - 15, :], src, ACT.Copy), ("evac", n), wait=False)
                elif n in (17, 18):
                    do(act.activation(pd[:, n - 17, HALO_D:], src, ACT.Copy), ("evac", n), wait=False)

            for n in range(7):
                evac(n)
            evac(7)
            need(act, DV, ("xs", 6))
            do(act.activation(tmp[5][32:64, 0, :], pc[32:64, 6, 1:1 + TB], ACT.Copy), wait=False)
            do(act.activation(tmp[5][64:128, 0, :], pc[64:128, 6, 1:1 + TB], ACT.Sigmoid), wait=False)
            do(act.activation(tmp[5][0:32, 0, :], pc[0:32, 6, 1:1 + TB], ACT.Tanh), "lt")
            evac(9)
            need(act, DV, ("xs", 5))
            for ct in range(2):
                need(act, PE, ("lw", ct))
                do(act.activation(tmp[0][:, ct, :], bank[4 + ct][:, :], ACT.Sigmoid, bias=cvc("w0", ct)), ("sig_w", ct), wait=False)
                need(act, PE, ("la", ct))
                do(act.activation(tmp[1][:, ct, :], bank[6 + ct][:, :], ACT.Sigmoid, bias=cvc("a0", ct)), ("sig_a", ct), wait=False)
            evac(11)
            evac(12)
            need(act, DV, "csx")
            v = lambda a: flat(a).rearrange("p (a b) -> p a b", b=P)
            krv = lambda j: kr[:, :, :, j, :].rearrange("p a b c -> p (a b) c")
            do(act.activation(krv(0), v(tmp[0]), ACT.Exp, scale=-EM05), "ex", wait=False)
            do(act.activation(krv(1), v(tmp[3]), ACT.Exp, scale=-EM05), "em", wait=False)
            dv = dsc[:, :, :, :].rearrange("p a b c -> p (a b) c")
            do(act.activation(dv[:, :, 0], v(tmp[2])[:, :, P // 2 - 1], ACT.Exp, scale=-EM05), wait=True)
            do(act.activation(dv[:, :, 1], v(tmp[3])[:, :, P - 1], ACT.Exp, scale=-EM05), "dsc", wait=False)
            do(act.activation(flat(tmp[2]), flat(tmp[3]), ACT.Exp, scale=EM05), "ep", wait=False)
            for ct in range(2):
                need(act, PE, ("ss", ct))
                do(act.activation(tmp[6][:, ct, :], bank[4 + ct][:, :], ACT.Sqrt, bias=epsc[:, 1:2]), ("knorm", ct), wait=False)
            evac(13)
            evac(14)
            evac(15)
            evac(16)
            for ct in range(2):
                need(act, PE, ("lg", ct))
                need(act, DV, "rp")
                do(act.activation(pc[:, ct, 1:1 + TB], bank[4 + ct][:, :], ACT.Copy), ("g", ct), wait=False)
            evac(17)
            evac(18)
            for ct in range(2):
                need(act, PE, ("gr", ct))
                do(act.activation(tmp[3][:, ct, :], bank[4 + ct][:, :], ACT.Sigmoid, bias=cvc("b_rg", ct)), ("gr", ct))
                need(act, PE, ("gi", ct))
                do(act.activation(tmp[4][:, ct, :], bank[6 + ct][:, :], ACT.Sigmoid, bias=cvc("b_ig", ct)), ("gi", ct), wait=False)
            for ct in range(2):
                do(act.activation(tmp[3][:, ct, :], tmp[3][:, ct, :], ACT.Tanh, scale=chalf[:, ct:ct + 1]), ("t", ct))
            do(act.activation(flat(tmp[5]), flat(tmp[3]), ACT.Sqrt), "sqt", wait=False)

            for w in range(2):
                for cc in range(2):
                    need(act, PE, ("tok", w, cc))
                    do(act.activation(rb[:, 4 * cc:4 * cc + 4, 0:64], bank[2 * cc][:, 0:256].rearrange("p (h k) -> p h k", k=64),
                                      ACT.Copy), wait=False)
                    do(act.activation(tk[:, cc, 0, :], bank[2 * cc][:, 256:512], ACT.Copy), wait=False)
                    do(act.activation(tk[:, cc, 1:3, :].rearrange("p a b -> p (a b)"), bank[2 * cc + 1][:, :], ACT.Copy),
                       ("tok", w, cc), wait=False)
                need(act, PE, ("av", w))
                do(act.activation(rb[:, :, 64:128], bank[0][:, :].rearrange("p (n k) -> p n k", k=64), ACT.Copy), ("av", w), wait=False)
                for lv in range(1, len(LEVELS)):
                    for cc in range(2):
                        need(act, PE, ("p", w, lv, cc))
                        do(act.activation(pm[:, 4 * cc:4 * cc + 4, :].rearrange("p a b -> p (a b)"), bank[1 + cc][:, :], ACT.Copy),
                           ("pm", w, lv, cc), wait=False)
                for cc in range(2):
                    need(act, PE, ("wg", w, cc))
                    do(act.activation(pm[:, 4 * cc:4 * cc + 4, :].rearrange("p a b -> p (a b)"), bank[1 + cc][:, :], ACT.Copy,
                                      scale=-1.0), ("wg", w, cc), wait=False)
                for cc in range(2):
                    ch = 2 * w + cc
                    need(act, PE, ("y", w, cc))
                    do(act.activation(tmp[0][:, :, ch * P:(ch + 1) * P], bank[6 + cc][:, 0:256].rearrange("p (c n) -> p c n", n=P),
                                      ACT.Copy), ("y", w, cc), wait=False)
            do(act.activation(small[:, 32:33], epsc[:, 3:4], ACT.Copy), "chunks", wait=False)
            for ct in range(2):
                need(act, DV, ("gnd", ct))
                do(act.activation(tmp[2][:, ct, :], tmp[0][:, ct, :], ACT.Square), "gnsq", wait=False)
            for ct in range(2):
                need(act, DV, ("lad", ct))
                do(act.activation(tmp[3][:, ct, :], ya[:, ct, :], ACT.Square), "lasq", wait=False)
            for ct in range(2):
                need(act, PE, ("gnv", ct))
                do(act.activation(tmp[2][:, ct, :], bank[1 + ct][:, :], ACT.Sqrt, bias=epsc[:, 2:3], scale=1.0 / 64), ("gns", ct), wait=False)
            need(act, PE, "lav")
            do(act.activation(tmp[4][:, 0, :], bank[3][:, :], ACT.Sqrt, bias=epsc[:, 0:1], scale=1.0 / 256), "las", wait=False)
            for ct in range(2):
                need(act, DV, ("laz", ct))
                do(act.activation(ya[:, ct, :], ya[:, ct, :], ACT.Silu, bias=cvc("ln_a_b", ct), scale=cvc("ln_a_g", ct)), "ya", wait=False)
            for tt in range(NCH):
                need(act, DV, ("var", tt))
                do(act.activation(small[:, 44:45], small[:, 41:42], ACT.Sqrt, bias=epsc[:, 0:1]), ("std", tt), wait=False)
                for k in range(2):
                    need(act, PE, ("u2t", tt, k))
                    do(act.activation(u2t[:, 4 * k:4 * k + 4, :].rearrange("p a b -> p (a b)"), bank[2 + k][:, :], ACT.Copy),
                       ("u2t", tt), wait=False)
                need(act, PE, ("score", tt))
                if tt:
                    need(act, DV, ("routed", tt - 1))
                do(act.activation(rt[:, 0:NE], bank[4][:, 0:NE], ACT.Sigmoid), ("score", tt), wait=False)
                need(act, PE, ("sh", tt))
                do(act.activation(hs, bank[5][:, 0:256], ACT.Silu), ("silu", tt), wait=False)
                need(act, PE, ("hst", tt))
                do(act.activation(hst, bank[6][:, 0:256], ACT.Copy), ("hst", tt), wait=False)
                need(act, PE, ("ysh", tt))
                if tt:
                    need(act, SS, tt - 1)
                for n in range(2):
                    do(act.activation(ysh[:, n * 512:(n + 1) * 512], bank[n][:, :], ACT.Copy), ("ysh", tt), wait=False)

        @block.vector
        def _(dve):
            do = stepper(dve, DV)
            v = lambda a: flat(a).rearrange("p (a b) -> p a b", b=P)
            krv = lambda j: kr[:, :, :, j, :].rearrange("p a b c -> p (a b) c")
            dve.wait_ge(XL.sem, 16)
            for c in range(DC):
                do(dve.tensor_scalar(ut[:, c, :], ut[:, c, :], sccol[:, c:c + 1], shcol[:, c:c + 1], ALU.mult, ALU.add), ("ut", c), wait=False)
            for j in (6, 0, 2, 4):
                m = 1 if j == 6 else 2
                need(dve, AC, ("evac", j + m - 1))
                if j == 6:
                    d = tmp[6][:, 0:1, :]
                else:
                    d = tmp[{0: 0, 2: 1, 4: 2}[j]][:, :, :]
                do(dve.tensor_copy(pclast[:, j:j + m], pc[:, j:j + m, TB]), wait=False)
                do(dve.tensor_tensor(d, pc[:, j:j + m, 0:TB], pc[:, j:j + m, 1:1 + TB], ALU.subtract))
                for i in range(m):
                    x = pc[:, j + i, 1:1 + TB]
                    do(dve.scalar_tensor_tensor(out=x, in0=d[:, i, :], scalar=cvc("mu_c", j + i), in1=x, op0=ALU.mult, op1=ALU.add),
                       ("xs", j + i))
            def gate_a(n):
                need(dve, PE, ("proj", n))
                need(dve, AC, ("evac", n - 1))
                do(dve.tensor_tensor(hid[:, (n - 8) // 2, HALO_A:], bank[n % 4][:, :], ya[:, (n - 8) // 2, :], ALU.mult), ("evac", n), wait=False)
            gate_a(8)
            for ct in range(2):
                do(dve.tensor_scalar(tmp[4][:, ct, :], pc[:, 2 + ct, 1:1 + TB], cvc("k_k", ct), None, ALU.mult))
                do(dve.tensor_tensor(tmp[6][:, ct, :], tmp[4][:, ct, :], tmp[4][:, ct, :], ALU.mult), "kksq")
            gate_a(10)
            for ct in range(2):
                need(dve, AC, ("sig_w", ct))
                do(dve.tensor_tensor_scan(tmp[2][:, ct, :], scan_keep[:, :], tmp[0][:, ct, :], 0.0, ALU.mult, ALU.add))
            mid = v(tmp[2])[:, :, P // 2 - 1:P // 2].to_broadcast([P, 2 * NCH, P])
            do(dve.tensor_tensor(v(tmp[3]), v(tmp[2]), mid, ALU.subtract))
            do(dve.tensor_tensor(flat(tmp[0]), flat(tmp[3]), flat(tmp[0]), ALU.subtract), "csx")
            for ct in range(2):
                need(dve, AC, ("knorm", ct))
                do(dve.reciprocal(tmp[6][:, ct, :], tmp[6][:, ct, :]))
            do(dve.tensor_tensor(flat(tmp[4]), flat(tmp[4]), flat(tmp[6]), ALU.mult))
            need(dve, AC, "ex")
            do(dve.tensor_tensor(krv(0), krv(0), v(tmp[4]), ALU.mult), "kp", wait=False)
            need(dve, AC, ("sig_a", 1))
            do(dve.tensor_tensor(flat(tmp[4]), flat(tmp[4]), flat(tmp[1]), ALU.mult))
            need(dve, AC, "ep")
            do(dve.tensor_tensor(flat(bh), flat(tmp[4]), flat(tmp[2]), ALU.mult), wait=False)
            for ct in range(2):
                k, r = pc[:, 2 + ct, 1:1 + TB], pc[:, ct, 1:1 + TB]
                do(dve.tensor_scalar(tmp[6][:, ct, :], tmp[1][:, ct, :], -1.0, cvc("k_a", ct), ALU.add, ALU.mult))
                do(dve.scalar_tensor_tensor(out=k, in0=tmp[6][:, ct, :], scalar=1.0, in1=k, op0=ALU.add, op1=ALU.mult))
                do(dve.tensor_tensor(kh[:, ct, :], k, tmp[2][:, ct, :], ALU.mult), wait=False)
                do(dve.scalar_tensor_tensor(out=tmp[6][:, ct, :], in0=r, scalar=cvc("r_k", ct), in1=k, op0=ALU.mult, op1=ALU.mult), "rkk")
            need(dve, AC, "em")
            do(dve.tensor_tensor(kr[:, :, :, 1, :].rearrange("p a b c -> p a b c"), kr[:, :, :, 1, :],
                                 pc[:, 0:2, 1:1 + TB].rearrange("p a (b c) -> p a b c", c=P), ALU.mult), "rp")
            for ct in range(2):
                need(dve, PE, ("bonus", ct))
                do(dve.tensor_tensor(tmp[1][:, ct, :], bank[6 + ct][:, :], pc[:, 4 + ct, 1:1 + TB], ALU.mult), "bonus", wait=False)
            for ct in range(2):
                need(dve, AC, ("evac", 11 + ct))
                u = tmp[2][:, ct, :]
                do(dve.tensor_scalar(u, xb[:, ct, HALO_B:], cvc("conv_b", 2 * 3 + ct), cvc("conv_b_bias", ct), ALU.mult, ALU.add))
                for k in range(3):
                    do(dve.scalar_tensor_tensor(out=u, in0=xb[:, ct, k:k + TB], scalar=cvc("conv_b", 2 * k + ct), in1=u,
                                                op0=ALU.mult, op1=ALU.add), ("u", ct))
            for ct in range(2):
                need(dve, PE, ("proj", 19 + ct))
                need(dve, AC, ("evac", 17 + ct))
                x = pd[:, ct, HALO_D:]
                do(dve.tensor_tensor(x, bank[(19 + ct) % 4][:, :], x, ALU.mult), ("evac", 19 + ct))
            need(dve, AC, ("evac", 16))
            for ct in range(2):
                a = tmp[6][:, ct, :]
                do(dve.tensor_scalar(a, pd[:, ct, HALO_D:], cvc("conv_d", 4 + ct), None, ALU.mult))
                for k in range(2):
                    do(dve.scalar_tensor_tensor(out=a, in0=pd[:, ct, k:k + TB], scalar=cvc("conv_d", 2 * k + ct), in1=a,
                                                op0=ALU.mult, op1=ALU.add))
            do(dve.tensor_tensor(flat(yd), flat(yd), flat(tmp[6]), ALU.mult))
            need(dve, AC, ("t", 1))
            do(dve.tensor_scalar(flat(tmp[6]), flat(tmp[3]), 1.0, None, ALU.add))
            do(dve.reciprocal(flat(tmp[6]), flat(tmp[6])))
            do(dve.tensor_tensor(flat(tmp[4]), flat(tmp[4]), flat(tmp[2]), ALU.mult))
            need(dve, AC, "sqt")
            do(dve.tensor_scalar(flat(tmp[3]), flat(tmp[6]), 2.0, -1.0, ALU.mult, ALU.add), wait=False)
            do(dve.scalar_tensor_tensor(out=flat(tmp[5]), in0=flat(tmp[5]), scalar=2.0, in1=flat(tmp[6]), op0=ALU.mult, op1=ALU.mult))
            do(dve.tensor_tensor(flat(tmp[4]), flat(tmp[4]), flat(tmp[5]), ALU.mult))
            for ct in range(2):
                do(dve.tensor_tensor_scan(tmp[2][:, ct, :], tmp[3][:, ct, :], tmp[4][:, ct, :], hlast[:, ct:ct + 1], ALU.mult, ALU.add))
                do(dve.tensor_copy(hlast[:, ct:ct + 1], tmp[2][:, ct, TB - 1:TB]), wait=False)
            need(dve, AC, ("evac", 14))
            do(dve.tensor_tensor(flat(yb), flat(yb), flat(tmp[2]), ALU.mult), "yb")

            taps = [(ct, k) for k in range(30, -1, -1) for ct in range(2)]

            tapped = []

            def tap(count):
                for _ in range(count):
                    if not taps:
                        return
                    ct, k = taps.pop(0)
                    if k < 30:
                        dve.wait_ge(DV.sem, tapped.pop(0))
                    a, x = ya[:, ct, :], hid[:, ct, k:k + TB]
                    if k == 30:
                        do(dve.tensor_scalar(a, x, cvc("conv_a", 2 * k + ct), cvc("conv_a_bias", ct), ALU.mult, ALU.add), wait=False)
                    else:
                        do(dve.scalar_tensor_tensor(out=a, in0=x, scalar=cvc("conv_a", 2 * k + ct), in1=a, op0=ALU.mult, op1=ALU.add),
                           "conv_a", wait=False)
                    tapped.append(DV.n)

            need(dve, PO, "zero")
            need(dve, DV, ("evac", 10))
            for w in range(2):
                for n in range(8):
                    need(dve, PE, ("g4", w, n))
                    do(dve.copy_predicated(gm[:, n, :], mask_u, bank[4 + n % 4][:, :]), ("gm", w, n), wait=False)
                need(dve, PO, ("em", w, 0))
                idb = ident[:, :].unsqueeze(1).to_broadcast([P, 4, P])
                for cc in range(2):
                    q = slice(4 * cc, 4 * cc + 4)
                    do(dve.tensor_tensor(xt[:, q, :], idb, em[:, q, :], ALU.subtract), ("xt", w, 0, cc), wait=False)
                    need(dve, PE, ("q", w, 0, cc))
                    do(dve.tensor_tensor(xi[:, q, :], idb, bank[3 + cc][:, :].rearrange("p (a b) -> p a b", b=P), ALU.subtract),
                       ("x", w, 0, cc), wait=False)
                for lv in range(1, len(LEVELS)):
                    tap(4)
                    for cc in range(2):
                        q = slice(4 * cc, 4 * cc + 4)
                        if lv < len(LEVELS) - 1:
                            need(dve, PE, ("q", w, lv, cc))
                            need(dve, DV, ("x", w, lv - 1, cc))
                            x = xi[:, q, :].rearrange("p a b -> p (a b)")
                            do(dve.tensor_tensor(x, x, bank[3 + cc][:, :], ALU.subtract), ("x", w, lv, cc), wait=False)
                        need(dve, PE, ("qt", w, lv, cc))
                        need(dve, DV, ("xt", w, lv - 1, cc))
                        x = xt[:, q, :].rearrange("p a b -> p (a b)")
                        do(dve.tensor_tensor(x, x, bank[5 + cc][:, :], ALU.subtract), ("xt", w, lv, cc), wait=False)
                tap(6)
                need(dve, PE, ("rk", w))
                for cc in range(2):
                    ch = 2 * w + cc
                    do(dve.tensor_tensor(rk[:, 2 * cc:2 * cc + 2, :], bank[3][:, cc * 256:(cc + 1) * 256].rearrange("p (a b) -> p a b", b=P),
                                         kr[:, :, ch, 1, :], ALU.add), ("rk", w), wait=False)
                e2 = eye2[:, :].unsqueeze(1).to_broadcast([P, 4, 64])
                do(dve.tensor_tensor(phi, bank[4][:, 0:256].rearrange("p (a b) -> p a b", b=64), e2, ALU.add), ("phi", w), wait=False)
                need(dve, AC, "dsc")
                for cc in range(2):
                    ch = 2 * w + cc
                    if cc or w:
                        last = (w, cc - 1) if cc else (0, 1)
                        need(dve, PE, ("y", *last))
                        need(dve, DV, ("st", *last))
                    for ct in range(2):
                        do(dve.tensor_scalar(s_in[:, ct, :], state[:, ct, :], dsc[:, ct, ch, 0:1], None, ALU.mult), ("sin", w, cc), wait=False)
                    need(dve, PE, ("st", w, cc))
                    for ct in range(2):
                        do(dve.tensor_scalar(state[:, ct, :], bank[5][:, ct * 64:(ct + 1) * 64], dsc[:, ct, ch, 1:2], None, ALU.mult),
                           ("st", w, cc), wait=False)
            do(dve.memset(small[:, 34:35], 0.0), "chunks", wait=False)
            tap(62)

            for ct in range(2):
                need(dve, PE, ("gnm", ct))
                x = tmp[0][:, ct, :]
                do(dve.scalar_tensor_tensor(out=x, in0=bank[1 + ct][:, :], scalar=-1.0 / 64, in1=x, op0=ALU.mult, op1=ALU.add), ("gnd", ct))
            need(dve, PE, "lam")
            for ct in range(2):
                x = ya[:, ct, :]
                do(dve.scalar_tensor_tensor(out=x, in0=bank[3][:, :], scalar=-1.0 / 256, in1=x, op0=ALU.mult, op1=ALU.add), ("lad", ct))
            for ct in range(2):
                need(dve, AC, ("gns", ct))
                x, s = tmp[0][:, ct, :], tmp[2][:, ct, :]
                do(dve.reciprocal(s, s))
                do(dve.tensor_tensor(x, x, s, ALU.mult))
                do(dve.tensor_scalar(x, x, cvc("gn_g", ct), cvc("gn_b", ct), ALU.mult, ALU.add))
                do(dve.tensor_tensor(x, x, tmp[1][:, ct, :], ALU.add))
                g = pc[:, ct, 1:1 + TB]
                do(dve.tensor_tensor(g, g, x, ALU.mult), "yc")
            need(dve, AC, "las")
            do(dve.reciprocal(tmp[4][:, 0, :], tmp[4][:, 0, :]))
            for ct in range(2):
                do(dve.tensor_tensor(ya[:, ct, :], ya[:, ct, :], tmp[4][:, 0, :], ALU.mult), ("laz", ct), wait=False)

            for tt in range(NCH):
                st = small[:, 46:58]
                mv = small[:, 40:42]
                need(dve, R0 if tt % 2 == 0 else R1, tt)
                if tt:
                    need(dve, ST, ("u2", tt - 1))
                for n in range(2):
                    need(dve, PE, ("out", tt, n))
                    ns = slice(n * 512, (n + 1) * 512)
                    do(dve.tensor_tensor(x1[:, ns], bank[n][:, :], g1p1[:, ns], ALU.mult), ("outev", tt), wait=(n == 1))
                do(dve.scalar_tensor_tensor(out=x1, in0=xr[tt % 2], scalar=ALPHA, in1=x1, op0=ALU.mult, op1=ALU.add), ("res", tt))
                for n in range(2):
                    do(dve.bn_stats(st[:, 6 * n:6 * n + 6], x1[:, n * 512:(n + 1) * 512]), wait=(n == 1))
                do(dve.bn_aggr(mv, st), ("var", tt))
                need(dve, AC, ("std", tt))
                do(dve.reciprocal(small[:, 44:45], small[:, 44:45]))
                do(dve.tensor_scalar(x1, x1, mv[:, 0:1], small[:, 44:45], ALU.subtract, ALU.mult))
                do(dve.tensor_tensor(x1, x1, ln1g[:, :], ALU.mult))
                do(dve.tensor_tensor(x1, x1, ln1b[:, :], ALU.add), ("x1", tt))
                if tt:
                    need(dve, ST, ("u2", tt - 1))
                do(dve.tensor_tensor(u2, x1, sc2p1[:, :], ALU.mult))
                do(dve.tensor_tensor(u2, u2, sh2r[:, :], ALU.add), ("u2", tt))
                need(dve, AC, ("score", tt))
                sc, bi = rt[:, 0:64], rt[:, 64:128]
                sel, g8 = rt[:, 128:192], rt[:, 192:256]
                gs, top, rep, keep = rt[:, 256:268], rt[:, 268:276], rt[:, 276:288], rt[:, 288:296]
                msk, slots, best, w8 = rt[:, 296:360], rt[:, 360:424], rt[:, 424:432], rt[:, 432:440]
                ssum, slf, idf = rt[:, 440:441], rt[:, 448:456], rt[:, 456:464]
                g3 = lambda a: a.rearrange("p (g e) -> p g e", e=8)
                do(dve.tensor_tensor(bi, sc, ebias[:, :], ALU.add))
                for g in range(NGR):
                    do(dve.max(g8[:, 8 * g:8 * g + 8], bi[:, 8 * g:8 * g + 8]), wait=(g == NGR - 1))
                do(dve.memset(gs[:, 8:12], 1.0e30), wait=False)
                do(dve.tensor_tensor(gs[:, 0:8], g3(g8)[:, :, 0], g3(g8)[:, :, 1], ALU.add))
                do(dve.max(top, gs))
                do(dve.match_replace(rep, top, gs, NEG))
                do(dve.tensor_scalar(keep, rep[:, 0:8], NEG, None, ALU.is_equal))
                kb = keep.unsqueeze(2).to_broadcast([P, NGR, 8])
                do(dve.tensor_tensor(g3(msk), g3(bi), kb, ALU.mult))
                do(dve.tensor_scalar(keep, keep, -NEG, NEG, ALU.mult, ALU.add))
                do(dve.tensor_tensor(g3(msk), g3(msk), kb, ALU.add))
                do(dve.max(best, msk))
                do(dve.match_replace(sel, best, msk, -NEG))
                do(dve.tensor_scalar(sel, sel, -NEG, None, ALU.is_equal), ("sel", tt))
                do(dve.max_index(idx8[:, :], best, msk))
                do(dve.tensor_copy(idf, idx8[:, :]))
                oh = flat(tmp[4])[:, 0:512].rearrange("p (j e) -> p j e", e=NE)
                pr = flat(tmp[4])[:, 512:1024].rearrange("p (j e) -> p j e", e=NE)
                do(dve.tensor_tensor(oh, iota_e[:, :, :], idf.unsqueeze(2).to_broadcast([P, TOPK, NE]), ALU.is_equal))
                do(dve.tensor_tensor(pr, oh, sc.unsqueeze(1).to_broadcast([P, TOPK, NE]), ALU.mult))
                do(dve.tensor_reduce(w8, pr, AX_X, ALU.add))
                do(dve.tensor_reduce(ssum, w8, AX_X, ALU.add))
                do(dve.reciprocal(ssum, ssum))
                need(dve, AC, ("silu", tt))
                do(dve.tensor_tensor(hs, hs, bank[5][:, 256:512], ALU.mult), ("hs", tt), wait=False)
                need(dve, PE, ("rank", tt))
                do(dve.scalar_tensor_tensor(out=slots, in0=iota_e[:, 0, :], scalar=float(CAP), in1=bank[7][:, 0:NE],
                                            op0=ALU.mult, op1=ALU.add))
                do(dve.tensor_tensor(cum_sel[:, :], cum_sel[:, :], sel, ALU.add), ("cum", tt), wait=False)
                do(dve.tensor_tensor(pr, oh, slots.unsqueeze(1).to_broadcast([P, TOPK, NE]), ALU.mult))
                do(dve.tensor_reduce(slf, pr, AX_X, ALU.add))
                if tt:
                    dve.wait_ge(lists_written, it * (16 * TOPK * NCH) + 16 * TOPK * tt)
                do(dve.tensor_copy(slot[:, :], slf), wait=False)
                do(dve.tensor_scalar(tw[:, :, 1].bitcast(F32), w8, ssum, ROUTED_SCALE, ALU.mult, ALU.mult), ("routed", tt), wait=False)

        @block.gpsimd
        def _(pool):
            do = stepper(pool, PO)
            need(pool, PE, ("proj", NPT - 1))
            need(pool, DV, ("ut", DC - 1))
            do(pool.memset(gm, 0.0), "zero")
            for w in range(2):
                need(pool, DV, ("gm", w, 7))
                for lv in range(len(LEVELS)):
                    if lv:
                        need(pool, PE, ("p", w, lv - 1, 1) if lv > 1 else ("q", w, 0, 1))
                    if lv == 1:
                        need(pool, DV, ("xt", w, 0, 1))
                    do(pool.tensor_tensor(em, gm[:, :, 0:P], levm[:, lv, :].unsqueeze(1).to_broadcast([P, 8, P]), ALU.mult),
                       ("em", w, lv), wait=False)
            need(pool, DV, "conv_a")
            do(pool.tensor_copy(hid[:, :, 0:HALO_A], hid[:, :, TB:TB + HALO_A]), wait=False)
            do(pool.tensor_copy(xb[:, :, 0:HALO_B], xb[:, :, TB:TB + HALO_B]), wait=False)
            do(pool.tensor_copy(pd[:, :, 0:HALO_D], pd[:, :, TB:TB + HALO_D]), wait=False)
            do(pool.tensor_copy(pc[:, :, 0], pclast[:, :]), wait=False)
            for tt in range(NCH):
                need(pool, DV, ("routed", tt))
                do(pool.tensor_copy(tw[:, :, 0], tok_id[:, bass.ds(it * NCH + tt, 1)].to_broadcast([P, TOPK])))
                for j in range(TOPK):
                    pool.indirect_dma_start(out=LISTS[:, :], out_offset=bass.IndirectOffsetOnAxis(ap=slot[:, j:j + 1], axis=0),
                                            in_=tw[:, j, :], in_offset=None).then_inc(lists_written, 16)
            pool.wait_ge(lists_written, it * (16 * TOPK * NCH) + 16 * TOPK * NCH)
            do(pool.tensor_tensor(pclast[:, 0:1], epsc[:, 0:1], epsc[:, 1:2], ALU.add))
      nc.all_engine_barrier(sems_to_clear=span)
    mix.close()

    PE, AC, DV, PO, XL, WE, WO, PL, R0, R1, SL, ST, SS = stage("tables")
    moe = ExitStack()
    tab = sb(moe, "tab", [1, NBLK, 4], I32)
    start = sb(moe, "start", [1, NE], I32)
    used = sb(moe, "used", [1, 4], I32)
    w13 = sb(moe, "w13", [P, 2, DC, 512])
    w2 = sb(moe, "w2", [P, 2, 2, D])
    lists = sb(moe, "lists", [P, NBLK + 2, 2], I32)
    small_t = ExitStack()
    nb = sb(small_t, "nb", [NE, 4])
    nbi = sb(small_t, "nbi", [NE, 2], I32)
    iob = sb(small_t, "iob", [NE, NBLK])
    cmp = sb(small_t, "cmp", [NE, NBLK])
    r = [sb(small_t, f"row{i}", [1, NBLK]) for i in range(5)]
    ri = [sb(small_t, f"rowi{i}", [1, NBLK], I32) for i in range(2)]
    with nc.Block() as block:
        @block.tensor
        def _(pe):
            def mark(mm, key):
                mm.then_inc(PE.sem, PE.mark(key))
            mark(pe.matmul(bank[0][0:NE, 0:1], cum_sel[:, :], ones[:, 0:1], start=True, stop=True), "count")
            need(pe, DV, "nb")
            mark(pe.matmul(bank[1][0:NE, 0:1], maskf[0:NE, P:P + NE], nb[:, 0:1], start=True, stop=True), "end")
            mark(pe.matmul(bank[2][0:1, 0:NE], nb[:, 0:1], maskf[0:NE, 0:NE], start=True, stop=True), "start")
            need(pe, DV, "cmp")
            mark(pe.matmul(bank[3][0:1, 0:NBLK], ones[0:NE, 0:1], cmp[:, :], start=True, stop=True), "e")
            mark(pe.matmul(bank[4][0:1, 0:NBLK], nb[:, 0:1], cmp[:, :], start=True, stop=True), "s")
            mark(pe.matmul(bank[5][0:1, 0:1], nb[:, 0:1], ones[0:NE, 0:1], start=True, stop=True), "used")

        @block.gpsimd
        def _(pool):
            do = stepper(pool, PO)
            do(pool.iota(iob[:, :], pattern=[[1, NBLK]], base=0, channel_multiplier=0, allow_small_or_imprecise_dtypes=True), "iob")

        @block.vector
        def _(dve):
            do = stepper(dve, DV)
            need(dve, PE, "count")
            do(dve.tensor_scalar(nbi[:, 0:1], bank[0][0:NE, 0:1], float(P - 1), None, ALU.add))
            do(dve.tensor_scalar(nbi[:, 1:2], nbi[:, 0:1], 7, None, ALU.arith_shift_right))
            do(dve.tensor_copy(nb[:, 0:1], nbi[:, 1:2]), "nb")
            need(dve, PE, "end")
            do(dve.tensor_copy(nb[:, 1:2], bank[1][0:NE, 0:1]))
            need(dve, PO, "iob")
            do(dve.tensor_scalar(cmp[:, :], iob[:, :], nb[:, 1:2], None, ALU.is_ge), "cmp")
            need(dve, PE, "start")
            do(dve.tensor_copy(start[:, :], bank[2][0:1, 0:NE]))
            need(dve, PE, "used")
            do(dve.tensor_copy(used[:, 0:1], bank[5][0:1, 0:1]))
            do(dve.tensor_tensor(r[0][:, :], iob[0:1, :], bank[4][0:1, 0:NBLK], ALU.subtract))
            do(dve.tensor_scalar(r[1][:, :], bank[3][0:1, 0:NBLK], float(CAP // P), None, ALU.mult))
            do(dve.tensor_tensor(r[0][:, :], r[0][:, :], r[1][:, :], ALU.add))
            do(dve.tensor_scalar(tab[:, :, 0], r[0][:, :], float(P), float(NE * CAP), ALU.mult, ALU.min))
            do(dve.tensor_scalar(ri[0][:, :], bank[3][0:1, 0:NBLK], float(NE - 1), None, ALU.min))
            do(dve.tensor_scalar(ri[1][:, :], ri[0][:, :], 1, None, ALU.bitwise_and))
            do(dve.tensor_copy(r[1][:, :], ri[0][:, :]))
            do(dve.tensor_copy(r[2][:, :], ri[1][:, :]))
            do(dve.tensor_copy(tab[:, :, 1], r[2][:, :]))
            do(dve.tensor_tensor(r[3][:, :], r[1][:, :], r[2][:, :], ALU.subtract))
            do(dve.tensor_scalar(tab[:, :, 2], r[3][:, :], 8.0, 16.0, ALU.mult, ALU.add))
            do(dve.tensor_tensor(r[3][:, :], r[1][:, :], r[2][:, :], ALU.add))
            do(dve.tensor_scalar(tab[:, :, 3], r[3][:, :], 8.0, 16.0, ALU.mult, ALU.max))
    nc.all_engine_barrier(sems_to_clear=span)
    small_t.close()

    xg = [sb(moe, f"xg{i}", [P, D]) for i in range(2)]
    xgt = [sb(moe, f"xgt{i}", [P, DC, P]) for i in range(2)]
    hm = [sb(moe, f"hm{i}", [P, DE]) for i in range(2)]
    hmt = [sb(moe, f"hmt{i}", [P, DE]) for i in range(2)]
    yo = [sb(moe, f"yo{i}", [P, D]) for i in range(2)]
    gidx = [sb(moe, f"gidx{i}", [P, 2], I32) for i in range(2)]
    sidx = [sb(moe, f"sidx{i}", [P, 2], I32) for i in range(2)]
    zero = sb(moe, "zero", [P, 1], I32)

    def sem(name):
        return top.enter_context(nc.semaphore(name))

    w13_loaded = [sem("w13_even_loaded"), sem("w13_odd_loaded")]
    w2_loaded = [sem("w2_even_loaded"), sem("w2_odd_loaded")]
    lists_loaded = sem("lists_loaded")
    idx_ready = sem("idx_ready")
    x_gathered = [sem("x0_gathered"), sem("x1_gathered")]
    x_turned = sem("x_turned")
    xt_ready_d = sem("xt_ready_d")
    xt_ready_a = sem("xt_ready_a")
    h_ready = sem("h_ready")
    gate_ready = sem("gate_ready")
    hm_ready = sem("hm_ready")
    h_turned = sem("h_turned")
    ht_ready = sem("ht_ready")
    y_ready = sem("y_ready")
    yo_d = sem("yo_d")
    yo_a = sem("yo_a")
    y_added = [sem("y0_added"), sem("y1_added")]
    yo_free = sem("yo_free")
    NPAIR = NBLK // 2
    def lead(eng, *sems):
        for s in sems:
            eng.sem_inc(s, 1)

    with nc.Block() as block:
        @block.sync
        def _(sp):
            w13v = t["w13"].rearrange("e (p c) n -> e p c n", c=DC)
            w2v = t["w2"].rearrange("e (p c) n -> e p c n", c=2)

            def load(e, q):
                sp.dma_start(w13[:, q, :, :], w13v[bass.ds(e, 1)].rearrange("e p c n -> p (e c) n")).then_inc(w13_loaded[q], 16)
                sp.dma_start(w2[:, q, :, :], w2v[bass.ds(e, 1)].rearrange("e p c n -> p (e c) n")).then_inc(w2_loaded[q], 16)

            for q in range(2):
                load(q, q)
            with sp.Fori(1, NE // 2) as i:
                for q in range(2):
                    first = sp.value_load(start[0:1, bass.ds(i * 2 + (q - 1), 1)], min_val=0, max_val=NBLK)
                    sp.wait_ge(y_ready, first + 1)
                    load(i * 2 + q, q)
            for q in range(2):
                sp.wait_ge(w13_loaded[q], 16 * NE // 2)
                sp.wait_ge(w2_loaded[q], 16 * NE // 2)
            sp.drain()

        @block.tensor
        def _(pe):
            lead(pe, y_ready)
            n = pe.value_load(used[0:1, 0:1], min_val=0, max_val=NBLK)
            with pe.Fori(0, NPAIR) as i:
                with pe.If(n > i * 2):
                    def turn_x(q):
                        b = i * 2 + q
                        pe.wait_ge(x_gathered[q], (i + 1) * 16)
                        pe.wait_ge(xt_ready_d, b + 1)
                        pe.wait_ge(xt_ready_a, b + 1)
                        v = xg[q][:, :].rearrange("p (n c) -> p n c", c=DC)
                        for k in range(DC):
                            mm = pe.transpose(bank[k // 4][:, (k % 4) * P:(k % 4 + 1) * P], v[:, :, k], ident[:, :])
                            if k % 4 == 3:
                                mm.then_inc(x_turned, 1)

                    def up(q):
                        b = i * 2 + q
                        par = pe.value_load(tab[0:1, bass.ds(b, 1), 1], min_val=0, max_val=1)
                        even = pe.value_load(tab[0:1, bass.ds(b, 1), 2], min_val=0, max_val=16 * NE)
                        odd = pe.value_load(tab[0:1, bass.ds(b, 1), 3], min_val=0, max_val=16 * NE)
                        pe.wait_ge(w13_loaded[0], even)
                        pe.wait_ge(w13_loaded[1], odd)
                        pe.wait_ge(w2_loaded[0], even)
                        pe.wait_ge(w2_loaded[1], odd)
                        pe.wait_ge(xt_ready_d, b + 2)
                        pe.wait_ge(xt_ready_a, b + 2)
                        w = w13[:, :, :, :].rearrange("p q c n -> p (q c) n")
                        for k in range(DC):
                            mm = pe.matmul(bank[2 + q][:, :], xgt[q][:, k, :], w[:, bass.ds(par * DC + k, 1), :].rearrange("p a n -> p (a n)"),
                                           start=(k == 0), stop=(k == DC - 1))
                        mm.then_inc(h_ready, 1)
                        return par

                    def turn_h(q):
                        pe.wait_ge(hm_ready, i * 2 + q + 1)
                        v = hm[q][:, :].rearrange("p (n c) -> p n c", c=2)
                        for k in range(2):
                            mm = pe.transpose(bank[4][:, k * P:(k + 1) * P], v[:, :, k], ident[:, :])
                        mm.then_inc(h_turned, 1)

                    def down(q, par):
                        b = i * 2 + q
                        pe.wait_ge(ht_ready, b + 1)
                        pe.wait_ge(yo_d, b + 1)
                        pe.wait_ge(yo_a, b + 1)
                        w = w2[:, :, :, :].rearrange("p q c n -> p (q c) n")
                        for h in range(2):
                            for k in range(2):
                                mm = pe.matmul(bank[5 + h][:, :], hmt[q][:, k * P:(k + 1) * P],
                                               w[:, bass.ds(par * 2 + k, 1), h * 512:(h + 1) * 512].rearrange("p a n -> p (a n)"),
                                               start=(k == 0), stop=(k == 1))
                        mm.then_inc(y_ready, 1)

                    turn_x(0)
                    p0 = up(0)
                    turn_x(1)
                    turn_h(0)
                    p1 = up(1)
                    down(0, p0)
                    turn_h(1)
                    down(1, p1)

        @block.scalar
        def _(act):
            lead(act, xt_ready_a, yo_a)
            n = act.value_load(used[0:1, 0:1], min_val=0, max_val=NBLK)
            act.wait_ge(lists_loaded, 16 * NBLK)
            with act.Fori(0, NPAIR) as i:
                with act.If(n > i * 2):
                    def copy_x(q):
                        b = i * 2 + q
                        act.wait_ge(x_turned, b * 2 + 2)
                        act.activation(xgt[q][:, 4:8, :].rearrange("p a b -> p (a b)"), bank[1][:, :], ACT.Copy).then_inc(xt_ready_a, 1)

                    def gate(q):
                        b = i * 2 + q
                        act.wait_ge(h_ready, b + 1)
                        act.activation(hm[q][:, :], bank[2 + q][:, 0:DE], ACT.Silu).then_inc(gate_ready, 1)

                    def out(q):
                        b = i * 2 + q
                        act.wait_ge(y_ready, b + 2)
                        act.wait_ge(yo_free, b + 1)
                        act.activation(yo[q][:, 512:1024], bank[6][:, :], ACT.Copy,
                                       scale=lists[:, bass.ds(b, 1), 1].bitcast(F32)).then_inc(yo_a, 1)

                    copy_x(0)
                    gate(0)
                    copy_x(1)
                    gate(1)
                    out(0)
                    out(1)

        @block.vector
        def _(dve):
            lead(dve, xt_ready_d, yo_d)
            n = dve.value_load(used[0:1, 0:1], min_val=0, max_val=NBLK)
            dve.wait_ge(lists_loaded, 16 * NBLK)
            with dve.Fori(0, NPAIR) as i:
                with dve.If(n > i * 2):
                    def copy_x(q):
                        b = i * 2 + q
                        dve.wait_ge(x_turned, b * 2 + 1)
                        dve.tensor_copy(xgt[q][:, 0:4, :].rearrange("p a b -> p (a b)"), bank[0][:, :]).then_inc(xt_ready_d, 1)

                    def times_up(q):
                        b = i * 2 + q
                        dve.wait_ge(gate_ready, b + 1)
                        dve.tensor_tensor(hm[q][:, :], hm[q][:, :], bank[2 + q][:, DE:2 * DE], ALU.mult).then_inc(hm_ready, 1)

                    def copy_h(q):
                        b = i * 2 + q
                        dve.wait_ge(h_turned, b + 1)
                        dve.tensor_copy(hmt[q][:, :], bank[4][:, 0:DE]).then_inc(ht_ready, 1)

                    def out(q):
                        b = i * 2 + q
                        dve.wait_ge(y_ready, b + 2)
                        dve.wait_ge(yo_free, b + 1)
                        dve.tensor_scalar(yo[q][:, 0:512], bank[5][:, :], lists[:, bass.ds(b, 1), 1].bitcast(F32), None,
                                          ALU.mult).then_inc(yo_d, 1)

                    copy_x(0)
                    times_up(0)
                    copy_x(1)
                    copy_h(0)
                    times_up(1)
                    out(0)
                    copy_h(1)
                    out(1)

        @block.gpsimd
        def _(pool):
            lead(pool, yo_free, yo_free)
            n = pool.value_load(used[0:1, 0:1], min_val=0, max_val=NBLK)
            lv = LISTS
            with pool.Fori(0, NBLK) as b:
                row = pool.value_load(tab[0:1, bass.ds(b, 1), 0], min_val=0, max_val=(NE + 1) * CAP - P)
                pool.dma_start(lists[:, bass.ds(b, 1), :].rearrange("p a c -> p (a c)"), lv[bass.ds(row, P), :]).then_inc(lists_loaded, 16)
            pool.wait_ge(lists_loaded, 16 * NBLK)
            pool.memset(lists[:, NBLK:NBLK + 2, :], 0).then_inc(idx_ready, 1)
            pool.memset(zero[:, :], 0).then_inc(idx_ready, 1)
            pool.wait_ge(idx_ready, 2)
            pool.sem_clear(idx_ready)

            def places(dst, b):
                pool.tensor_copy(dst[:, 1:2], lists[:, bass.ds(b, 1), 0]).then_inc(idx_ready, 1)
                pool.wait_ge(idx_ready, 1)

            def gather(q):
                pool.tensor_tensor(gidx[q][:, 0:1], gidx[q][:, 1:2], zero[:, :], ALU.add).then_inc(idx_ready, 1)
                pool.wait_ge(idx_ready, 2)
                pool.indirect_dma_start(out=xg[q][:, :], out_offset=None, in_=U2[:, :],
                                        in_offset=bass.IndirectOffsetOnAxis(ap=gidx[q][:, 0:1], axis=0)).then_inc(x_gathered[q], 16)
                pool.sem_clear(idx_ready)

            for q in range(2):
                places(gidx[q], q)
                gather(q)
            with pool.Fori(0, NPAIR) as i:
                with pool.If(n > i * 2):
                    for q in range(2):
                        places(gidx[q], i * 2 + q + 2)
                        pool.wait_ge(x_turned, i * 4 + 2 * q + 2)
                        pool.wait_ge(x_gathered[q], (i + 1) * 16)
                        gather(q)
                    for q in range(2):
                        b = i * 2 + q
                        places(sidx[q], b)
                        pool.wait_ge(yo_d, b + 2)
                        pool.wait_ge(yo_a, b + 2)
                        pool.tensor_tensor(sidx[q][:, 0:1], sidx[q][:, 1:2], zero[:, :], ALU.add).then_inc(idx_ready, 1)
                        pool.wait_ge(idx_ready, 2)
                        pool.indirect_dma_start(out=YACC[:, :], out_offset=bass.IndirectOffsetOnAxis(ap=sidx[q][:, 0:1], axis=0),
                                                in_=yo[q][:, :], in_offset=None, compute_op=ALU.add).then_inc(y_added[q], 16)
                        pool.sem_clear(idx_ready)
                        pool.wait_ge(y_added[q], (i + 1) * 16)
                        pool.sem_inc(yo_free, 1)
            pairs = pool.snap((n + 1) // 2)
            for q in range(2):
                pool.wait_ge(y_added[q], pairs * 16)
                pool.wait_ge(x_gathered[q], pairs * 16 + 16)
            pool.tensor_tensor(zero[:, :], gidx[0][:, 1:2], gidx[0][:, 1:2], ALU.subtract).then_inc(idx_ready, 1)
            pool.wait_ge(idx_ready, 1)
    moe.close()

    fin = ExitStack()
    PE, AC, DV, PO, XL, WE, WO, PL, R0, R1, SL, ST, SS = stage("final")
    xa = [sb(fin, f"xa{i}", [P, D]) for i in range(2)]
    yy = [sb(fin, f"yy{i}", [P, D]) for i in range(2)]
    ln2g = sb(fin, "ln2g", [P, D])
    ln2b = sb(fin, "ln2b", [P, D])
    fs = sb(fin, "fs", [P, 32])
    NT = SEQ // P
    with nc.Fori(0, NT // 2) as it:
        with nc.Block() as block:
            @block.sync
            def _(sp):
                sp.dma_start(ln2g[:, :], t["ln2_g"][0, :].partition_broadcast(P)).then_inc(PL.sem, 16)
                sp.dma_start(ln2b[:, :], t["ln2_b"][0, :].partition_broadcast(P)).then_inc(PL.sem, 16)
                for q in range(2):
                    rows_ = bass.ds(it * 2 * P + q * P, P)
                    sp.dma_start(xa[q][:, :], X1[rows_, :]).then_inc((R0, R1)[q].sem, 16)
                    sp.dma_start(yy[q][:, :], YACC[rows_, :]).then_inc((WE, WO)[q].sem, 16)
                for q in range(2):
                    need(sp, DV, ("o", q))
                    sp.dma_start(t["out"][bass.ds(it * 2 * P + q * P, P), :], xa[q][:, :]).then_inc(ST.sem, 16)
                sp.wait_ge(ST.sem, 32)
                sp.drain()

            @block.scalar
            def _(act):
                do = stepper(act, AC)
                for q in range(2):
                    need(act, DV, ("var", q))
                    do(act.activation(fs[:, 16 * q + 14:16 * q + 15], fs[:, 16 * q + 13:16 * q + 14], ACT.Sqrt, bias=epsc[:, 0:1]),
                       ("std", q), wait=False)

            @block.vector
            def _(dve):
                do = stepper(dve, DV)
                for q in range(2):
                    x, y = xa[q][:, :], yy[q][:, :]
                    st, mv, sd = fs[:, 16 * q:16 * q + 12], fs[:, 16 * q + 12:16 * q + 14], fs[:, 16 * q + 14:16 * q + 15]
                    dve.wait_ge((R0, R1)[q].sem, 16)
                    dve.wait_ge((WE, WO)[q].sem, 16)
                    do(dve.tensor_tensor(y, y, g2p1[:, :], ALU.mult))
                    do(dve.scalar_tensor_tensor(out=x, in0=x, scalar=ALPHA, in1=y, op0=ALU.mult, op1=ALU.add))
                    for n in range(2):
                        do(dve.bn_stats(st[:, 6 * n:6 * n + 6], x[:, n * 512:(n + 1) * 512]), wait=(n == 1))
                    do(dve.bn_aggr(mv, st), ("var", q))
                    need(dve, AC, ("std", q))
                    do(dve.reciprocal(sd, sd))
                    do(dve.tensor_scalar(x, x, mv[:, 0:1], sd, ALU.subtract, ALU.mult))
                    dve.wait_ge(PL.sem, 32)
                    do(dve.tensor_tensor(x, x, ln2g[:, :], ALU.mult))
                    do(dve.tensor_tensor(x, x, ln2b[:, :], ALU.add), ("o", q))
        nc.all_engine_barrier(sems_to_clear=span)
    fin.close()
    top.close()


_CHANNEL = [n for n in CV]
_TILES = [8, 9, 10, 11, 12, 13, 14, 2, 0, 3, 1, 4, 5, 6, 7, 15, 16, 17, 18, 19, 20]


def kernel(**inputs):
    import numpy as _np
    import concourse.bacc as _bacc
    from concourse import mybir as _mybir
    from concourse.bass_utils import run_bass_kernel_spmd as _run

    x = {k: _np.asarray(v) for k, v in inputs.items()}
    arrays = {
        "x": x["x"][0],
        "xt": x["x"][0].T.reshape(P, DC, SEQ),
        "c": x["c"],
        "w_in": x["w_in"][0].reshape(P, DC, NPT, P)[:, :, _TILES].reshape(P, DC, NGRP, GRP * P).transpose(0, 2, 1, 3),
        "chan": _np.concatenate([x[n][0].reshape(-1, P) for n in _CHANNEL]).T,
        "lora": _np.concatenate([x[n][0] for n in ("w_w2", "w_a2", "w_g2")]),
    }
    for n in ("w_mod", "w_out", "w_rg", "w_ig", "w_router", "w13", "w2", "ws13", "ws2"):
        arrays[n] = x[n][0]
    for n in ("b_mod", "e_bias", "ln1_g", "ln1_b", "ln2_g", "ln2_b"):
        arrays[n] = x[n]
    arrays = {f"in_{k}": _np.ascontiguousarray(v) for k, v in arrays.items()}
    for Count.final in (False, True):
        nc = _bacc.Bacc("TRN2", target_bir_lowering=False, num_devices=1)
        t = {k[3:]: nc.dram_tensor(k, a.shape, _mybir.dt.from_np(a.dtype), kind="ExternalInput").ap() for k, a in arrays.items()}
        t["out"] = nc.dram_tensor("out_rows", (SEQ, D), F32, kind="ExternalOutput").ap()
        build(nc, t)
    r = _run(nc, [arrays], core_ids=[0])
    return r.results[0]["out_rows"].reshape(x["x"].shape)
```

```python
from contextlib import ExitStack

import concourse.bass as bass
from concourse import mybir

P = 128
D = 1024
DC = D // P
SEQ = 2048
TB = 512
NTB = SEQ // TB
NCH = TB // P
NPROJ = 2688
NPT = NPROJ // P
GRP = 3
NGRP = NPT // GRP
HALO_A, HALO_B, HALO_D = 30, 3, 2
NE = 64
TOPK = 8
NGR = 8
DE = 256
NBLK = 192
CAP = SEQ
LEVELS = [1, 2, 4, 8, 16, 32, 64]
ALPHA = 2.0 ** 0.25
LN_EPS = 1e-5
GN_EPS = 64e-5
ROUTED_SCALE = 2.5
EM05 = 0.6065306597126334
NEG = -1.0e30

F32 = mybir.dt.float32
F32R = mybir.dt.float32r
I32 = mybir.dt.int32
U32 = mybir.dt.uint32
ACT = mybir.ActivationFunctionType
ALU = mybir.AluOpType
AX_X = mybir.AxisListType.X

CV = {}
for _n, _w in (("conv_a", 62), ("conv_a_bias", 2), ("ln_a_g", 2), ("ln_a_b", 2), ("conv_b", 8),
               ("conv_b_bias", 2), ("b_rg", 2), ("b_ig", 2), ("lru_lambda", 2), ("mu_c", 7), ("w0", 2),
               ("a0", 2), ("k_k", 2), ("k_a", 2), ("r_k", 2), ("gn_g", 2), ("gn_b", 2), ("conv_d", 6)):
    CV[_n] = sum(w for _, w in CV.values()), _w
NCV = sum(w for _, w in CV.values())


class Count:

    seen = {}

    def __init__(self, sem, part):
        self.sem, self.n, self.part = sem, 0, (part, sem.name)

    def mark(self, key, by=1):
        self.n += by
        Count.seen[self.part, key] = self.n
        return by

    def at(self, key):
        if Count.final:
            return Count.seen[self.part, key]
        return 1

    final = False


def build(nc, t):
    top = ExitStack()

    def dram(name, shape, dt=F32):
        return nc.dram_tensor(name, shape, dt, kind="Internal").ap()

    U2 = dram("u2_rows", (SEQ + P, D))
    X1 = dram("x1_rows", (SEQ, D))
    YACC = dram("y_acc", (SEQ + P, D))
    LISTS = dram("expert_lists", ((NE + 1) * CAP, 2), I32)

    names = ["pe_steps", "act_steps", "dve_steps", "pool_steps", "x_loaded", "w_even_loaded", "w_odd_loaded",
             "params_loaded", "rows0_loaded", "rows1_loaded", "shared_w_loaded", "rows_stored", "shared_stored"]
    handles = [top.enter_context(nc.semaphore(n)) for n in names]
    span = range(min(h.num for h in handles), max(h.num for h in handles) + 1)
    assert len(span) == len(handles)
    lists_written = top.enter_context(nc.semaphore("lists_written"))

    def stage(tag):
        return [Count(h, tag) for h in handles]

    def need(eng, c, key):
        eng.wait_ge(c.sem, c.at(key))

    def stepper(eng, c):
        def do(ins, key=None, wait=True):
            ins.then_inc(c.sem, c.mark(key if key is not None else ("step", c.n)))
            if wait:
                eng.wait_ge(c.sem, c.n)
        return do

    def sb(stack, name, shape, dt=F32):
        return stack.enter_context(nc.sbuf_tensor(name, shape, dt))

    bank = [top.enter_context(nc.psum_tensor(f"bank{i}", [P, 512], F32)) for i in range(8)]

    ident = sb(top, "ident", [P, P])
    ones = sb(top, "ones", [P, P])
    maskf = sb(top, "maskf", [P, 512])
    cum_sel = sb(top, "cum_sel", [P, NE])
    g2p1 = sb(top, "g2p1", [P, D])
    epsc = sb(top, "epsc", [P, 4])

    mix = ExitStack()

    def mb(name, shape, dt=F32):
        return sb(mix, name, shape, dt)

    levm = mb("levm", [P, len(LEVELS), P])
    blk1 = mb("blk1", [P, P])
    scan_keep = mb("scan_keep", [P, TB])
    iota_e = mb("iota_e", [P, TOPK, NE])
    tok_id = mb("tok_id", [P, SEQ // P], I32)
    eye2 = mb("eye2", [P, 64])
    cv = mb("cv", [P, NCV])
    chalf = mb("chalf", [P, 2])
    ebias = mb("ebias", [P, NE])
    shcol = mb("shcol", [P, DC])
    sccol = mb("sccol", [P, DC])
    wout = mb("wout", [P, DC, D])
    wrt = mb("wrt", [P, DC, NE])
    lora = mb("lora", [P, 256])
    wri = mb("wri", [P, 2, 2, P])
    g1p1 = mb("g1p1", [P, D])
    sc2p1 = mb("sc2p1", [P, D])
    sh2r = mb("sh2r", [P, D])
    ln1g = mb("ln1g", [P, D])
    ln1b = mb("ln1b", [P, D])
    hid = mb("hid", [P, 2, HALO_A + TB])
    ya = mb("ya", [P, 2, TB])
    xb = mb("xb", [P, 2, HALO_B + TB])
    yb = mb("yb", [P, 2, TB])
    hlast = mb("hlast", [P, 2])
    pd = mb("pd", [P, 2, HALO_D + TB])
    yd = mb("yd", [P, 2, TB])
    pc = mb("pc", [P, 7, 1 + TB])
    pclast = mb("pclast", [P, 7])
    tmp = [mb(f"tmp{i}", [P, 2, TB]) for i in range(7)]
    kr = mb("kr", [P, 2, NCH, 2, P])
    bh = mb("bh", [P, 2, TB])
    kh = mb("kh", [P, 2, TB])
    state = mb("state", [P, 2, 64])
    s_in = mb("s_in", [P, 2, 64])
    dsc = mb("dsc", [P, 2, NCH, 2])
    small = mb("small", [P, 64])
    rt = mb("rt", [P, 512])
    tw = mb("tw", [P, TOPK, 2], I32)
    slot = mb("slot", [P, TOPK], I32)
    idx8 = mb("idx8", [P, TOPK], U32)
    ARENA = 45 * 256
    arena = mb("arena", [P, ARENA])
    taken = [0]

    def cut(*dims):
        n = 1
        for d in dims:
            n *= d
        a = arena[:, taken[0]:taken[0] + n]
        taken[0] += n
        assert taken[0] <= ARENA, taken
        if len(dims) == 2:
            return a.rearrange("p (a b) -> p a b", a=dims[0])
        if len(dims) == 3:
            return a.rearrange("p (a b c) -> p a b c", a=dims[0], b=dims[1])
        return a

    def cvc(name, i=0):
        o, w = CV[name]
        assert i < w
        return cv[:, o + i:o + i + 1]

    def flat(a):
        return a[:, :, :].rearrange("p a b -> p (a b)")

    PE, AC, DV, PO, XL, WE, WO, PL, R0, R1, SL, ST, SS = stage("setup")
    MC = 6 * D // 512
    taken[0] = 0
    wm = [cut(DC, 512) for _ in range(2)]
    crep = cut(DC, P)
    rows = [flat(kh), flat(bh), g1p1[:, :], sh2r[:, :], sc2p1[:, :], g2p1[:, :]]
    brow = [flat(x) for x in (*tmp[0:5], yd)]
    listpat = kr[0:NE + 1, :, :, :, :].rearrange("p a b c d -> p (a b c d)").bitcast(I32)
    with nc.Block() as block:
        @block.gpsimd
        def _(pool):
            do = stepper(pool, PO)
            for a, v in ((ones, 1.0), (ident, 0.0), (maskf, 1.0), (levm, 0.0), (blk1, 0.0), (scan_keep, 1.0), (wri, 0.0),
                         (hid, 0.0), (xb, 0.0), (pd, 0.0), (pc, 0.0), (hlast, 0.0), (state, 0.0), (cum_sel, 0.0), (eye2, 0.0)):
                do(pool.memset(a[tuple([slice(None)] * len(a.shape))], v), ("set", a.name), wait=False)
            for j, v in enumerate((LN_EPS, 1e-12, GN_EPS, 1.0)):
                do(pool.memset(epsc[:, j:j + 1], v), ("eps", j))
            do(pool.affine_select(out=ident[:, :], in_=ident[:, :], compare_op=ALU.not_equal, fill=1.0, base=0,
                                  pattern=[[-1, P]], channel_multiplier=1))
            for j in range(4):
                m = maskf[:, j * P:(j + 1) * P]
                do(pool.affine_select(out=m, in_=m, compare_op=ALU.is_ge if j % 2 else ALU.is_gt, fill=0.0, base=0,
                                      pattern=[[1, P]], channel_multiplier=-1))
            for j, m in enumerate(LEVELS):
                nb = P // (2 * m)
                v = levm[:, j, :].rearrange("p (n h m) -> p n h m", h=2, m=m)[:, :, 1, :]
                do(pool.memset(v, 1.0))
                do(pool.affine_select(out=v, in_=v, compare_op=ALU.is_ge, fill=0.0, base=0,
                                      pattern=[[-2 * m, nb], [0, m]], channel_multiplier=1))
                do(pool.affine_select(out=v, in_=v, compare_op=ALU.is_ge, fill=0.0, base=m - 1,
                                      pattern=[[2 * m, nb], [0, m]], channel_multiplier=-1))
            for h in range(2):
                do(pool.memset(blk1[64 * h:64 * h + 64, 64 * h:64 * h + 64], 1.0))
                e = eye2[64 * h:64 * h + 64, :]
                do(pool.affine_select(out=e, in_=e, compare_op=ALU.not_equal, fill=1.0, base=0,
                                      pattern=[[-1, 64]], channel_multiplier=1))
            do(pool.memset(scan_keep[:, :].rearrange("p (c n) -> p c n", n=P)[:, :, 0:1], 0.0))
            do(pool.iota(iota_e[:, :, :], pattern=[[0, TOPK], [1, NE]], base=0, channel_multiplier=0,
                         allow_small_or_imprecise_dtypes=True))
            do(pool.iota(tok_id[:, :], pattern=[[P, SEQ // P]], base=0, channel_multiplier=1))
            lp = listpat.rearrange("p (b n c) -> p b n c", n=P, c=2)
            do(pool.memset(lp[:, :, :, 1], 0))
            do(pool.iota(lp[:, :, :, 0], pattern=[[0, CAP // P // 2], [1, P]], base=SEQ, channel_multiplier=0), "list")

        @block.sync
        def _(sp):
            sp.dma_start(small[:, 0:DC], t["c"].rearrange("a (p c) -> p (a c)", c=DC)).then_inc(XL.sem, 16)
            w = t["w_mod"].rearrange("(p c) n -> p c n", c=DC)
            for j in range(MC):
                if j >= 2:
                    need(sp, PE, ("mod", j - 2))
                c = (WE, WO)[j % 2]
                sp.dma_start(wm[j % 2], w[:, :, j * 512:(j + 1) * 512]).then_inc(c.sem, c.mark(j, 16))
            need(sp, PO, "list")
            lv = LISTS.rearrange("(e h n) c -> e h (n c)", h=2, n=CAP // 2)
            for h in range(2):
                sp.dma_start(lv[:, h, :], listpat).then_inc(ST.sem, 16)
            z = flat(hid)[:, 0:D]
            sp.dma_start(U2[SEQ:SEQ + P, :], z).then_inc(ST.sem, 16)
            sp.dma_start(YACC[SEQ:SEQ + P, :], z).then_inc(ST.sem, 16)
            sp.wait_ge(ST.sem, 64)
            sp.drain()

        @block.scalar
        def _(act):
            do = stepper(act, AC)

            def load(dst, src):
                act.dma_start(dst, src).then_inc(PL.sem, PL.mark("all", 16))
            load(cv[:, :], t["chan"])
            for r in range(6):
                load(brow[r], t["b_mod"][0, r * D:(r + 1) * D].partition_broadcast(P))
            load(wout[:, :, :], t["w_out"].rearrange("(t p) n -> p t n", p=P))
            load(wrt[:, :, :], t["w_router"].rearrange("(p c) n -> p c n", c=DC))
            load(lora[:, :], t["lora"])
            need(act, PO, ("set", "wri"))
            for g, nme in enumerate(("w_rg", "w_ig")):
                for h in range(4):
                    o = 64 * (h % 2)
                    load(wri[o:o + 64, g, h // 2, o:o + 64], t[nme][h])
            load(ln1g[:, :], t["ln1_g"][0, :].partition_broadcast(P))
            load(ln1b[:, :], t["ln1_b"][0, :].partition_broadcast(P))
            load(ebias[:, :], t["e_bias"][0, :].partition_broadcast(P))
            act.wait_ge(XL.sem, 16)
            do(act.activation(small[:, 8:8 + DC], small[:, 0:DC], ACT.Silu))
            need(act, PO, ("set", "ones"))
            for k in range(DC):
                do(act.activation(crep[:, k, :], ones[:, :], ACT.Copy, scale=small[:, 8 + k:9 + k]), ("crep", k))
            act.wait_ge(PL.sem, PL.n)
            o = CV["lru_lambda"][0]
            do(act.activation(small[:, 16:18], cv[:, o:o + 2], ACT.Abs))
            do(act.activation(small[:, 16:18], small[:, 16:18], ACT.Exp, scale=-1.0), "ylam")

        @block.tensor
        def _(pe):
            need(pe, AC, ("crep", DC - 1))
            for j in range(MC):
                c = (WE, WO)[j % 2]
                need(pe, c, j)
                if j >= 4:
                    need(pe, DV, ("mod", j - 4))
                for k in range(DC):
                    mm = pe.matmul(bank[j % 4][:, :], crep[:, k, :], wm[j % 2][:, k, :], start=(k == 0), stop=(k == DC - 1))
                mm.then_inc(PE.sem, PE.mark(("mod", j)))
            need(pe, DV, ("row", 1))
            for r in range(2):
                v = rows[r][0:1, :].rearrange("p (n c) -> p n c", c=DC)
                for k in range(DC):
                    mm = pe.matmul(bank[5][:, r * DC + k:r * DC + k + 1], v[:, :, k], ones[0:1, 0:1], start=True, stop=True)
            mm.then_inc(PE.sem, PE.mark("cols"))

        @block.vector
        def _(dve):
            do = stepper(dve, DV)
            need(dve, PL, "all")
            for j in range(MC):
                r, o = j // 2, (j % 2) * 512
                need(dve, PE, ("mod", j))
                do(dve.tensor_tensor(rows[r][:, o:o + 512], bank[j % 4][:, :], brow[r][:, o:o + 512], ALU.add), ("mod", j))
                if j % 2:
                    if r in (1, 2, 4, 5):
                        do(dve.tensor_scalar(rows[r], rows[r], 1.0, None, ALU.add), ("row", r))
            need(dve, PE, "cols")
            do(dve.tensor_copy(shcol[:, :], bank[5][:, 0:DC]))
            do(dve.tensor_copy(sccol[:, :], bank[5][:, DC:2 * DC]))
            need(dve, AC, "ylam")
            y, z, z2, acc = (small[:, 16 + 2 * i:18 + 2 * i] for i in range(4))
            o = CV["lru_lambda"][0]
            do(dve.tensor_scalar(z, y, 2.0, None, ALU.add))
            do(dve.reciprocal(z, z))
            do(dve.tensor_tensor(z, z, y, ALU.mult))
            do(dve.tensor_tensor(z2, z, z, ALU.mult))
            do(dve.memset(acc, 1.0 / 19))
            for n in range(17, 0, -2):
                do(dve.tensor_tensor(acc, acc, z2, ALU.mult))
                do(dve.tensor_scalar(acc, acc, 1.0 / n, None, ALU.add))
            do(dve.tensor_tensor(acc, acc, z, ALU.mult))
            do(dve.tensor_scalar(z, cv[:, o:o + 2], -1.0, 0.0, ALU.mult, ALU.max))
            do(dve.scalar_tensor_tensor(out=acc, in0=acc, scalar=2.0, in1=z, op0=ALU.mult, op1=ALU.add))
            do(dve.tensor_scalar(chalf[:, :], acc, 4.0, None, ALU.mult))
    nc.all_engine_barrier(sems_to_clear=span)

    PE, AC, DV, PO, XL, WE, WO, PL, R0, R1, SL, ST, SS = stage("mix")
    taken[0] = 0
    ut = cut(DC, TB)
    wb = [cut(DC, GRP * P) for _ in range(2)]
    taken[0] = 0
    gm = cut(8, 4 * P)
    em = cut(8, P)
    xi = cut(8, P)
    xt = cut(8, P)
    pm = cut(8, P)
    rb = cut(8, P)
    tk = cut(2, 3, 256)
    rk = cut(4, P)
    phi = cut(4, 64)
    taken[0] = 0
    ws13 = cut(DC, 512)
    ws2 = cut(2, D)
    xr = [cut(D) for _ in range(2)]
    x1 = cut(D)
    u2 = cut(D)
    u2t = cut(DC, P)
    ysh = flat(tmp[2])
    hs = tmp[3][:, 0, 0:256]
    hst = tmp[3][:, 1, 0:256]
    mask_u = maskf[:, :].bitcast(U32)
    TAIL = list(range(7, NPT))
    EVEN = lambda n: WE if n % 2 == 0 else WO

    with nc.Fori(0, NTB) as it:
      with nc.Block() as block:
        @block.sync
        def _(sp):
            sp.dma_start(ut, t["xt"][:, :, bass.ds(it * TB, TB)]).then_inc(XL.sem, 16)
            for g in range(NGRP):
                if g >= 2:
                    need(sp, PE, ("proj", GRP * (g - 1) - 1))
                sp.dma_start(wb[g % 2], t["w_in"][:, g]).then_inc(EVEN(g).sem, EVEN(g).mark(g, 16))
            need(sp, PE, "chunks")
            need(sp, DV, "chunks")
            need(sp, AC, "chunks")
            sp.dma_start(ws13, t["ws13"].rearrange("(p c) n -> p c n", c=DC)).then_inc(SL.sem, 16)
            sp.dma_start(ws2, t["ws2"].rearrange("(p c) n -> p c n", c=2)).then_inc(SL.sem, 16)

            def load_rows(tt):
                c = (R0, R1)[tt % 2]
                sp.dma_start(xr[tt % 2], t["x"][bass.ds(it * TB + tt * P, P), :]).then_inc(c.sem, c.mark(tt, 16))

            for tt in range(2):
                load_rows(tt)
            for tt in range(NCH):
                need(sp, DV, ("x1", tt))
                sp.dma_start(X1[bass.ds(it * TB + tt * P, P), :], x1).then_inc(ST.sem, ST.mark(("x1", tt), 16))
                if tt + 2 < NCH:
                    load_rows(tt + 2)
                need(sp, DV, ("u2", tt))
                sp.dma_start(U2[bass.ds(it * TB + tt * P, P), :], u2).then_inc(ST.sem, ST.mark(("u2", tt), 16))
                need(sp, AC, ("ysh", tt))
                sp.dma_start(YACC[bass.ds(it * TB + tt * P, P), :], ysh).then_inc(SS.sem, SS.mark(tt, 16))
            sp.wait_ge(ST.sem, ST.n)
            sp.wait_ge(SS.sem, SS.n)
            sp.drain()

        @block.tensor
        def _(pe):
            def mark(mm, key):
                mm.then_inc(PE.sem, PE.mark(key))

            for c in range(DC):
                need(pe, DV, ("ut", c))
            for n in range(NPT):
                g = n // GRP
                if n % GRP == 0:
                    need(pe, EVEN(g), g)
                if n >= 4:
                    need(pe, *((DV, ("evac", n - 4)) if n - 4 in (8, 10, 19, 20) else (AC, ("evac", n - 4))))
                for c in range(DC):
                    mm = pe.matmul(bank[n % 4][:, :], wb[g % 2][:, c, (n % GRP) * P:(n % GRP + 1) * P], ut[:, c, :],
                                   start=(c == 0), stop=(c == DC - 1))
                mark(mm, ("proj", n))
                if n == 8:
                    need(pe, AC, "lt")
                    for ct in range(2):
                        mark(pe.matmul(bank[4 + ct][:, :], lora[0:32, ct * P:(ct + 1) * P], tmp[5][0:32, 0, :],
                                       start=True, stop=True), ("lw", ct))
                        mark(pe.matmul(bank[6 + ct][:, :], lora[32:64, ct * P:(ct + 1) * P], tmp[5][32:64, 0, :],
                                       start=True, stop=True), ("la", ct))
                if n == 12:
                    need(pe, DV, "kksq")
                    for ct in range(2):
                        need(pe, AC, ("sig_w", ct))
                        mark(pe.matmul(bank[4 + ct][:, :], blk1[:, :], tmp[6][:, ct, :], start=True, stop=True), ("ss", ct))
                if n == 15:
                    need(pe, DV, "rkk")
                    for ct in range(2):
                        need(pe, AC, ("sig_a", ct))
                        mark(pe.matmul(bank[6 + ct][:, :], blk1[:, :], tmp[6][:, ct, :], start=True, stop=True), ("bonus", ct))
                    for ct in range(2):
                        need(pe, AC, ("knorm", ct))
                        mark(pe.matmul(bank[4 + ct][:, :], lora[64:128, ct * P:(ct + 1) * P], tmp[5][64:128, 0, :],
                                       start=True, stop=True), ("lg", ct))
            need(pe, DV, ("u", 1))
            need(pe, DV, "bonus")
            need(pe, AC, ("g", 1))
            for ct in range(2):
                mark(pe.matmul(bank[4 + ct][:, :], wri[:, 0, ct, :], tmp[2][:, ct, :], start=True, stop=True), ("gr", ct))
                mark(pe.matmul(bank[6 + ct][:, :], wri[:, 1, ct, :], tmp[2][:, ct, :], start=True, stop=True), ("gi", ct))

            need(pe, AC, ("evac", 18))
            need(pe, DV, ("evac", 20))
            need(pe, DV, "rp")
            need(pe, AC, ("gi", 1))
            for w in range(2):
                if w:
                    need(pe, AC, ("y", 0, 1))
                    need(pe, DV, ("st", 0, 1))
                for cc in range(2):
                    ch = 2 * w + cc
                    cs = slice(ch * P, (ch + 1) * P)
                    for ct in range(2):
                        pe.transpose(bank[2 * cc][:, ct * P:(ct + 1) * P], kr[:, ct, ch, 0, :], ident[:, :])
                        pe.transpose(bank[2 * cc][:, (2 + ct) * P:(3 + ct) * P], pc[:, 4 + ct, 1 + ch * P:1 + (ch + 1) * P], ident[:, :])
                        pe.transpose(bank[2 * cc + 1][:, ct * P:(ct + 1) * P], kh[:, ct, cs], ident[:, :])
                        mm = pe.transpose(bank[2 * cc + 1][:, (2 + ct) * P:(3 + ct) * P], bh[:, ct, cs], ident[:, :])
                    mark(mm, ("tok", w, cc))
                for n in range(8):
                    cc, h = n // 4, n % 4
                    ct, o, ch = h // 2, 64 * (h % 2), 2 * w + cc
                    cs = slice(ch * P, (ch + 1) * P)
                    if n >= 4:
                        need(pe, DV, ("gm", w, n - 4))
                    rhs = kr[o:o + 64, ct, ch, :, :].rearrange("p a b -> p (a b)")
                    pe.matmul(bank[4 + h][:, 0:256], bh[o:o + 64, ct, cs], rhs, start=True, stop=True)
                    mark(pe.matmul(bank[4 + h][:, 256:512], kh[o:o + 64, ct, cs], rhs, start=True, stop=True), ("g4", w, n))
                need(pe, AC, ("tok", w, 1))
                for n in range(8):
                    cc, h = n // 4, n % 4
                    need(pe, DV, ("gm", w, n))
                    mm = pe.matmul(bank[0][:, n * 64:(n + 1) * 64], gm[:, n, 256:384], tk[:, cc, 0, h * 64:(h + 1) * 64], start=True, stop=True)
                mark(mm, ("av", w))
                need(pe, PO, ("em", w, 0))
                for cc in range(2):
                    for h in range(4):
                        n = 4 * cc + h
                        mm = pe.matmul(bank[3 + cc][:, h * P:(h + 1) * P], em[:, n, :], ident[:, :], start=True, stop=True)
                    mark(mm, ("q", w, 0, cc))
                for lv in range(1, len(LEVELS)):
                    need(pe, PO, ("em", w, lv))
                    for cc in range(2):
                        need(pe, DV, ("x", w, lv - 1, cc))
                        for h in range(4):
                            n = 4 * cc + h
                            mm = pe.matmul(bank[1 + cc][:, h * P:(h + 1) * P], em[:, n, :], xi[:, n, :], start=True, stop=True)
                        mark(mm, ("p", w, lv, cc))
                    for cc in range(2):
                        need(pe, AC, ("pm", w, lv, cc))
                        need(pe, DV, ("xt", w, lv - 1, cc))
                        if lv < len(LEVELS) - 1:
                            for h in range(4):
                                n = 4 * cc + h
                                mm = pe.matmul(bank[3 + cc][:, h * P:(h + 1) * P], xt[:, n, :], pm[:, n, :], start=True, stop=True)
                            mark(mm, ("q", w, lv, cc))
                        for h in range(4):
                            n = 4 * cc + h
                            mm = pe.matmul(bank[5 + cc][:, h * P:(h + 1) * P], pm[:, n, :], xt[:, n, :], start=True, stop=True)
                        mark(mm, ("qt", w, lv, cc))
                need(pe, AC, ("av", w))
                for cc in range(2):
                    need(pe, DV, ("xt", w, len(LEVELS) - 1, cc))
                    for h in range(4):
                        n = 4 * cc + h
                        mm = pe.matmul(bank[1 + cc][:, h * P:(h + 1) * P], xt[:, n, :], rb[:, n, :], start=True, stop=True)
                    mark(mm, ("wg", w, cc))
                for cc in range(2):
                    need(pe, AC, ("wg", w, cc))
                    for h in range(4):
                        n, o, ct = 4 * cc + h, 64 * (h % 2), h // 2
                        q = 2 * cc + ct
                        pe.matmul(bank[3][o:o + 64, q * P:(q + 1) * P], pm[:, n, 0:64], gm[:, n, 128:256], start=True, stop=True)
                        mm = pe.matmul(bank[4][o:o + 64, q * 64:(q + 1) * 64], pm[:, n, 0:64], tk[:, cc, 2, h * 64:(h + 1) * 64],
                                       start=True, stop=True)
                mark(mm, ("rk", w))
                need(pe, DV, ("rk", w))
                need(pe, DV, ("phi", w))
                for cc in range(2):
                    need(pe, DV, ("sin", w, cc))
                    for h in range(4):
                        n, o, ct = 4 * cc + h, 64 * (h % 2), h // 2
                        q = 2 * cc + ct
                        vt = tk[:, cc, 0, h * 64:(h + 1) * 64]
                        out = bank[5][o:o + 64, ct * 64:(ct + 1) * 64]
                        pe.matmul(out, tk[:, cc, 1, h * 64:(h + 1) * 64], vt, start=True, stop=False)
                        pe.matmul(out, tk[:, cc, 2, h * 64:(h + 1) * 64], pm[:, n, 64:128], start=False, stop=False)
                        mm = pe.matmul(out, phi[o:o + 64, q, :], s_in[o:o + 64, ct, :], start=False, stop=True)
                    mark(mm, ("st", w, cc))
                    for h in range(4):
                        n, o, ct = 4 * cc + h, 64 * (h % 2), h // 2
                        q = 2 * cc + ct
                        vt = tk[:, cc, 0, h * 64:(h + 1) * 64]
                        out = bank[6 + cc][o:o + 64, ct * P:(ct + 1) * P]
                        pe.matmul(out, vt, gm[:, n, 384:512], start=True, stop=False)
                        pe.matmul(out, pm[:, n, 64:128], gm[:, n, 128:256], start=False, stop=False)
                        mm = pe.matmul(out, s_in[o:o + 64, ct, :], rk[o:o + 64, q, :], start=False, stop=True)
                    mark(mm, ("y", w, cc))
            mark(pe.matmul(bank[0][0:1, 0:1], ones[0:1, 0:1], ones[0:1, 0:1], start=True, stop=True), "chunks")

            need(pe, AC, ("y", 1, 1))
            for ct in range(2):
                mark(pe.matmul(bank[1 + ct][:, :], blk1[:, :], tmp[0][:, ct, :], start=True, stop=True), ("gnm", ct))
            need(pe, DV, "conv_a")
            for ct in range(2):
                mm = pe.matmul(bank[3][:, :], ones[:, :], ya[:, ct, :], start=(ct == 0), stop=(ct == 1))
            mark(mm, "lam")
            need(pe, AC, "gnsq")
            for ct in range(2):
                need(pe, DV, ("gnd", ct))
                mark(pe.matmul(bank[1 + ct][:, :], blk1[:, :], tmp[2][:, ct, :], start=True, stop=True), ("gnv", ct))
            need(pe, AC, "lasq")
            for ct in range(2):
                mm = pe.matmul(bank[3][:, :], ones[:, :], tmp[3][:, ct, :], start=(ct == 0), stop=(ct == 1))
            mark(mm, "lav")

            for tt in range(NCH):
                ts = slice(tt * P, (tt + 1) * P)
                if tt == 0:
                    need(pe, DV, "yc")
                    need(pe, AC, "ya")
                else:
                    need(pe, AC, ("ysh", tt - 1))
                mats = [ya[:, 0, ts], ya[:, 1, ts], yb[:, 0, ts], yb[:, 1, ts],
                        pc[:, 0, 1 + tt * P:1 + (tt + 1) * P], pc[:, 1, 1 + tt * P:1 + (tt + 1) * P], yd[:, 0, ts], yd[:, 1, ts]]
                for n in range(2):
                    for k in range(DC):
                        mm = pe.matmul(bank[n][:, :], mats[k], wout[:, k, n * 512:(n + 1) * 512], start=(k == 0), stop=(k == DC - 1))
                    mark(mm, ("out", tt, n))
                need(pe, DV, ("u2", tt))
                v = u2.rearrange("p (n c) -> p n c", c=DC)
                for k in range(DC):
                    mm = pe.transpose(bank[2 + k // 4][:, (k % 4) * P:(k % 4 + 1) * P], v[:, :, k], ident[:, :])
                    if k % 4 == 3:
                        mark(mm, ("u2t", tt, k // 4))
                need(pe, AC, ("u2t", tt))
                if tt:
                    need(pe, AC, ("score", tt - 1))
                for k in range(DC):
                    mm = pe.matmul(bank[4][:, 0:NE], u2t[:, k, :], wrt[:, k, :], start=(k == 0), stop=(k == DC - 1))
                mark(mm, ("score", tt))
                if tt == 0:
                    pe.wait_ge(SL.sem, 32)
                for k in range(DC):
                    mm = pe.matmul(bank[5][:, :], u2t[:, k, :], ws13[:, k, :], start=(k == 0), stop=(k == DC - 1))
                mark(mm, ("sh", tt))
                need(pe, DV, ("hs", tt))
                pe.matmul(bank[7][:, 0:NE], maskf[:, 0:P], rt[:, 128:128 + NE], start=True, stop=False)
                mark(pe.matmul(bank[7][:, 0:NE], ones[:, :], cum_sel[:, :], start=False, stop=True), ("rank", tt))
                v = hs.rearrange("p (n c) -> p n c", c=2)
                for k in range(2):
                    mm = pe.transpose(bank[6][:, k * P:(k + 1) * P], v[:, :, k], ident[:, :])
                mark(mm, ("hst", tt))
                need(pe, AC, ("hst", tt))
                for n in range(2):
                    for k in range(2):
                        mm = pe.matmul(bank[n][:, :], hst[:, k * P:(k + 1) * P], ws2[:, k, n * 512:(n + 1) * 512],
                                       start=(k == 0), stop=(k == 1))
                mark(mm, ("ysh", tt))

        @block.scalar
        def _(act):
            do = stepper(act, AC)

            def evac(n):
                need(act, PE, ("proj", n))
                src = bank[n % 4][:, :]
                if n < 7:
                    do(act.activation(pc[:, n, 1:1 + TB], src, ACT.Copy), ("evac", n), wait=False)
                elif n in (7, 9):
                    do(act.activation(ya[:, (n - 7) // 2, :], src, ACT.Sigmoid), ("evac", n), wait=False)
                elif n in (11, 12):
                    do(act.activation(xb[:, n - 11, HALO_B:], src, ACT.Copy), ("evac", n), wait=False)
                elif n in (13, 14):
                    do(act.activation(yb[:, n - 13, :], src, ACT.Gelu_apprx_tanh), ("evac", n), wait=False)
                elif n in (15, 16):
                    do(act.activation(yd[:, n - 15, :], src, ACT.Copy), ("evac", n), wait=False)
                elif n in (17, 18):
                    do(act.activation(pd[:, n - 17, HALO_D:], src, ACT.Copy), ("evac", n), wait=False)

            for n in range(7):
                evac(n)
            evac(7)
            need(act, DV, ("xs", 6))
            do(act.activation(tmp[5][32:64, 0, :], pc[32:64, 6, 1:1 + TB], ACT.Copy), wait=False)
            do(act.activation(tmp[5][64:128, 0, :], pc[64:128, 6, 1:1 + TB], ACT.Sigmoid), wait=False)
            do(act.activation(tmp[5][0:32, 0, :], pc[0:32, 6, 1:1 + TB], ACT.Tanh), "lt")
            evac(9)
            need(act, DV, ("xs", 5))
            for ct in range(2):
                need(act, PE, ("lw", ct))
                do(act.activation(tmp[0][:, ct, :], bank[4 + ct][:, :], ACT.Sigmoid, bias=cvc("w0", ct)), ("sig_w", ct), wait=False)
                need(act, PE, ("la", ct))
                do(act.activation(tmp[1][:, ct, :], bank[6 + ct][:, :], ACT.Sigmoid, bias=cvc("a0", ct)), ("sig_a", ct), wait=False)
            evac(11)
            evac(12)
            need(act, DV, "csx")
            v = lambda a: flat(a).rearrange("p (a b) -> p a b", b=P)
            krv = lambda j: kr[:, :, :, j, :].rearrange("p a b c -> p (a b) c")
            do(act.activation(krv(0), v(tmp[0]), ACT.Exp, scale=-EM05), "ex", wait=False)
            do(act.activation(krv(1), v(tmp[3]), ACT.Exp, scale=-EM05), "em", wait=False)
            dv = dsc[:, :, :, :].rearrange("p a b c -> p (a b) c")
            do(act.activation(dv[:, :, 0], v(tmp[2])[:, :, P // 2 - 1], ACT.Exp, scale=-EM05), wait=True)
            do(act.activation(dv[:, :, 1], v(tmp[3])[:, :, P - 1], ACT.Exp, scale=-EM05), "dsc", wait=False)
            do(act.activation(flat(tmp[2]), flat(tmp[3]), ACT.Exp, scale=EM05), "ep", wait=False)
            for ct in range(2):
                need(act, PE, ("ss", ct))
                do(act.activation(tmp[6][:, ct, :], bank[4 + ct][:, :], ACT.Sqrt, bias=epsc[:, 1:2]), ("knorm", ct), wait=False)
            evac(13)
            evac(14)
            evac(15)
            evac(16)
            for ct in range(2):
                need(act, PE, ("lg", ct))
                need(act, DV, "rp")
                do(act.activation(pc[:, ct, 1:1 + TB], bank[4 + ct][:, :], ACT.Copy), ("g", ct), wait=False)
            evac(17)
            evac(18)
            for ct in range(2):
                need(act, PE, ("gr", ct))
                do(act.activation(tmp[3][:, ct, :], bank[4 + ct][:, :], ACT.Sigmoid, bias=cvc("b_rg", ct)), ("gr", ct))
                need(act, PE, ("gi", ct))
                do(act.activation(tmp[4][:, ct, :], bank[6 + ct][:, :], ACT.Sigmoid, bias=cvc("b_ig", ct)), ("gi", ct), wait=False)
            for ct in range(2):
                do(act.activation(tmp[3][:, ct, :], tmp[3][:, ct, :], ACT.Tanh, scale=chalf[:, ct:ct + 1]), ("t", ct))
            do(act.activation(flat(tmp[5]), flat(tmp[3]), ACT.Sqrt), "sqt", wait=False)

            for w in range(2):
                for cc in range(2):
                    need(act, PE, ("tok", w, cc))
                    do(act.activation(rb[:, 4 * cc:4 * cc + 4, 0:64], bank[2 * cc][:, 0:256].rearrange("p (h k) -> p h k", k=64),
                                      ACT.Copy), wait=False)
                    do(act.activation(tk[:, cc, 0, :], bank[2 * cc][:, 256:512], ACT.Copy), wait=False)
                    do(act.activation(tk[:, cc, 1:3, :].rearrange("p a b -> p (a b)"), bank[2 * cc + 1][:, :], ACT.Copy),
                       ("tok", w, cc), wait=False)
                need(act, PE, ("av", w))
                do(act.activation(rb[:, :, 64:128], bank[0][:, :].rearrange("p (n k) -> p n k", k=64), ACT.Copy), ("av", w), wait=False)
                for lv in range(1, len(LEVELS)):
                    for cc in range(2):
                        need(act, PE, ("p", w, lv, cc))
                        do(act.activation(pm[:, 4 * cc:4 * cc + 4, :].rearrange("p a b -> p (a b)"), bank[1 + cc][:, :], ACT.Copy),
                           ("pm", w, lv, cc), wait=False)
                for cc in range(2):
                    need(act, PE, ("wg", w, cc))
                    do(act.activation(pm[:, 4 * cc:4 * cc + 4, :].rearrange("p a b -> p (a b)"), bank[1 + cc][:, :], ACT.Copy,
                                      scale=-1.0), ("wg", w, cc), wait=False)
                for cc in range(2):
                    ch = 2 * w + cc
                    need(act, PE, ("y", w, cc))
                    do(act.activation(tmp[0][:, :, ch * P:(ch + 1) * P], bank[6 + cc][:, 0:256].rearrange("p (c n) -> p c n", n=P),
                                      ACT.Copy), ("y", w, cc), wait=False)
            do(act.activation(small[:, 32:33], epsc[:, 3:4], ACT.Copy), "chunks", wait=False)
            for ct in range(2):
                need(act, DV, ("gnd", ct))
                do(act.activation(tmp[2][:, ct, :], tmp[0][:, ct, :], ACT.Square), "gnsq", wait=False)
            for ct in range(2):
                need(act, DV, ("lad", ct))
                do(act.activation(tmp[3][:, ct, :], ya[:, ct, :], ACT.Square), "lasq", wait=False)
            for ct in range(2):
                need(act, PE, ("gnv", ct))
                do(act.activation(tmp[2][:, ct, :], bank[1 + ct][:, :], ACT.Sqrt, bias=epsc[:, 2:3], scale=1.0 / 64), ("gns", ct), wait=False)
            need(act, PE, "lav")
            do(act.activation(tmp[4][:, 0, :], bank[3][:, :], ACT.Sqrt, bias=epsc[:, 0:1], scale=1.0 / 256), "las", wait=False)
            for ct in range(2):
                need(act, DV, ("laz", ct))
                do(act.activation(ya[:, ct, :], ya[:, ct, :], ACT.Silu, bias=cvc("ln_a_b", ct), scale=cvc("ln_a_g", ct)), "ya", wait=False)
            for tt in range(NCH):
                need(act, DV, ("var", tt))
                do(act.activation(small[:, 44:45], small[:, 41:42], ACT.Sqrt, bias=epsc[:, 0:1]), ("std", tt), wait=False)
                for k in range(2):
                    need(act, PE, ("u2t", tt, k))
                    do(act.activation(u2t[:, 4 * k:4 * k + 4, :].rearrange("p a b -> p (a b)"), bank[2 + k][:, :], ACT.Copy),
                       ("u2t", tt), wait=False)
                need(act, PE, ("score", tt))
                if tt:
                    need(act, DV, ("routed", tt - 1))
                do(act.activation(rt[:, 0:NE], bank[4][:, 0:NE], ACT.Sigmoid), ("score", tt), wait=False)
                need(act, PE, ("sh", tt))
                do(act.activation(hs, bank[5][:, 0:256], ACT.Silu), ("silu", tt), wait=False)
                need(act, PE, ("hst", tt))
                do(act.activation(hst, bank[6][:, 0:256], ACT.Copy), ("hst", tt), wait=False)
                need(act, PE, ("ysh", tt))
                if tt:
                    need(act, SS, tt - 1)
                for n in range(2):
                    do(act.activation(ysh[:, n * 512:(n + 1) * 512], bank[n][:, :], ACT.Copy), ("ysh", tt), wait=False)

        @block.vector
        def _(dve):
            do = stepper(dve, DV)
            v = lambda a: flat(a).rearrange("p (a b) -> p a b", b=P)
            krv = lambda j: kr[:, :, :, j, :].rearrange("p a b c -> p (a b) c")
            dve.wait_ge(XL.sem, 16)
            for c in range(DC):
                do(dve.tensor_scalar(ut[:, c, :], ut[:, c, :], sccol[:, c:c + 1], shcol[:, c:c + 1], ALU.mult, ALU.add), ("ut", c), wait=False)
            for j in (6, 0, 2, 4):
                m = 1 if j == 6 else 2
                need(dve, AC, ("evac", j + m - 1))
                if j == 6:
                    d = tmp[6][:, 0:1, :]
                else:
                    d = tmp[{0: 0, 2: 1, 4: 2}[j]][:, :, :]
                do(dve.tensor_copy(pclast[:, j:j + m], pc[:, j:j + m, TB]), wait=False)
                do(dve.tensor_tensor(d, pc[:, j:j + m, 0:TB], pc[:, j:j + m, 1:1 + TB], ALU.subtract))
                for i in range(m):
                    x = pc[:, j + i, 1:1 + TB]
                    do(dve.scalar_tensor_tensor(out=x, in0=d[:, i, :], scalar=cvc("mu_c", j + i), in1=x, op0=ALU.mult, op1=ALU.add),
                       ("xs", j + i))
            def gate_a(n):
                need(dve, PE, ("proj", n))
                need(dve, AC, ("evac", n - 1))
                do(dve.tensor_tensor(hid[:, (n - 8) // 2, HALO_A:], bank[n % 4][:, :], ya[:, (n - 8) // 2, :], ALU.mult), ("evac", n), wait=False)
            gate_a(8)
            for ct in range(2):
                do(dve.tensor_scalar(tmp[4][:, ct, :], pc[:, 2 + ct, 1:1 + TB], cvc("k_k", ct), None, ALU.mult))
                do(dve.tensor_tensor(tmp[6][:, ct, :], tmp[4][:, ct, :], tmp[4][:, ct, :], ALU.mult), "kksq")
            gate_a(10)
            for ct in range(2):
                need(dve, AC, ("sig_w", ct))
                do(dve.tensor_tensor_scan(tmp[2][:, ct, :], scan_keep[:, :], tmp[0][:, ct, :], 0.0, ALU.mult, ALU.add))
            mid = v(tmp[2])[:, :, P // 2 - 1:P // 2].to_broadcast([P, 2 * NCH, P])
            do(dve.tensor_tensor(v(tmp[3]), v(tmp[2]), mid, ALU.subtract))
            do(dve.tensor_tensor(flat(tmp[0]), flat(tmp[3]), flat(tmp[0]), ALU.subtract), "csx")
            for ct in range(2):
                need(dve, AC, ("knorm", ct))
                do(dve.reciprocal(tmp[6][:, ct, :], tmp[6][:, ct, :]))
            do(dve.tensor_tensor(flat(tmp[4]), flat(tmp[4]), flat(tmp[6]), ALU.mult))
            need(dve, AC, "ex")
            do(dve.tensor_tensor(krv(0), krv(0), v(tmp[4]), ALU.mult), "kp", wait=False)
            need(dve, AC, ("sig_a", 1))
            do(dve.tensor_tensor(flat(tmp[4]), flat(tmp[4]), flat(tmp[1]), ALU.mult))
            need(dve, AC, "ep")
            do(dve.tensor_tensor(flat(bh), flat(tmp[4]), flat(tmp[2]), ALU.mult), wait=False)
            for ct in range(2):
                k, r = pc[:, 2 + ct, 1:1 + TB], pc[:, ct, 1:1 + TB]
                do(dve.tensor_scalar(tmp[6][:, ct, :], tmp[1][:, ct, :], -1.0, cvc("k_a", ct), ALU.add, ALU.mult))
                do(dve.scalar_tensor_tensor(out=k, in0=tmp[6][:, ct, :], scalar=1.0, in1=k, op0=ALU.add, op1=ALU.mult))
                do(dve.tensor_tensor(kh[:, ct, :], k, tmp[2][:, ct, :], ALU.mult), wait=False)
                do(dve.scalar_tensor_tensor(out=tmp[6][:, ct, :], in0=r, scalar=cvc("r_k", ct), in1=k, op0=ALU.mult, op1=ALU.mult), "rkk")
            need(dve, AC, "em")
            do(dve.tensor_tensor(kr[:, :, :, 1, :].rearrange("p a b c -> p a b c"), kr[:, :, :, 1, :],
                                 pc[:, 0:2, 1:1 + TB].rearrange("p a (b c) -> p a b c", c=P), ALU.mult), "rp")
            for ct in range(2):
                need(dve, PE, ("bonus", ct))
                do(dve.tensor_tensor(tmp[1][:, ct, :], bank[6 + ct][:, :], pc[:, 4 + ct, 1:1 + TB], ALU.mult), "bonus", wait=False)
            for ct in range(2):
                need(dve, AC, ("evac", 11 + ct))
                u = tmp[2][:, ct, :]
                do(dve.tensor_scalar(u, xb[:, ct, HALO_B:], cvc("conv_b", 2 * 3 + ct), cvc("conv_b_bias", ct), ALU.mult, ALU.add))
                for k in range(3):
                    do(dve.scalar_tensor_tensor(out=u, in0=xb[:, ct, k:k + TB], scalar=cvc("conv_b", 2 * k + ct), in1=u,
                                                op0=ALU.mult, op1=ALU.add), ("u", ct))
            for ct in range(2):
                need(dve, PE, ("proj", 19 + ct))
                need(dve, AC, ("evac", 17 + ct))
                x = pd[:, ct, HALO_D:]
                do(dve.tensor_tensor(x, bank[(19 + ct) % 4][:, :], x, ALU.mult), ("evac", 19 + ct))
            need(dve, AC, ("evac", 16))
            for ct in range(2):
                a = tmp[6][:, ct, :]
                do(dve.tensor_scalar(a, pd[:, ct, HALO_D:], cvc("conv_d", 4 + ct), None, ALU.mult))
                for k in range(2):
                    do(dve.scalar_tensor_tensor(out=a, in0=pd[:, ct, k:k + TB], scalar=cvc("conv_d", 2 * k + ct), in1=a,
                                                op0=ALU.mult, op1=ALU.add))
            do(dve.tensor_tensor(flat(yd), flat(yd), flat(tmp[6]), ALU.mult))
            need(dve, AC, ("t", 1))
            do(dve.tensor_scalar(flat(tmp[6]), flat(tmp[3]), 1.0, None, ALU.add))
            do(dve.reciprocal(flat(tmp[6]), flat(tmp[6])))
            do(dve.tensor_tensor(flat(tmp[4]), flat(tmp[4]), flat(tmp[2]), ALU.mult))
            need(dve, AC, "sqt")
            do(dve.tensor_scalar(flat(tmp[3]), flat(tmp[6]), 2.0, -1.0, ALU.mult, ALU.add), wait=False)
            do(dve.scalar_tensor_tensor(out=flat(tmp[5]), in0=flat(tmp[5]), scalar=2.0, in1=flat(tmp[6]), op0=ALU.mult, op1=ALU.mult))
            do(dve.tensor_tensor(flat(tmp[4]), flat(tmp[4]), flat(tmp[5]), ALU.mult))
            for ct in range(2):
                do(dve.tensor_tensor_scan(tmp[2][:, ct, :], tmp[3][:, ct, :], tmp[4][:, ct, :], hlast[:, ct:ct + 1], ALU.mult, ALU.add))
                do(dve.tensor_copy(hlast[:, ct:ct + 1], tmp[2][:, ct, TB - 1:TB]), wait=False)
            need(dve, AC, ("evac", 14))
            do(dve.tensor_tensor(flat(yb), flat(yb), flat(tmp[2]), ALU.mult), "yb")

            taps = [(ct, k) for k in range(30, -1, -1) for ct in range(2)]

            tapped = []

            def tap(count):
                for _ in range(count):
                    if not taps:
                        return
                    ct, k = taps.pop(0)
                    if k < 30:
                        dve.wait_ge(DV.sem, tapped.pop(0))
                    a, x = ya[:, ct, :], hid[:, ct, k:k + TB]
                    if k == 30:
                        do(dve.tensor_scalar(a, x, cvc("conv_a", 2 * k + ct), cvc("conv_a_bias", ct), ALU.mult, ALU.add), wait=False)
                    else:
                        do(dve.scalar_tensor_tensor(out=a, in0=x, scalar=cvc("conv_a", 2 * k + ct), in1=a, op0=ALU.mult, op1=ALU.add),
                           "conv_a", wait=False)
                    tapped.append(DV.n)

            need(dve, PO, "zero")
            need(dve, DV, ("evac", 10))
            for w in range(2):
                for n in range(8):
                    need(dve, PE, ("g4", w, n))
                    do(dve.copy_predicated(gm[:, n, :], mask_u, bank[4 + n % 4][:, :]), ("gm", w, n), wait=False)
                need(dve, PO, ("em", w, 0))
                idb = ident[:, :].unsqueeze(1).to_broadcast([P, 4, P])
                for cc in range(2):
                    q = slice(4 * cc, 4 * cc + 4)
                    do(dve.tensor_tensor(xt[:, q, :], idb, em[:, q, :], ALU.subtract), ("xt", w, 0, cc), wait=False)
                    need(dve, PE, ("q", w, 0, cc))
                    do(dve.tensor_tensor(xi[:, q, :], idb, bank[3 + cc][:, :].rearrange("p (a b) -> p a b", b=P), ALU.subtract),
                       ("x", w, 0, cc), wait=False)
                for lv in range(1, len(LEVELS)):
                    tap(4)
                    for cc in range(2):
                        q = slice(4 * cc, 4 * cc + 4)
                        if lv < len(LEVELS) - 1:
                            need(dve, PE, ("q", w, lv, cc))
                            need(dve, DV, ("x", w, lv - 1, cc))
                            x = xi[:, q, :].rearrange("p a b -> p (a b)")
                            do(dve.tensor_tensor(x, x, bank[3 + cc][:, :], ALU.subtract), ("x", w, lv, cc), wait=False)
                        need(dve, PE, ("qt", w, lv, cc))
                        need(dve, DV, ("xt", w, lv - 1, cc))
                        x = xt[:, q, :].rearrange("p a b -> p (a b)")
                        do(dve.tensor_tensor(x, x, bank[5 + cc][:, :], ALU.subtract), ("xt", w, lv, cc), wait=False)
                tap(6)
                need(dve, PE, ("rk", w))
                for cc in range(2):
                    ch = 2 * w + cc
                    do(dve.tensor_tensor(rk[:, 2 * cc:2 * cc + 2, :], bank[3][:, cc * 256:(cc + 1) * 256].rearrange("p (a b) -> p a b", b=P),
                                         kr[:, :, ch, 1, :], ALU.add), ("rk", w), wait=False)
                e2 = eye2[:, :].unsqueeze(1).to_broadcast([P, 4, 64])
                do(dve.tensor_tensor(phi, bank[4][:, 0:256].rearrange("p (a b) -> p a b", b=64), e2, ALU.add), ("phi", w), wait=False)
                need(dve, AC, "dsc")
                for cc in range(2):
                    ch = 2 * w + cc
                    if cc or w:
                        last = (w, cc - 1) if cc else (0, 1)
                        need(dve, PE, ("y", *last))
                        need(dve, DV, ("st", *last))
                    for ct in range(2):
                        do(dve.tensor_scalar(s_in[:, ct, :], state[:, ct, :], dsc[:, ct, ch, 0:1], None, ALU.mult), ("sin", w, cc), wait=False)
                    need(dve, PE, ("st", w, cc))
                    for ct in range(2):
                        do(dve.tensor_scalar(state[:, ct, :], bank[5][:, ct * 64:(ct + 1) * 64], dsc[:, ct, ch, 1:2], None, ALU.mult),
                           ("st", w, cc), wait=False)
            do(dve.memset(small[:, 34:35], 0.0), "chunks", wait=False)
            tap(62)

            for ct in range(2):
                need(dve, PE, ("gnm", ct))
                x = tmp[0][:, ct, :]
                do(dve.scalar_tensor_tensor(out=x, in0=bank[1 + ct][:, :], scalar=-1.0 / 64, in1=x, op0=ALU.mult, op1=ALU.add), ("gnd", ct))
            need(dve, PE, "lam")
            for ct in range(2):
                x = ya[:, ct, :]
                do(dve.scalar_tensor_tensor(out=x, in0=bank[3][:, :], scalar=-1.0 / 256, in1=x, op0=ALU.mult, op1=ALU.add), ("lad", ct))
            for ct in range(2):
                need(dve, AC, ("gns", ct))
                x, s = tmp[0][:, ct, :], tmp[2][:, ct, :]
                do(dve.reciprocal(s, s))
                do(dve.tensor_tensor(x, x, s, ALU.mult))
                do(dve.tensor_scalar(x, x, cvc("gn_g", ct), cvc("gn_b", ct), ALU.mult, ALU.add))
                do(dve.tensor_tensor(x, x, tmp[1][:, ct, :], ALU.add))
                g = pc[:, ct, 1:1 + TB]
                do(dve.tensor_tensor(g, g, x, ALU.mult), "yc")
            need(dve, AC, "las")
            do(dve.reciprocal(tmp[4][:, 0, :], tmp[4][:, 0, :]))
            for ct in range(2):
                do(dve.tensor_tensor(ya[:, ct, :], ya[:, ct, :], tmp[4][:, 0, :], ALU.mult), ("laz", ct), wait=False)

            for tt in range(NCH):
                st = small[:, 46:58]
                mv = small[:, 40:42]
                need(dve, R0 if tt % 2 == 0 else R1, tt)
                if tt:
                    need(dve, ST, ("u2", tt - 1))
                for n in range(2):
                    need(dve, PE, ("out", tt, n))
                    ns = slice(n * 512, (n + 1) * 512)
                    do(dve.tensor_tensor(x1[:, ns], bank[n][:, :], g1p1[:, ns], ALU.mult), ("outev", tt), wait=(n == 1))
                do(dve.scalar_tensor_tensor(out=x1, in0=xr[tt % 2], scalar=ALPHA, in1=x1, op0=ALU.mult, op1=ALU.add), ("res", tt))
                for n in range(2):
                    do(dve.bn_stats(st[:, 6 * n:6 * n + 6], x1[:, n * 512:(n + 1) * 512]), wait=(n == 1))
                do(dve.bn_aggr(mv, st), ("var", tt))
                need(dve, AC, ("std", tt))
                do(dve.reciprocal(small[:, 44:45], small[:, 44:45]))
                do(dve.tensor_scalar(x1, x1, mv[:, 0:1], small[:, 44:45], ALU.subtract, ALU.mult))
                do(dve.tensor_tensor(x1, x1, ln1g[:, :], ALU.mult))
                do(dve.tensor_tensor(x1, x1, ln1b[:, :], ALU.add), ("x1", tt))
                if tt:
                    need(dve, ST, ("u2", tt - 1))
                do(dve.tensor_tensor(u2, x1, sc2p1[:, :], ALU.mult))
                do(dve.tensor_tensor(u2, u2, sh2r[:, :], ALU.add), ("u2", tt))
                need(dve, AC, ("score", tt))
                sc, bi = rt[:, 0:64], rt[:, 64:128]
                sel, g8 = rt[:, 128:192], rt[:, 192:256]
                gs, top, rep, keep = rt[:, 256:268], rt[:, 268:276], rt[:, 276:288], rt[:, 288:296]
                msk, slots, best, w8 = rt[:, 296:360], rt[:, 360:424], rt[:, 424:432], rt[:, 432:440]
                ssum, slf, idf = rt[:, 440:441], rt[:, 448:456], rt[:, 456:464]
                g3 = lambda a: a.rearrange("p (g e) -> p g e", e=8)
                do(dve.tensor_tensor(bi, sc, ebias[:, :], ALU.add))
                for g in range(NGR):
                    do(dve.max(g8[:, 8 * g:8 * g + 8], bi[:, 8 * g:8 * g + 8]), wait=(g == NGR - 1))
                do(dve.memset(gs[:, 8:12], 1.0e30), wait=False)
                do(dve.tensor_tensor(gs[:, 0:8], g3(g8)[:, :, 0], g3(g8)[:, :, 1], ALU.add))
                do(dve.max(top, gs))
                do(dve.match_replace(rep, top, gs, NEG))
                do(dve.tensor_scalar(keep, rep[:, 0:8], NEG, None, ALU.is_equal))
                kb = keep.unsqueeze(2).to_broadcast([P, NGR, 8])
                do(dve.tensor_tensor(g3(msk), g3(bi), kb, ALU.mult))
                do(dve.tensor_scalar(keep, keep, -NEG, NEG, ALU.mult, ALU.add))
                do(dve.tensor_tensor(g3(msk), g3(msk), kb, ALU.add))
                do(dve.max(best, msk))
                do(dve.match_replace(sel, best, msk, -NEG))
                do(dve.tensor_scalar(sel, sel, -NEG, None, ALU.is_equal), ("sel", tt))
                do(dve.max_index(idx8[:, :], best, msk))
                do(dve.tensor_copy(idf, idx8[:, :]))
                oh = flat(tmp[4])[:, 0:512].rearrange("p (j e) -> p j e", e=NE)
                pr = flat(tmp[4])[:, 512:1024].rearrange("p (j e) -> p j e", e=NE)
                do(dve.tensor_tensor(oh, iota_e[:, :, :], idf.unsqueeze(2).to_broadcast([P, TOPK, NE]), ALU.is_equal))
                do(dve.tensor_tensor(pr, oh, sc.unsqueeze(1).to_broadcast([P, TOPK, NE]), ALU.mult))
                do(dve.tensor_reduce(w8, pr, AX_X, ALU.add))
                do(dve.tensor_reduce(ssum, w8, AX_X, ALU.add))
                do(dve.reciprocal(ssum, ssum))
                need(dve, AC, ("silu", tt))
                do(dve.tensor_tensor(hs, hs, bank[5][:, 256:512], ALU.mult), ("hs", tt), wait=False)
                need(dve, PE, ("rank", tt))
                do(dve.scalar_tensor_tensor(out=slots, in0=iota_e[:, 0, :], scalar=float(CAP), in1=bank[7][:, 0:NE],
                                            op0=ALU.mult, op1=ALU.add))
                do(dve.tensor_tensor(cum_sel[:, :], cum_sel[:, :], sel, ALU.add), ("cum", tt), wait=False)
                do(dve.tensor_tensor(pr, oh, slots.unsqueeze(1).to_broadcast([P, TOPK, NE]), ALU.mult))
                do(dve.tensor_reduce(slf, pr, AX_X, ALU.add))
                if tt:
                    dve.wait_ge(lists_written, it * (16 * TOPK * NCH) + 16 * TOPK * tt)
                do(dve.tensor_copy(slot[:, :], slf), wait=False)
                do(dve.tensor_scalar(tw[:, :, 1].bitcast(F32), w8, ssum, ROUTED_SCALE, ALU.mult, ALU.mult), ("routed", tt), wait=False)

        @block.gpsimd
        def _(pool):
            do = stepper(pool, PO)
            need(pool, PE, ("proj", NPT - 1))
            need(pool, DV, ("ut", DC - 1))
            do(pool.memset(gm, 0.0), "zero")
            for w in range(2):
                need(pool, DV, ("gm", w, 7))
                for lv in range(len(LEVELS)):
                    if lv:
                        need(pool, PE, ("p", w, lv - 1, 1) if lv > 1 else ("q", w, 0, 1))
                    if lv == 1:
                        need(pool, DV, ("xt", w, 0, 1))
                    do(pool.tensor_tensor(em, gm[:, :, 0:P], levm[:, lv, :].unsqueeze(1).to_broadcast([P, 8, P]), ALU.mult),
                       ("em", w, lv), wait=False)
            need(pool, DV, "conv_a")
            do(pool.tensor_copy(hid[:, :, 0:HALO_A], hid[:, :, TB:TB + HALO_A]), wait=False)
            do(pool.tensor_copy(xb[:, :, 0:HALO_B], xb[:, :, TB:TB + HALO_B]), wait=False)
            do(pool.tensor_copy(pd[:, :, 0:HALO_D], pd[:, :, TB:TB + HALO_D]), wait=False)
            do(pool.tensor_copy(pc[:, :, 0], pclast[:, :]), wait=False)
            for tt in range(NCH):
                need(pool, DV, ("routed", tt))
                do(pool.tensor_copy(tw[:, :, 0], tok_id[:, bass.ds(it * NCH + tt, 1)].to_broadcast([P, TOPK])))
                for j in range(TOPK):
                    pool.indirect_dma_start(out=LISTS[:, :], out_offset=bass.IndirectOffsetOnAxis(ap=slot[:, j:j + 1], axis=0),
                                            in_=tw[:, j, :], in_offset=None).then_inc(lists_written, 16)
            pool.wait_ge(lists_written, it * (16 * TOPK * NCH) + 16 * TOPK * NCH)
            do(pool.tensor_tensor(pclast[:, 0:1], epsc[:, 0:1], epsc[:, 1:2], ALU.add))
      nc.all_engine_barrier(sems_to_clear=span)
    mix.close()

    PE, AC, DV, PO, XL, WE, WO, PL, R0, R1, SL, ST, SS = stage("tables")
    moe = ExitStack()
    ROW, PAR, NEED, SPLIT, EVEN_W, ODD_W, PAR1 = range(7)
    NTAB = NBLK + 2
    tab = sb(moe, "tab", [1, NTAB, 8], I32)
    turn_e = sb(moe, "turn_e", [1, NE], I32)
    used = sb(moe, "used", [1, 4], I32)
    LST = NBLK + 4
    lists = sb(moe, "lists", [P, LST, 2], I32)
    small_t = ExitStack()
    nb = sb(small_t, "nb", [NE, 8])
    nbi = sb(small_t, "nbi", [NE, 2], I32)
    iob = sb(small_t, "iob", [NE, NTAB])
    ioe = sb(small_t, "ioe", [NE, 1])
    cmp = sb(small_t, "cmp", [NE, NTAB])
    hot = sb(small_t, "hot", [NE, NE])
    r = [sb(small_t, f"row{i}", [1, NTAB]) for i in range(6)]
    ri = [sb(small_t, f"rowi{i}", [1, NTAB], I32) for i in range(2)]
    urow = sb(small_t, "urow", [1, 2])
    with nc.Block() as block:
        @block.tensor
        def _(pe):
            def mark(mm, key):
                mm.then_inc(PE.sem, PE.mark(key))
            mark(pe.matmul(bank[0][0:NE, 0:1], cum_sel[:, :], ones[:, 0:1], start=True, stop=True), "count")
            need(pe, DV, "has")
            mark(pe.matmul(bank[1][0:NE, 0:1], maskf[0:NE, P:P + NE], nb[:, 0:1], start=True, stop=True), "end")
            mark(pe.matmul(bank[2][0:NE, 0:1], maskf[0:NE, 0:NE], nb[:, 2:3], start=True, stop=True), "turn")
            mark(pe.matmul(bank[5][0:1, 0:1], nb[:, 0:1], ones[0:NE, 0:1], start=True, stop=True), "blocks")
            mark(pe.matmul(bank[5][0:1, 8:9], nb[:, 2:3], ones[0:NE, 0:1], start=True, stop=True), "turns")
            need(pe, DV, "cmp")
            mark(pe.matmul(bank[3][0:1, 0:NTAB], ones[0:NE, 0:1], cmp[:, :], start=True, stop=True), "e")
            mark(pe.matmul(bank[4][0:1, 0:NTAB], nb[:, 0:1], cmp[:, :], start=True, stop=True), "s")
            mark(pe.matmul(bank[6][0:1, 0:NTAB], nb[:, 2:3], cmp[:, :], start=True, stop=True), "o")
            need(pe, DV, "hot")
            mark(pe.matmul(bank[7][0:1, 0:NE], ioe[:, :], hot[:, :], start=True, stop=True), "turn_e")

        @block.gpsimd
        def _(pool):
            do = stepper(pool, PO)
            do(pool.iota(iob[:, :], pattern=[[1, NTAB]], base=0, channel_multiplier=0, allow_small_or_imprecise_dtypes=True))
            do(pool.iota(ioe[:, :], pattern=[[1, 1]], base=0, channel_multiplier=1, allow_small_or_imprecise_dtypes=True), "iota")
            do(pool.memset(lists[:, NBLK:LST, :], 0))

        @block.vector
        def _(dve):
            do = stepper(dve, DV)
            need(dve, PE, "count")
            do(dve.tensor_scalar(nbi[:, 0:1], bank[0][0:NE, 0:1], float(P - 1), None, ALU.add))
            do(dve.tensor_scalar(nbi[:, 1:2], nbi[:, 0:1], 7, None, ALU.arith_shift_right))
            do(dve.tensor_copy(nb[:, 0:1], nbi[:, 1:2]))
            do(dve.tensor_scalar(nb[:, 2:3], nb[:, 0:1], 1.0, None, ALU.min), "has")
            need(dve, PE, "end")
            do(dve.tensor_copy(nb[:, 1:2], bank[1][0:NE, 0:1]))
            need(dve, PO, "iota")
            do(dve.tensor_scalar(cmp[:, :], iob[:, :], nb[:, 1:2], None, ALU.is_ge), "cmp")
            need(dve, PE, "turn")
            do(dve.tensor_copy(nb[:, 3:4], bank[2][0:NE, 0:1]))
            do(dve.tensor_scalar(hot[:, :], iob[:, 0:NE], nb[:, 3:4], nb[:, 2:3], ALU.is_equal, ALU.mult), "hot")
            need(dve, PE, "turns")
            do(dve.tensor_copy(urow[:, 0:1], bank[5][0:1, 0:1]))
            do(dve.tensor_copy(urow[:, 1:2], bank[5][0:1, 8:9]))
            do(dve.tensor_copy(used[:, 0:2], urow[:, :]))
            need(dve, PE, "o")
            do(dve.tensor_tensor(r[0][:, :], iob[0:1, :], bank[4][0:1, 0:NTAB], ALU.subtract))
            do(dve.tensor_scalar(r[1][:, :], bank[3][0:1, 0:NTAB], float(CAP // P), None, ALU.mult))
            do(dve.tensor_tensor(r[1][:, :], r[0][:, :], r[1][:, :], ALU.add))
            do(dve.tensor_scalar(tab[:, :, ROW], r[1][:, :], float(P), float(NE * CAP), ALU.mult, ALU.min))
            do(dve.tensor_scalar(urow[:, 1:2], urow[:, 1:2], -1.0, None, ALU.add))
            do(dve.tensor_scalar(r[2][:, :], bank[6][0:1, 0:NTAB], urow[:, 1:2], None, ALU.min))
            do(dve.tensor_copy(ri[0][:, :], r[2][:, :]))
            do(dve.tensor_scalar(ri[1][:, :], ri[0][:, :], 1, None, ALU.bitwise_and))
            do(dve.tensor_copy(r[3][:, :], ri[1][:, :]))
            do(dve.tensor_copy(tab[:, :, PAR], r[3][:, :]))
            do(dve.tensor_scalar(tab[:, :, NEED], r[2][:, :], 1.0, None, ALU.add))
            do(dve.tensor_scalar(tab[:, :, PAR1], r[3][:, :], -1.0, 1.0, ALU.mult, ALU.add))
            do(dve.tensor_scalar(r[4][:, :], r[0][:, :], 0.0, None, ALU.is_equal))
            do(dve.tensor_scalar(r[5][:, :], r[2][:, :], urow[:, 1:2], None, ALU.is_lt))
            do(dve.tensor_tensor(tab[:, :, SPLIT], r[4][:, :], r[5][:, :], ALU.mult))
            do(dve.tensor_tensor(r[4][:, :], r[2][:, :], r[3][:, :], ALU.add))
            do(dve.tensor_scalar(tab[:, :, EVEN_W], r[4][:, :], 8.0, 16.0, ALU.mult, ALU.add))
            do(dve.tensor_tensor(r[4][:, :], r[2][:, :], r[3][:, :], ALU.subtract))
            do(dve.tensor_scalar(tab[:, :, ODD_W], r[4][:, :], 8.0, 16.0, ALU.mult, ALU.add))
            need(dve, PE, "turn_e")
            do(dve.tensor_copy(turn_e[:, :], bank[7][0:1, 0:NE]))
    nc.all_engine_barrier(sems_to_clear=span)
    small_t.close()

    raw13 = sb(moe, "raw13", [P, 2, DC * 512])
    raw2 = sb(moe, "raw2", [P, 2, 2 * D])
    w13p = [sb(moe, f"w13_{n}", [P, 2 * DC, 512], F32R) for n in ("high", "low")]
    w2p = [sb(moe, f"w2_{n}", [P, 2 * 2, D], F32R) for n in ("high", "low")]
    xg = [sb(moe, f"xg{i}", [P, D]) for i in range(2)]
    xt_p = [[sb(moe, f"xt{i}_{n}", [P, DC, P], F32R) for n in ("high", "low")] for i in range(2)]
    hm = [sb(moe, f"hm{i}", [P, DE]) for i in range(2)]
    ht_p = [[sb(moe, f"ht{i}_{n}", [P, DE], F32R) for n in ("high", "low")] for i in range(2)]
    yo = [sb(moe, f"yo{i}", [P, D]) for i in range(2)]
    gidx = [sb(moe, f"gidx{i}", [P, 2], I32) for i in range(2)]
    sidx = [sb(moe, f"sidx{i}", [P, 2], I32) for i in range(2)]
    zero = sb(moe, "zero", [P, 1], I32)
    PARTS = ((0, 0), (0, 1), (1, 0))

    def sem(name):
        return top.enter_context(nc.semaphore(name))

    w13_loaded = [sem("w13_even_loaded"), sem("w13_odd_loaded")]
    w2_loaded = [sem("w2_even_loaded"), sem("w2_odd_loaded")]
    loads_done = sem("loads_done")
    w13_high = sem("w13_high")
    w13_low = sem("w13_low")
    w2_high = sem("w2_high")
    w2_low = sem("w2_low")
    lists_loaded = [sem("lists_even_loaded"), sem("lists_odd_loaded")]
    idx_ready = sem("idx_ready")
    x_gathered = [sem("x0_gathered"), sem("x1_gathered")]
    x_turned = sem("x_turned")
    xt_high = sem("xt_high")
    xt_low = sem("xt_low")
    h_ready = sem("h_ready")
    gate_ready = sem("gate_ready")
    hm_ready = sem("hm_ready")
    h_turned = sem("h_turned")
    ht_high = sem("ht_high")
    ht_low = sem("ht_low")
    y_ready = sem("y_ready")
    yo_d = sem("yo_d")
    yo_a = sem("yo_a")
    y_added = [sem("y0_added"), sem("y1_added")]
    yo_free = sem("yo_free")
    NPAIR = NBLK // 2
    PIECES = 4

    HB = (4, 7)
    with nc.Block() as block:
        @block.sync
        def _(sp):
            w13v = t["w13"].rearrange("e (p c) n -> e p (c n)", c=DC)
            w2v = t["w2"].rearrange("e (p c) n -> e p (c n)", c=2)
            turns = sp.value_load(used[0:1, 1:2], min_val=1, max_val=NE)

            def load13(o, q):
                e = sp.value_load(turn_e[0:1, bass.ds(o, 1)], min_val=0, max_val=NE - 1)
                sp.dma_start(raw13[:, q, :], w13v[bass.ds(e, 1)].rearrange("e p n -> p (e n)")).then_inc(w13_loaded[q], 16)
                return e

            def load2(e, q):
                sp.dma_start(raw2[:, q, :], w2v[bass.ds(e, 1)].rearrange("e p n -> p (e n)")).then_inc(w2_loaded[q], 16)

            for q in range(2):
                load2(load13(q, q), q)
            with sp.Fori(0, NBLK // 2) as i:
                row = sp.value_load(tab[0:1, bass.ds(i * 2 + 1, 1), ROW], min_val=0, max_val=(NE + 1) * CAP - P)
                sp.dma_start(lists[:, bass.ds(i * 2 + 1, 1), :].rearrange("p a c -> p (a c)"),
                             LISTS[bass.ds(row, P), :]).then_inc(lists_loaded[1], 16)
            with sp.Fori(1, NE // 2) as i:
                with sp.If(turns > i * 2):
                    for q in range(2):
                        sp.wait_ge(w13_low, i * 2 + q - 1)
                        e = load13(i * 2 + q, q)
                        sp.wait_ge(w2_low, i * 2 + q - 1)
                        load2(e, q)
            pairs = sp.snap((turns + 1) // 2)
            for q in range(2):
                sp.wait_ge(w13_loaded[q], pairs * 16)
                sp.wait_ge(w2_loaded[q], pairs * 16)
            sp.sem_inc(loads_done, 1)
            sp.wait_ge(loads_done, 1)
            sp.drain()

        @block.tensor
        def _(pe):
            pe.sem_inc(y_ready, 1)
            pe.sem_inc(h_ready, 1)
            n = pe.value_load(used[0:1, 0:1], min_val=1, max_val=NBLK)

            def turn_x(q):
                v = xg[q][:, :].rearrange("p (n c) -> p n c", c=DC)
                for k in range(DC):
                    mm = pe.transpose(bank[k // 4][:, (k % 4) * P:(k % 4 + 1) * P], v[:, :, k], ident[:, :])
                    if k % 4 == 3:
                        mm.then_inc(x_turned, 1)

            def turn_h(b, q):
                pe.wait_ge(hm_ready, b + 1)
                v = hm[q][:, :].rearrange("p (n c) -> p n c", c=2)
                for k in range(2):
                    mm = pe.transpose(bank[HB[q]][:, k * P:(k + 1) * P], v[:, :, k], ident[:, :])
                mm.then_inc(h_turned, 1)

            def up(b, q):
                par = pe.value_load(tab[0:1, bass.ds(b, 1), PAR], min_val=0, max_val=1)
                turn = pe.value_load(tab[0:1, bass.ds(b, 1), NEED], min_val=1, max_val=NE)
                pe.wait_ge(w13_low, turn)
                pe.wait_ge(xt_low, b * 2 + 2)
                for k in range(DC):
                    for m, (xp, wp) in enumerate(PARTS):
                        mm = pe.matmul(bank[2 + q][:, :], xt_p[q][xp][:, k, :],
                                       w13p[wp][:, bass.ds(par * DC + k, 1), :].rearrange("p a n -> p (a n)"),
                                       start=(k == 0 and m == 0), stop=(k == DC - 1 and m == 2))
                mm.then_inc(h_ready, 1)

            def down(b, q):
                par = pe.value_load(tab[0:1, bass.ds(b, 1), PAR], min_val=0, max_val=1)
                turn = pe.value_load(tab[0:1, bass.ds(b, 1), NEED], min_val=1, max_val=NE)
                pe.wait_ge(w2_low, turn)
                pe.wait_ge(ht_low, b + 1)
                pe.wait_ge(yo_d, b + 1)
                pe.wait_ge(yo_a, b + 1)
                for h in range(2):
                    for k in range(2):
                        for m, (xp, wp) in enumerate(PARTS):
                            mm = pe.matmul(bank[5 + h][:, :], ht_p[q][xp][:, k * P:(k + 1) * P],
                                           w2p[wp][:, bass.ds(par * 2 + k, 1), h * 512:(h + 1) * 512].rearrange("p a n -> p (a n)"),
                                           start=(k == 0 and m == 0), stop=(k == 1 and m == 2))
                mm.then_inc(y_ready, 1)

            for b in range(2):
                pe.wait_ge(x_gathered[b], 16)
                if b:
                    pe.wait_ge(xt_low, 2)
                turn_x(b)
            up(0, 0)
            pe.wait_ge(x_gathered[0], 32)
            pe.wait_ge(xt_low, 4)
            turn_x(0)
            turn_h(0, 0)
            with pe.Fori(0, NPAIR) as i:
                with pe.If(n > i * 2):
                    for s in range(2):
                        b, q = i * 2 + s + 1, 1 - s
                        up(b, q)
                        pe.wait_ge(x_gathered[q], i * 16 + 32 + 16 * s)
                        pe.wait_ge(xt_low, b * 2 + 4)
                        turn_x(q)
                        down(b - 1, s)
                        turn_h(b, q)

        @block.scalar
        def _(act):
            act.sem_inc(yo_a, 1)
            n = act.value_load(used[0:1, 0:1], min_val=1, max_val=NBLK)
            with act.Fori(0, NBLK // 2) as i:
                row = act.value_load(tab[0:1, bass.ds(i * 2, 1), ROW], min_val=0, max_val=(NE + 1) * CAP - P)
                act.dma_start(lists[:, bass.ds(i * 2, 1), :].rearrange("p a c -> p (a c)"),
                              LISTS[bass.ds(row, P), :]).then_inc(lists_loaded[0], 16)

            def split13(par):
                w = DC // PIECES
                for k in range(PIECES):
                    act.activation(w13p[0][:, bass.ds(par * DC + k * w, w), :].rearrange("p a n -> p (a n)"),
                                   raw13[:, bass.ds(par, 1), k * w * 512:(k + 1) * w * 512].rearrange("p a n -> p (a n)"),
                                   ACT.Copy).then_inc(w13_high, 1)

            def split2(par):
                act.activation(w2p[0][:, bass.ds(par * 2, 2), :].rearrange("p a n -> p (a n)"),
                               raw2[:, bass.ds(par, 1), :].rearrange("p a n -> p (a n)"), ACT.Copy).then_inc(w2_high, 1)

            def copy_x(b, q):
                for h in range(2):
                    act.wait_ge(x_turned, b * 2 + 1 + h)
                    act.activation(xt_p[q][0][:, 4 * h:4 * h + 4, :].rearrange("p a b -> p (a b)"), bank[h][:, :],
                                   ACT.Copy).then_inc(xt_high, 1)

            def next_turn(b, loaded, done, split):
                flag = act.value_load(tab[0:1, bass.ds(b, 1), SPLIT], min_val=0, max_val=1)
                with act.If(flag > 0):
                    even = act.value_load(tab[0:1, bass.ds(b, 1), EVEN_W], min_val=16, max_val=16 * NE)
                    odd = act.value_load(tab[0:1, bass.ds(b, 1), ODD_W], min_val=16, max_val=16 * NE)
                    par = act.value_load(tab[0:1, bass.ds(b, 1), PAR1], min_val=0, max_val=1)
                    act.wait_ge(loaded[0], even)
                    act.wait_ge(loaded[1], odd)
                    act.wait_ge(done, b + 1)
                    split(par)

            def gate(b, q):
                act.wait_ge(h_ready, b + 2)
                act.activation(hm[q][:, :], bank[2 + q][:, 0:DE], ACT.Silu).then_inc(gate_ready, 1)

            act.wait_ge(w13_loaded[0], 16)
            split13(0)
            act.wait_ge(w2_loaded[0], 16)
            split2(0)
            for b in range(2):
                copy_x(b, b)
            for c in lists_loaded:
                act.wait_ge(c, 8 * NBLK)
            act.wait_ge(w13_loaded[1], 16)
            act.wait_ge(h_ready, 1)
            next_turn(0, w13_loaded, h_ready, split13)
            gate(0, 0)
            copy_x(2, 0)
            with act.Fori(0, NPAIR) as i:
                with act.If(n > i * 2):
                    for s in range(2):
                        b, q = i * 2 + s + 1, 1 - s
                        act.wait_ge(h_turned, b)
                        act.activation(ht_p[s][0][:, :], bank[HB[s]][:, 0:DE], ACT.Copy).then_inc(ht_high, 1)
                        next_turn(b - 1, w2_loaded, y_ready, split2)
                        next_turn(b, w13_loaded, h_ready, split13)
                        gate(b, q)
                        copy_x(b + 2, q)
                        act.wait_ge(y_ready, b + 1)
                        act.wait_ge(yo_free, b)
                        act.activation(yo[s][:, 512:1024], bank[6][:, :], ACT.Copy,
                                       scale=lists[:, bass.ds(b - 1, 1), 1].bitcast(F32)).then_inc(yo_a, 1)

        @block.vector
        def _(dve):
            dve.sem_inc(yo_d, 1)
            n = dve.value_load(used[0:1, 0:1], min_val=1, max_val=NBLK)

            def split13(par, turn):
                w = DC // PIECES
                for k in range(PIECES):
                    dve.wait_ge(w13_high, turn * PIECES + k + 1)
                    at = bass.ds(par * DC + k * w, w)
                    mm = dve.tensor_tensor(w13p[1][:, at, :].rearrange("p a n -> p (a n)"),
                                           raw13[:, bass.ds(par, 1), k * w * 512:(k + 1) * w * 512].rearrange("p a n -> p (a n)"),
                                           w13p[0][:, at, :].rearrange("p a n -> p (a n)").bitcast(F32), ALU.subtract)
                mm.then_inc(w13_low, 1)

            def split2(par, turn):
                dve.wait_ge(w2_high, turn + 1)
                dve.tensor_tensor(w2p[1][:, bass.ds(par * 2, 2), :].rearrange("p a n -> p (a n)"),
                                  raw2[:, bass.ds(par, 1), :].rearrange("p a n -> p (a n)"),
                                  w2p[0][:, bass.ds(par * 2, 2), :].rearrange("p a n -> p (a n)").bitcast(F32),
                                  ALU.subtract).then_inc(w2_low, 1)

            def copy_x(b, q):
                for h in range(2):
                    dve.wait_ge(xt_high, b * 2 + 1 + h)
                    dve.tensor_tensor(xt_p[q][1][:, 4 * h:4 * h + 4, :].rearrange("p a b -> p (a b)"), bank[h][:, :],
                                      xt_p[q][0][:, 4 * h:4 * h + 4, :].rearrange("p a b -> p (a b)").bitcast(F32),
                                      ALU.subtract).then_inc(xt_low, 1)

            def next_turn(b, split):
                flag = dve.value_load(tab[0:1, bass.ds(b, 1), SPLIT], min_val=0, max_val=1)
                with dve.If(flag > 0):
                    turn = dve.value_load(tab[0:1, bass.ds(b, 1), NEED], min_val=1, max_val=NE)
                    par = dve.value_load(tab[0:1, bass.ds(b, 1), PAR1], min_val=0, max_val=1)
                    split(par, turn)

            def times_up(b, q):
                dve.wait_ge(gate_ready, b + 1)
                dve.tensor_tensor(hm[q][:, :], hm[q][:, :], bank[2 + q][:, DE:2 * DE], ALU.mult).then_inc(hm_ready, 1)

            split13(0, 0)
            split2(0, 0)
            for b in range(2):
                copy_x(b, b)
            for c in lists_loaded:
                dve.wait_ge(c, 8 * NBLK)
            next_turn(0, split13)
            times_up(0, 0)
            copy_x(2, 0)
            with dve.Fori(0, NPAIR) as i:
                with dve.If(n > i * 2):
                    for s in range(2):
                        b, q = i * 2 + s + 1, 1 - s
                        dve.wait_ge(ht_high, b)
                        dve.tensor_tensor(ht_p[s][1][:, :], bank[HB[s]][:, 0:DE], ht_p[s][0][:, :].bitcast(F32),
                                          ALU.subtract).then_inc(ht_low, 1)
                        next_turn(b - 1, split2)
                        next_turn(b, split13)
                        times_up(b, q)
                        copy_x(b + 2, q)
                        dve.wait_ge(y_ready, b + 1)
                        dve.wait_ge(yo_free, b)
                        dve.tensor_scalar(yo[s][:, 0:512], bank[5][:, :], lists[:, bass.ds(b - 1, 1), 1].bitcast(F32), None,
                                          ALU.mult).then_inc(yo_d, 1)

        @block.gpsimd
        def _(pool):
            pool.sem_inc(yo_free, 2)
            n = pool.value_load(used[0:1, 0:1], min_val=1, max_val=NBLK)
            pool.memset(zero[:, :], 0).then_inc(idx_ready, 1)
            pool.wait_ge(idx_ready, 1)
            for c in lists_loaded:
                pool.wait_ge(c, 8 * NBLK)
            pool.sem_clear(idx_ready)

            def places(dst, b):
                pool.tensor_copy(dst[:, 1:2], lists[:, bass.ds(b, 1), 0]).then_inc(idx_ready, 1)
                pool.wait_ge(idx_ready, 1)

            def gather(q):
                pool.tensor_tensor(gidx[q][:, 0:1], gidx[q][:, 1:2], zero[:, :], ALU.add).then_inc(idx_ready, 1)
                pool.wait_ge(idx_ready, 2)
                pool.indirect_dma_start(out=xg[q][:, :], out_offset=None, in_=U2[:, :],
                                        in_offset=bass.IndirectOffsetOnAxis(ap=gidx[q][:, 0:1], axis=0)).then_inc(x_gathered[q], 16)
                pool.sem_clear(idx_ready)

            for b in range(4):
                places(gidx[b % 2], b)
                if b >= 2:
                    pool.wait_ge(x_turned, 2 * b - 2)
                    pool.wait_ge(x_gathered[b % 2], 16)
                gather(b % 2)
            with pool.Fori(0, NPAIR) as i:
                with pool.If(n > i * 2):
                    for q in range(2):
                        b = i * 2 + q
                        places(gidx[q], b + 4)
                        pool.wait_ge(x_turned, b * 2 + 6)
                        pool.wait_ge(x_gathered[q], i * 16 + 32)
                        gather(q)
                        places(sidx[q], b)
                        pool.wait_ge(yo_d, b + 2)
                        pool.wait_ge(yo_a, b + 2)
                        pool.tensor_tensor(sidx[q][:, 0:1], sidx[q][:, 1:2], zero[:, :], ALU.add).then_inc(idx_ready, 1)
                        pool.wait_ge(idx_ready, 2)
                        pool.indirect_dma_start(out=YACC[:, :], out_offset=bass.IndirectOffsetOnAxis(ap=sidx[q][:, 0:1], axis=0),
                                                in_=yo[q][:, :], in_offset=None, compute_op=ALU.add).then_inc(y_added[q], 16)
                        pool.sem_clear(idx_ready)
                        pool.wait_ge(y_added[q], (i + 1) * 16)
                        pool.sem_inc(yo_free, 1)
            pairs = pool.snap((n + 1) // 2)
            for q in range(2):
                pool.wait_ge(y_added[q], pairs * 16)
                pool.wait_ge(x_gathered[q], pairs * 16 + 32)
            pool.tensor_tensor(zero[:, :], gidx[0][:, 1:2], gidx[0][:, 1:2], ALU.subtract).then_inc(idx_ready, 1)
            pool.wait_ge(idx_ready, 1)
    moe.close()

    fin = ExitStack()
    NT = SEQ // P
    NB4 = 4
    xa = sb(fin, "xa", [P, NB4, D])
    yy = sb(fin, "yy", [P, NB4, D])
    ln2g = sb(fin, "ln2g", [P, D])
    ln2b = sb(fin, "ln2b", [P, D])
    fs = sb(fin, "fs", [P, NB4, 18])
    ln_loaded = sem("ln_loaded")
    rows_in = [sem(f"rows_in{q}") for q in range(NB4)]
    tile_stats = sem("tile_stats")
    tile_std = sem("tile_std")
    tile_shift = sem("tile_shift")
    tile_normed = sem("tile_normed")
    tile_scaled = sem("tile_scaled")
    tile_done = sem("tile_done")
    rows_out = [sem(f"rows_out{q}") for q in range(NB4)]
    own = sem("final_steps")
    with nc.Block() as block:
        def tile_rows(b):
            return bass.ds(b * P, P)

        @block.sync
        def _(sp):
            sp.dma_start(ln2g[:, :], t["ln2_g"][0, :].partition_broadcast(P)).then_inc(ln_loaded, 16)
            sp.dma_start(ln2b[:, :], t["ln2_b"][0, :].partition_broadcast(P)).then_inc(ln_loaded, 16)

            def load(b, q):
                sp.dma_start(xa[:, q, :], X1[tile_rows(b), :]).then_inc(rows_in[q], 16)
                sp.dma_start(yy[:, q, :], YACC[tile_rows(b), :]).then_inc(rows_in[q], 16)

            for q in range(NB4):
                load(q, q)
            with sp.Fori(1, NT // NB4) as i:
                for q in range(NB4):
                    sp.wait_ge(rows_out[q], i * 16)
                    load(i * NB4 + q, q)
            sp.drain()

        @block.scalar
        def _(act):
            with act.Fori(0, NT // NB4) as i:
                for q in range(NB4):
                    b = i * NB4 + q
                    act.wait_ge(tile_stats, b + 1)
                    act.activation(fs[:, q, 14:15], fs[:, q, 13:14], ACT.Sqrt, bias=epsc[:, 0:1]).then_inc(tile_std, 1)
                    act.wait_ge(tile_shift, b + 1)
                    act.activation(xa[:, q, :], xa[:, q, :], ACT.Identity, bias=fs[:, q, 16:17],
                                   scale=fs[:, q, 15:16]).then_inc(tile_normed, 1)
                    act.wait_ge(tile_done, b + 1)
                    act.dma_start(t["out"][tile_rows(b), :], xa[:, q, :]).then_inc(rows_out[q], 16)
            for q in range(NB4):
                act.wait_ge(rows_out[q], 16 * NT // NB4)
            act.drain()

        @block.gpsimd
        def _(pool):
            pool.wait_ge(ln_loaded, 32)
            with pool.Fori(0, NT // NB4) as i:
                for q in range(NB4):
                    pool.wait_ge(tile_normed, i * NB4 + q + 1)
                    pool.tensor_tensor(yy[:, q, :], xa[:, q, :], ln2g[:, :], ALU.mult).then_inc(tile_scaled, 1)

        @block.vector
        def _(dve):
            dve.wait_ge(ln_loaded, 32)
            with dve.Fori(0, NT // NB4) as i:
                for q in range(NB4):
                    b = i * NB4 + q
                    x, y = xa[:, q, :], yy[:, q, :]
                    st, mv, sd, rs, nm = fs[:, q, 0:12], fs[:, q, 12:14], fs[:, q, 14:15], fs[:, q, 15:16], fs[:, q, 16:17]
                    n = [0]

                    def do(ins, wait=True):
                        ins.then_inc(own, 1)
                        n[0] += 1
                        if wait:
                            dve.wait_ge(own, n[0])
                    dve.wait_ge(rows_in[q], i * 32 + 32)
                    do(dve.tensor_tensor(y, y, g2p1[:, :], ALU.mult))
                    do(dve.scalar_tensor_tensor(out=x, in0=x, scalar=ALPHA, in1=y, op0=ALU.mult, op1=ALU.add))
                    do(dve.bn_stats(st[:, 0:6], x[:, 0:512]), wait=False)
                    do(dve.bn_stats(st[:, 6:12], x[:, 512:1024]))
                    dve.bn_aggr(mv, st).then_inc(tile_stats, 1)
                    dve.wait_ge(tile_std, b + 1)
                    do(dve.reciprocal(rs, sd))
                    dve.scalar_tensor_tensor(out=nm, in0=mv[:, 0:1], scalar=-1.0, in1=rs, op0=ALU.mult, op1=ALU.mult)\
                        .then_inc(tile_shift, 1)
                    dve.wait_ge(tile_scaled, b + 1)
                    dve.tensor_tensor(x, y, ln2b[:, :], ALU.add).then_inc(tile_done, 1)
                    dve.sem_clear(own)
    fin.close()
    top.close()


_CHANNEL = [n for n in CV]
_TILES = [8, 9, 10, 11, 12, 13, 14, 2, 0, 3, 1, 4, 5, 6, 7, 15, 16, 17, 18, 19, 20]


def kernel(**inputs):
    import numpy as _np
    import concourse.bacc as _bacc
    from concourse import mybir as _mybir
    from concourse.bass_utils import run_bass_kernel_spmd as _run

    x = {k: _np.asarray(v) for k, v in inputs.items()}
    arrays = {
        "x": x["x"][0],
        "xt": x["x"][0].T.reshape(P, DC, SEQ),
        "c": x["c"],
        "w_in": x["w_in"][0].reshape(P, DC, NPT, P)[:, :, _TILES].reshape(P, DC, NGRP, GRP * P).transpose(0, 2, 1, 3),
        "chan": _np.concatenate([x[n][0].reshape(-1, P) for n in _CHANNEL]).T,
        "lora": _np.concatenate([x[n][0] for n in ("w_w2", "w_a2", "w_g2")]),
    }
    for n in ("w_mod", "w_out", "w_rg", "w_ig", "w_router", "w13", "w2", "ws13", "ws2"):
        arrays[n] = x[n][0]
    for n in ("b_mod", "e_bias", "ln1_g", "ln1_b", "ln2_g", "ln2_b"):
        arrays[n] = x[n]
    arrays = {f"in_{k}": _np.ascontiguousarray(v) for k, v in arrays.items()}
    for Count.final in (False, True):
        nc = _bacc.Bacc("TRN2", target_bir_lowering=False, num_devices=1)
        t = {k[3:]: nc.dram_tensor(k, a.shape, _mybir.dt.from_np(a.dtype), kind="ExternalInput").ap() for k, a in arrays.items()}
        t["out"] = nc.dram_tensor("out_rows", (SEQ, D), F32, kind="ExternalOutput").ap()
        build(nc, t)
    r = _run(nc, [arrays], core_ids=[0])
    return r.results[0]["out_rows"].reshape(x["x"].shape)
```

```python
from contextlib import ExitStack

import concourse.bass as bass
from concourse import mybir

P = 128
D = 1024
DC = D // P
SEQ = 2048
TB = 512
NTB = SEQ // TB
NCH = TB // P
NPROJ = 2688
NPT = NPROJ // P
GRP = 3
NGRP = NPT // GRP
HALO_A, HALO_B, HALO_D = 30, 3, 2
NE = 64
TOPK = 8
NGR = 8
DE = 256
NBLK = 192
CAP = SEQ
LEVELS = [1, 2, 4, 8, 16, 32, 64]
ALPHA = 2.0 ** 0.25
LN_EPS = 1e-5
GN_EPS = 64e-5
ROUTED_SCALE = 2.5
EM05 = 0.6065306597126334
NEG = -1.0e30

F32 = mybir.dt.float32
F32R = mybir.dt.float32r
I32 = mybir.dt.int32
U32 = mybir.dt.uint32
ACT = mybir.ActivationFunctionType
ALU = mybir.AluOpType
AX_X = mybir.AxisListType.X

CV = {}
for _n, _w in (("conv_a", 62), ("conv_a_bias", 2), ("ln_a_g", 2), ("ln_a_b", 2), ("conv_b", 8),
               ("conv_b_bias", 2), ("b_rg", 2), ("b_ig", 2), ("lru_lambda", 2), ("mu_c", 7), ("w0", 2),
               ("a0", 2), ("k_k", 2), ("k_a", 2), ("r_k", 2), ("gn_g", 2), ("gn_b", 2), ("conv_d", 6)):
    CV[_n] = sum(w for _, w in CV.values()), _w
NCV = sum(w for _, w in CV.values())


class Count:

    seen = {}

    def __init__(self, sem, part):
        self.sem, self.n, self.part = sem, 0, (part, sem.name)

    def mark(self, key, by=1):
        self.n += by
        Count.seen[self.part, key] = self.n
        return by

    def at(self, key):
        if Count.final:
            return Count.seen[self.part, key]
        return 1

    final = False


def build(nc, t):
    top = ExitStack()

    def dram(name, shape, dt=F32):
        return nc.dram_tensor(name, shape, dt, kind="Internal").ap()

    U2 = dram("u2_rows", (SEQ + P, D))
    X1 = dram("x1_rows", (SEQ, D))
    YACC = dram("y_acc", (SEQ + P, D))
    LISTS = dram("expert_lists", ((NE + 1) * CAP, 2), I32)

    names = ["pe_steps", "act_steps", "dve_steps", "pool_steps", "x_loaded", "w_even_loaded", "w_odd_loaded",
             "params_loaded", "rows0_loaded", "rows1_loaded", "shared_w_loaded", "u2_stored", "shared_stored",
             "x1_even_stored", "x1_odd_stored"]
    handles = [top.enter_context(nc.semaphore(n)) for n in names]
    span = range(min(h.num for h in handles), max(h.num for h in handles) + 1)
    assert len(span) == len(handles)
    lists_written = top.enter_context(nc.semaphore("lists_written"))
    wout_loaded = top.enter_context(nc.semaphore("wout_loaded"))

    def stage(tag):
        return [Count(h, tag) for h in handles]

    def need(eng, c, key):
        eng.wait_ge(c.sem, c.at(key))

    def stepper(eng, c):
        def do(ins, key=None, wait=True):
            ins.then_inc(c.sem, c.mark(key if key is not None else ("step", c.n)))
            if wait:
                eng.wait_ge(c.sem, c.n)
        return do

    def sb(stack, name, shape, dt=F32):
        return stack.enter_context(nc.sbuf_tensor(name, shape, dt))

    bank = [top.enter_context(nc.psum_tensor(f"bank{i}", [P, 512], F32)) for i in range(8)]

    ident = sb(top, "ident", [P, P])
    ones = sb(top, "ones", [P, P])
    maskf = sb(top, "maskf", [P, 512])
    cum_sel = sb(top, "cum_sel", [P, NE])
    g2p1 = sb(top, "g2p1", [P, D])
    epsc = sb(top, "epsc", [P, 4])

    tw = sb(top, "tw", [P, TOPK, 2], I32)
    slot = sb(top, "slot", [P, TOPK], I32)

    mix = ExitStack()

    def mb(name, shape, dt=F32):
        return sb(mix, name, shape, dt)

    levm = mb("levm", [P, len(LEVELS), P])
    blk1 = mb("blk1", [P, P])
    scan_keep = mb("scan_keep", [P, TB])
    iota_e = mb("iota_e", [P, TOPK, NE])
    tok_id = mb("tok_id", [P, SEQ // P], I32)
    eye2 = mb("eye2", [P, 64])
    cv = mb("cv", [P, NCV])
    chalf = mb("chalf", [P, 2])
    ebias = mb("ebias", [P, NE])
    shcol = mb("shcol", [P, DC])
    sccol = mb("sccol", [P, DC])
    wout = mb("wout", [P, DC, D])
    wrt = mb("wrt", [P, DC, NE])
    lora = mb("lora", [P, 256])
    wri = mb("wri", [P, 2, 2, P])
    g1p1 = mb("g1p1", [P, D])
    sc2p1 = mb("sc2p1", [P, D])
    sh2r = mb("sh2r", [P, D])
    ln1g = mb("ln1g", [P, D])
    ln1b = mb("ln1b", [P, D])
    hid = mb("hid", [P, 2, HALO_A + TB])
    ya = mb("ya", [P, 2, TB])
    xb = mb("xb", [P, 2, HALO_B + TB])
    yb = mb("yb", [P, 2, TB])
    hlast = mb("hlast", [P, 2])
    pd = mb("pd", [P, 2, HALO_D + TB])
    yd = mb("yd", [P, 2, TB])
    pc = mb("pc", [P, 7, 1 + TB])
    pclast = mb("pclast", [P, 7])
    tmp = [mb(f"tmp{i}", [P, 2, TB]) for i in range(7)]
    factors = mb("factors", [P, 8 * TB])
    kr = factors[:, 0:4 * TB].rearrange("p (t c j n) -> p t c j n", t=2, c=NCH, j=2)
    bh = factors[:, 4 * TB:6 * TB].rearrange("p (t n) -> p t n", t=2)
    kh = factors[:, 6 * TB:8 * TB].rearrange("p (t n) -> p t n", t=2)
    state = mb("state", [P, 2, 64])
    s_in = mb("s_in", [P, 2, 64])
    dsc = mb("dsc", [P, 2, NCH, 2])
    small = mb("small", [P, 64])
    rt = mb("rt", [P, 512])
    idx8 = mb("idx8", [P, TOPK], U32)
    ARENA = 45 * 256
    arena = mb("arena", [P, ARENA])
    taken = [0]

    def cut(*dims):
        n = 1
        for d in dims:
            n *= d
        a = arena[:, taken[0]:taken[0] + n]
        taken[0] += n
        assert taken[0] <= ARENA, taken
        if len(dims) == 2:
            return a.rearrange("p (a b) -> p a b", a=dims[0])
        if len(dims) == 3:
            return a.rearrange("p (a b c) -> p a b c", a=dims[0], b=dims[1])
        return a

    def cvc(name, i=0):
        o, w = CV[name]
        assert i < w
        return cv[:, o + i:o + i + 1]

    def flat(a):
        return a[:, :, :].rearrange("p a b -> p (a b)")

    PE, AC, DV, PO, XL, WE, WO, PL, R0, R1, SL, ST, SS, X0, X1S = stage("setup")
    MC = 6 * D // 512
    taken[0] = 0
    wm = [cut(DC, 512) for _ in range(2)]
    crep = cut(DC, P)
    taken[0] = 0
    ut = cut(DC, TB)
    wb = [cut(DC, GRP * P) for _ in range(2)]
    rows = [flat(kh), flat(bh), g1p1[:, :], sh2r[:, :], sc2p1[:, :], g2p1[:, :]]
    brow = [flat(x) for x in (*tmp[0:5], yd)]
    listpat = kr[0:NE + 1, :, :, :, :].rearrange("p a b c d -> p (a b c d)").bitcast(I32)
    with nc.Block() as block:
        @block.gpsimd
        def _(pool):
            do = stepper(pool, PO)
            for a, v in ((ones, 1.0), (ident, 0.0), (maskf, 1.0), (levm, 0.0), (blk1, 0.0), (scan_keep, 1.0), (wri, 0.0),
                         (hid, 0.0), (xb, 0.0), (pd, 0.0), (pc, 0.0), (hlast, 0.0), (state, 0.0), (cum_sel, 0.0), (eye2, 0.0)):
                do(pool.memset(a[tuple([slice(None)] * len(a.shape))], v), ("set", a.name), wait=False)
            for j, v in enumerate((LN_EPS, 1e-12, GN_EPS, 1.0)):
                do(pool.memset(epsc[:, j:j + 1], v), ("eps", j))
            do(pool.affine_select(out=ident[:, :], in_=ident[:, :], compare_op=ALU.not_equal, fill=1.0, base=0,
                                  pattern=[[-1, P]], channel_multiplier=1))
            for j in range(4):
                m = maskf[:, j * P:(j + 1) * P]
                do(pool.affine_select(out=m, in_=m, compare_op=ALU.is_ge if j % 2 else ALU.is_gt, fill=0.0, base=0,
                                      pattern=[[1, P]], channel_multiplier=-1))
            for j, m in enumerate(LEVELS):
                nb = P // (2 * m)
                v = levm[:, j, :].rearrange("p (n h m) -> p n h m", h=2, m=m)[:, :, 1, :]
                do(pool.memset(v, 1.0))
                do(pool.affine_select(out=v, in_=v, compare_op=ALU.is_ge, fill=0.0, base=0,
                                      pattern=[[-2 * m, nb], [0, m]], channel_multiplier=1))
                do(pool.affine_select(out=v, in_=v, compare_op=ALU.is_ge, fill=0.0, base=m - 1,
                                      pattern=[[2 * m, nb], [0, m]], channel_multiplier=-1))
            for h in range(2):
                do(pool.memset(blk1[64 * h:64 * h + 64, 64 * h:64 * h + 64], 1.0))
                e = eye2[64 * h:64 * h + 64, :]
                do(pool.affine_select(out=e, in_=e, compare_op=ALU.not_equal, fill=1.0, base=0,
                                      pattern=[[-1, 64]], channel_multiplier=1))
            do(pool.memset(scan_keep[:, :].rearrange("p (c n) -> p c n", n=P)[:, :, 0:1], 0.0))
            do(pool.iota(iota_e[:, :, :], pattern=[[0, TOPK], [1, NE]], base=0, channel_multiplier=0,
                         allow_small_or_imprecise_dtypes=True))
            do(pool.iota(tok_id[:, :], pattern=[[P, SEQ // P]], base=0, channel_multiplier=1))
            do(pool.memset(tw[:, :, :], 0))
            do(pool.iota(slot[:, :], pattern=[[P, TOPK]], base=NE * CAP + P, channel_multiplier=1))
            lp = listpat.rearrange("p (b n c) -> p b n c", n=P, c=2)
            do(pool.memset(lp[:, :, :, 1], 0))
            do(pool.iota(lp[:, :, :, 0], pattern=[[0, CAP // P // 2], [1, P]], base=SEQ, channel_multiplier=0), "list")

        @block.sync
        def _(sp):
            sp.dma_start(small[:, 0:DC], t["c"].rearrange("a (p c) -> p (a c)", c=DC)).then_inc(XL.sem, 16)
            w = t["w_mod"].rearrange("(p c) n -> p c n", c=DC)
            for j in range(MC):
                if j >= 2:
                    need(sp, PE, ("mod", j - 2))
                c = (WE, WO)[j % 2]
                sp.dma_start(wm[j % 2], w[:, :, j * 512:(j + 1) * 512]).then_inc(c.sem, c.mark(j, 16))
                if j == MC // 2:
                    need(sp, PO, "list")
                    lv = LISTS.rearrange("(e h n) c -> e h (n c)", h=2, n=CAP // 2)
                    for h in range(2):
                        sp.dma_start(lv[:, h, :], listpat).then_inc(ST.sem, 16)
                    z = flat(hid)[:, 0:D]
                    sp.dma_start(U2[SEQ:SEQ + P, :], z).then_inc(ST.sem, 16)
                    sp.dma_start(YACC[SEQ:SEQ + P, :], z).then_inc(ST.sem, 16)
            need(sp, PE, ("mod", MC - 2))
            sp.dma_start(ut, t["xt"][:, :, 0:TB]).then_inc(SL.sem, 16)
            need(sp, PE, ("mod", MC - 1))
            sp.dma_start(wb[0], t["w_in"][:, 0]).then_inc(SL.sem, 16)
            sp.wait_ge(ST.sem, 64)
            sp.wait_ge(SL.sem, 32)
            sp.drain()

        @block.scalar
        def _(act):
            do = stepper(act, AC)

            act.wait_ge(XL.sem, 16)
            do(act.activation(small[:, 8:8 + DC], small[:, 0:DC], ACT.Silu))
            need(act, PO, ("set", "ones"))
            for k in range(DC):
                do(act.activation(crep[:, k, :], ones[:, :], ACT.Copy, scale=small[:, 8 + k:9 + k]), ("crep", k), wait=False)
            for r in range(6):
                act.dma_start(brow[r], t["b_mod"][0, r * D:(r + 1) * D].partition_broadcast(P)).then_inc(R0.sem, 16)
            act.dma_start(cv[:, :], t["chan"]).then_inc(R1.sem, 16)

            act.wait_ge(R1.sem, 16)
            o = CV["lru_lambda"][0]
            do(act.activation(small[:, 16:18], cv[:, o:o + 2], ACT.Abs))
            do(act.activation(small[:, 16:18], small[:, 16:18], ACT.Exp, scale=-1.0), "ylam")
            def load(dst, src):
                act.dma_start(dst, src).then_inc(PL.sem, 16)
                PL.mark("all", 16)
            need(act, PE, ("mod", 3))
            load(wrt[:, :, :], t["w_router"].rearrange("(p c) n -> p c n", c=DC))
            load(lora[:, :], t["lora"])
            need(act, PO, ("set", "wri"))
            for g, nme in enumerate(("w_rg", "w_ig")):
                for h in range(4):
                    o = 64 * (h % 2)
                    load(wri[o:o + 64, g, h // 2, o:o + 64], t[nme][h])
            load(ln1g[:, :], t["ln1_g"][0, :].partition_broadcast(P))
            load(ln1b[:, :], t["ln1_b"][0, :].partition_broadcast(P))
            load(ebias[:, :], t["e_bias"][0, :].partition_broadcast(P))
            need(act, PE, ("mod", MC - 2))
            act.dma_start(wout[:, :, :], t["w_out"].rearrange("(t p) n -> p t n", p=P)).then_inc(wout_loaded, 16)
            act.wait_ge(PL.sem, PL.n)
            act.drain()

        @block.tensor
        def _(pe):
            need(pe, AC, ("crep", DC - 1))
            for j in range(MC):
                c = (WE, WO)[j % 2]
                need(pe, c, j)
                if j >= 4:
                    need(pe, DV, ("mod", j - 4))
                for k in range(DC):
                    mm = pe.matmul(bank[j % 4][:, :], crep[:, k, :], wm[j % 2][:, k, :], start=(k == 0), stop=(k == DC - 1))
                mm.then_inc(PE.sem, PE.mark(("mod", j)))
                if j == 6:
                    need(pe, DV, ("row", 1))
                    for r in range(2):
                        v = rows[r][0:1, :].rearrange("p (n c) -> p n c", c=DC)
                        for k in range(DC):
                            mm = pe.matmul(bank[5][:, r * DC + k:r * DC + k + 1], v[:, :, k], ones[0:1, 0:1], start=True, stop=True)
                    mm.then_inc(PE.sem, PE.mark("cols"))

        @block.vector
        def _(dve):
            do = stepper(dve, DV)
            need(dve, AC, "ylam")
            y, z, z2, acc = (small[:, 16 + 2 * i:18 + 2 * i] for i in range(4))
            o = CV["lru_lambda"][0]
            do(dve.tensor_scalar(z, y, 2.0, None, ALU.add))
            do(dve.reciprocal(z, z))
            do(dve.tensor_tensor(z, z, y, ALU.mult))
            do(dve.tensor_tensor(z2, z, z, ALU.mult))
            do(dve.memset(acc, 1.0 / 19))
            for n in range(17, 0, -2):
                do(dve.tensor_tensor(acc, acc, z2, ALU.mult))
                do(dve.tensor_scalar(acc, acc, 1.0 / n, None, ALU.add))
            do(dve.tensor_tensor(acc, acc, z, ALU.mult))
            do(dve.tensor_scalar(z, cv[:, o:o + 2], -1.0, 0.0, ALU.mult, ALU.max))
            do(dve.scalar_tensor_tensor(out=acc, in0=acc, scalar=2.0, in1=z, op0=ALU.mult, op1=ALU.add))
            do(dve.tensor_scalar(chalf[:, :], acc, 4.0, None, ALU.mult))
            dve.wait_ge(R0.sem, 6 * 16)
            for j in range(MC):
                r, o = j // 2, (j % 2) * 512
                need(dve, PE, ("mod", j))
                do(dve.tensor_tensor(rows[r][:, o:o + 512], bank[j % 4][:, :], brow[r][:, o:o + 512], ALU.add), ("mod", j))
                if j % 2:
                    if r in (1, 2, 4, 5):
                        do(dve.tensor_scalar(rows[r], rows[r], 1.0, None, ALU.add), ("row", r))
            need(dve, PE, "cols")
            do(dve.tensor_copy(shcol[:, :], bank[5][:, 0:DC]))
            do(dve.tensor_copy(sccol[:, :], bank[5][:, DC:2 * DC]))
    nc.all_engine_barrier(sems_to_clear=span)

    PE, AC, DV, PO, XL, WE, WO, PL, R0, R1, SL, ST, SS, X0, X1S = stage("mix")
    taken[0] = 0
    gm = cut(8, 4 * P)
    em = cut(8, P)
    xi = cut(8, P)
    xt = cut(8, P)
    pm = cut(8, P)
    rb = cut(8, P)
    tk = cut(2, 3, 256)
    rk = cut(4, P)
    phi = cut(4, 64)
    ws13 = factors[:, :].rearrange("p (c n) -> p c n", c=DC)
    taken[0] = DC * TB + DC * GRP * P
    ws2 = cut(2, D)
    xr = [cut(D) for _ in range(2)]
    x1 = [flat(tmp[0]), flat(tmp[1])]
    u2 = flat(tmp[5])
    u2t = flat(tmp[6]).rearrange("p (c n) -> p c n", c=DC)
    ysh = flat(tmp[2])
    hs = tmp[3][:, 0, 0:256]
    hst = tmp[3][:, 1, 0:256]
    mask_u = maskf[:, :].bitcast(U32)
    EVEN = lambda n: WE if n % 2 == 0 else WO

    def write_entries(pool):
        for j in range(TOPK):
            pool.indirect_dma_start(out=LISTS[:, :], out_offset=bass.IndirectOffsetOnAxis(ap=slot[:, j:j + 1], axis=0),
                                    in_=tw[:, j, :], in_offset=None).then_inc(lists_written, 16)

    with nc.Fori(0, NTB) as it:
      with nc.Block() as block:
        @block.sync
        def _(sp):
            for g in range(1, NGRP):
                if g >= 2:
                    need(sp, PE, ("proj", GRP * (g - 1) - 1))
                sp.dma_start(wb[g % 2], t["w_in"][:, g]).then_inc(EVEN(g).sem, EVEN(g).mark(g, 16))
            need(sp, PE, ("y", 1, 1))
            need(sp, DV, ("st", 1, 1))
            need(sp, AC, ("y", 1, 1))
            sp.dma_start(ws13, t["ws13"].rearrange("(p c) n -> p c n", c=DC)).then_inc(SL.sem, 16)
            sp.dma_start(ws2, t["ws2"].rearrange("(p c) n -> p c n", c=2)).then_inc(SL.sem, 16)

            def load_rows(tt):
                c = (R0, R1)[tt % 2]
                sp.dma_start(xr[tt % 2], t["x"][bass.ds(it * TB + tt * P, P), :]).then_inc(c.sem, c.mark(tt, 16))

            for tt in range(2):
                load_rows(tt)
            following = sp.snap((it + 1) % NTB)
            sp.dma_start(ut, t["xt"][:, :, bass.ds(following * TB, TB)]).then_inc(XL.sem, 16)
            sp.dma_start(wb[0], t["w_in"][:, 0]).then_inc(XL.sem, 16)
            for tt in range(NCH):
                need(sp, DV, ("x1", tt))
                sp.dma_start(X1[bass.ds(it * TB + tt * P, P), :], x1[tt % 2]).then_inc((X0, X1S)[tt % 2].sem, (X0, X1S)[tt % 2].mark(tt, 16))
                if tt + 2 < NCH:
                    load_rows(tt + 2)
                need(sp, DV, ("u2", tt))
                sp.dma_start(U2[bass.ds(it * TB + tt * P, P), :], u2).then_inc(ST.sem, ST.mark(("u2", tt), 16))
                need(sp, AC, ("ysh", tt))
                sp.dma_start(YACC[bass.ds(it * TB + tt * P, P), :], ysh).then_inc(SS.sem, SS.mark(tt, 16))
            sp.wait_ge(XL.sem, 32)
            sp.wait_ge(ST.sem, ST.n)
            sp.wait_ge(SS.sem, SS.n)
            sp.wait_ge(X0.sem, X0.n)
            sp.wait_ge(X1S.sem, X1S.n)
            sp.drain()

        @block.tensor
        def _(pe):
            def mark(mm, key):
                mm.then_inc(PE.sem, PE.mark(key))

            for n in range(NPT):
                g = n // GRP
                if n % GRP == 0 and g:
                    need(pe, EVEN(g), g)
                if n >= 4:
                    need(pe, *((DV, ("evac", n - 4)) if n - 4 in (8, 10, 19, 20) else (AC, ("evac", n - 4))))
                for c in range(DC):
                    if n == 0:
                        need(pe, DV, ("ut", c))
                    mm = pe.matmul(bank[n % 4][:, :], wb[g % 2][:, c, (n % GRP) * P:(n % GRP + 1) * P], ut[:, c, :],
                                   start=(c == 0), stop=(c == DC - 1))
                mark(mm, ("proj", n))
                if n == 8:
                    need(pe, AC, "lt")
                    for ct in range(2):
                        mark(pe.matmul(bank[4 + ct][:, :], lora[0:32, ct * P:(ct + 1) * P], tmp[5][0:32, 0, :],
                                       start=True, stop=True), ("lw", ct))
                        mark(pe.matmul(bank[6 + ct][:, :], lora[32:64, ct * P:(ct + 1) * P], tmp[5][32:64, 0, :],
                                       start=True, stop=True), ("la", ct))
                if n == 12:
                    need(pe, DV, "kksq")
                    for ct in range(2):
                        need(pe, AC, ("sig_w", ct))
                        mark(pe.matmul(bank[4 + ct][:, :], blk1[:, :], tmp[6][:, ct, :], start=True, stop=True), ("ss", ct))
                if n == 15:
                    need(pe, DV, "rkk")
                    for ct in range(2):
                        need(pe, AC, ("sig_a", ct))
                        mark(pe.matmul(bank[6 + ct][:, :], blk1[:, :], tmp[6][:, ct, :], start=True, stop=True), ("bonus", ct))
                    for ct in range(2):
                        need(pe, AC, ("knorm", ct))
                        mark(pe.matmul(bank[4 + ct][:, :], lora[64:128, ct * P:(ct + 1) * P], tmp[5][64:128, 0, :],
                                       start=True, stop=True), ("lg", ct))
            need(pe, DV, ("u", 1))
            need(pe, DV, "bonus")
            need(pe, AC, ("g", 1))
            for ct in range(2):
                mark(pe.matmul(bank[4 + ct][:, :], wri[:, 0, ct, :], tmp[2][:, ct, :], start=True, stop=True), ("gr", ct))
                mark(pe.matmul(bank[6 + ct][:, :], wri[:, 1, ct, :], tmp[2][:, ct, :], start=True, stop=True), ("gi", ct))

            need(pe, AC, ("evac", 18))
            need(pe, DV, ("evac", 20))
            need(pe, DV, "rp")
            need(pe, AC, ("gi", 1))
            for w in range(2):
                if w:
                    need(pe, AC, ("y", 0, 1))
                    need(pe, DV, ("st", 0, 1))
                for cc in range(2):
                    ch = 2 * w + cc
                    cs = slice(ch * P, (ch + 1) * P)
                    for ct in range(2):
                        pe.transpose(bank[2 * cc][:, ct * P:(ct + 1) * P], kr[:, ct, ch, 0, :], ident[:, :])
                        pe.transpose(bank[2 * cc][:, (2 + ct) * P:(3 + ct) * P], pc[:, 4 + ct, 1 + ch * P:1 + (ch + 1) * P], ident[:, :])
                        pe.transpose(bank[2 * cc + 1][:, ct * P:(ct + 1) * P], kh[:, ct, cs], ident[:, :])
                        mm = pe.transpose(bank[2 * cc + 1][:, (2 + ct) * P:(3 + ct) * P], bh[:, ct, cs], ident[:, :])
                    mark(mm, ("tok", w, cc))
                for n in range(8):
                    cc, h = n // 4, n % 4
                    ct, o, ch = h // 2, 64 * (h % 2), 2 * w + cc
                    cs = slice(ch * P, (ch + 1) * P)
                    if n >= 4:
                        need(pe, DV, ("gm", w, n - 4))
                    rhs = kr[o:o + 64, ct, ch, :, :].rearrange("p a b -> p (a b)")
                    pe.matmul(bank[4 + h][:, 0:256], bh[o:o + 64, ct, cs], rhs, start=True, stop=True)
                    mark(pe.matmul(bank[4 + h][:, 256:512], kh[o:o + 64, ct, cs], rhs, start=True, stop=True), ("g4", w, n))
                need(pe, AC, ("tok", w, 1))
                for n in range(8):
                    cc, h = n // 4, n % 4
                    need(pe, DV, ("gm", w, n))
                    mm = pe.matmul(bank[0][:, n * 64:(n + 1) * 64], gm[:, n, 256:384], tk[:, cc, 0, h * 64:(h + 1) * 64], start=True, stop=True)
                mark(mm, ("av", w))
                need(pe, PO, ("em", w, 0))
                for cc in range(2):
                    for h in range(4):
                        n = 4 * cc + h
                        mm = pe.matmul(bank[3 + cc][:, h * P:(h + 1) * P], em[:, n, :], ident[:, :], start=True, stop=True)
                    mark(mm, ("q", w, 0, cc))
                for lv in range(1, len(LEVELS)):
                    need(pe, PO, ("em", w, lv))
                    for cc in range(2):
                        need(pe, DV, ("x", w, lv - 1, cc))
                        for h in range(4):
                            n = 4 * cc + h
                            mm = pe.matmul(bank[1 + cc][:, h * P:(h + 1) * P], em[:, n, :], xi[:, n, :], start=True, stop=True)
                        mark(mm, ("p", w, lv, cc))
                    if w == 1 and lv in (1, 3):
                        if lv == 1:
                            need(pe, DV, "conv_a")
                        else:
                            need(pe, AC, "lasq")
                        for ct in range(2):
                            mm = pe.matmul(bank[7][:, :], ones[:, :], ya[:, ct, :] if lv == 1 else tmp[3][:, ct, :],
                                           start=(ct == 0), stop=(ct == 1))
                        mark(mm, "lam" if lv == 1 else "lav")
                    for cc in range(2):
                        need(pe, AC, ("pm", w, lv, cc))
                        need(pe, DV, ("xt", w, lv - 1, cc))
                        if lv < len(LEVELS) - 1:
                            for h in range(4):
                                n = 4 * cc + h
                                mm = pe.matmul(bank[3 + cc][:, h * P:(h + 1) * P], xt[:, n, :], pm[:, n, :], start=True, stop=True)
                            mark(mm, ("q", w, lv, cc))
                        for h in range(4):
                            n = 4 * cc + h
                            mm = pe.matmul(bank[5 + cc][:, h * P:(h + 1) * P], pm[:, n, :], xt[:, n, :], start=True, stop=True)
                        mark(mm, ("qt", w, lv, cc))
                need(pe, AC, ("av", w))
                for cc in range(2):
                    need(pe, DV, ("xt", w, len(LEVELS) - 1, cc))
                    for h in range(4):
                        n = 4 * cc + h
                        mm = pe.matmul(bank[1 + cc][:, h * P:(h + 1) * P], xt[:, n, :], rb[:, n, :], start=True, stop=True)
                    mark(mm, ("wg", w, cc))
                for cc in range(2):
                    need(pe, AC, ("wg", w, cc))
                    for h in range(4):
                        n, o, ct = 4 * cc + h, 64 * (h % 2), h // 2
                        q = 2 * cc + ct
                        pe.matmul(bank[3][o:o + 64, q * P:(q + 1) * P], pm[:, n, 0:64], gm[:, n, 128:256], start=True, stop=True)
                        mm = pe.matmul(bank[4][o:o + 64, q * 64:(q + 1) * 64], pm[:, n, 0:64], tk[:, cc, 2, h * 64:(h + 1) * 64],
                                       start=True, stop=True)
                mark(mm, ("rk", w))
                need(pe, DV, ("rk", w))
                need(pe, DV, ("phi", w))
                for cc in range(2):
                    need(pe, DV, ("sin", w, cc))
                    for h in range(4):
                        n, o, ct = 4 * cc + h, 64 * (h % 2), h // 2
                        q = 2 * cc + ct
                        vt = tk[:, cc, 0, h * 64:(h + 1) * 64]
                        out = bank[5][o:o + 64, ct * 64:(ct + 1) * 64]
                        pe.matmul(out, tk[:, cc, 1, h * 64:(h + 1) * 64], vt, start=True, stop=False)
                        pe.matmul(out, tk[:, cc, 2, h * 64:(h + 1) * 64], pm[:, n, 64:128], start=False, stop=False)
                        mm = pe.matmul(out, phi[o:o + 64, q, :], s_in[o:o + 64, ct, :], start=False, stop=True)
                    mark(mm, ("st", w, cc))
                    for h in range(4):
                        n, o, ct = 4 * cc + h, 64 * (h % 2), h // 2
                        q = 2 * cc + ct
                        vt = tk[:, cc, 0, h * 64:(h + 1) * 64]
                        out = bank[6 + cc][o:o + 64, ct * P:(ct + 1) * P]
                        pe.matmul(out, vt, gm[:, n, 384:512], start=True, stop=False)
                        pe.matmul(out, pm[:, n, 64:128], gm[:, n, 128:256], start=False, stop=False)
                        mm = pe.matmul(out, s_in[o:o + 64, ct, :], rk[o:o + 64, q, :], start=False, stop=True)
                    mark(mm, ("y", w, cc))

            def out_products(tt, n, ks, first=False, last=False):
                ts = slice(tt * P, (tt + 1) * P)
                mats = [ya[:, 0, ts], ya[:, 1, ts], yb[:, 0, ts], yb[:, 1, ts],
                        pc[:, 0, 1 + tt * P:1 + (tt + 1) * P], pc[:, 1, 1 + tt * P:1 + (tt + 1) * P], yd[:, 0, ts], yd[:, 1, ts]]
                for k in ks:
                    mm = pe.matmul(bank[n][:, :], mats[k], wout[:, k, n * 512:(n + 1) * 512],
                                   start=(first and k == ks[0]), stop=(last and k == ks[-1]))
                if last:
                    mark(mm, ("out", tt, n))

            OTHERS, RWKV = (0, 1, 2, 3, 6, 7), (4, 5)
            need(pe, AC, ("y", 1, 1))
            for ct in range(2):
                mark(pe.matmul(bank[2 + ct][:, :], blk1[:, :], tmp[0][:, ct, :], start=True, stop=True), ("gnm", ct))
            need(pe, AC, "ya")
            need(pe, DV, "yb")
            need(pe, DV, "yd")
            pe.wait_ge(wout_loaded, 16)
            out_products(0, 0, OTHERS, first=True)
            need(pe, AC, "gnsq")
            for ct in range(2):
                need(pe, DV, ("gnd", ct))
                mark(pe.matmul(bank[2 + ct][:, :], blk1[:, :], tmp[2][:, ct, :], start=True, stop=True), ("gnv", ct))
            out_products(0, 1, OTHERS, first=True)
            need(pe, DV, ("yc", 0))
            for n in range(2):
                out_products(0, n, RWKV, last=True)

            def rank(tt):
                need(pe, DV, ("sel", tt))
                pe.matmul(bank[7][:, 0:NE], maskf[:, 0:P], rt[:, 128:128 + NE], start=True, stop=False)
                mark(pe.matmul(bank[7][:, 0:NE], ones[:, :], cum_sel[:, :], start=False, stop=True), ("rank", tt))

            for tt in range(NCH):
                if tt + 1 < NCH:
                    need(pe, DV, ("outev", tt))
                    if tt + 1 == NCH // 2:
                        need(pe, DV, ("yc", 1))
                    out_products(tt + 1, 0, range(DC), first=True, last=True)
                    if tt:
                        rank(tt - 1)
                    out_products(tt + 1, 1, range(DC), first=True, last=True)
                else:
                    rank(tt - 1)
                if tt:
                    need(pe, AC, ("ysh", tt - 1))
                need(pe, DV, ("u2", tt))
                v = u2.rearrange("p (n c) -> p n c", c=DC)
                for k in range(DC):
                    mm = pe.transpose(bank[2 + k // 4][:, (k % 4) * P:(k % 4 + 1) * P], v[:, :, k], ident[:, :])
                    if k % 4 == 3:
                        mark(mm, ("u2t", tt, k // 4))
                need(pe, AC, ("u2t", tt))
                if tt:
                    need(pe, AC, ("score", tt - 1))
                for k in range(DC):
                    mm = pe.matmul(bank[4][:, 0:NE], u2t[:, k, :], wrt[:, k, :], start=(k == 0), stop=(k == DC - 1))
                mark(mm, ("score", tt))
                if tt == 0:
                    pe.wait_ge(SL.sem, 32)
                for k in range(DC):
                    mm = pe.matmul(bank[5][:, :], u2t[:, k, :], ws13[:, k, :], start=(k == 0), stop=(k == DC - 1))
                mark(mm, ("sh", tt))
                need(pe, DV, ("hs", tt))
                v = hs.rearrange("p (n c) -> p n c", c=2)
                for k in range(2):
                    mm = pe.transpose(bank[6][:, k * P:(k + 1) * P], v[:, :, k], ident[:, :])
                mark(mm, ("hst", tt))
                need(pe, AC, ("hst", tt))
                for n in range(2):
                    for k in range(2):
                        mm = pe.matmul(bank[2 + n][:, :], hst[:, k * P:(k + 1) * P], ws2[:, k, n * 512:(n + 1) * 512],
                                       start=(k == 0), stop=(k == 1))
                mark(mm, ("ysh", tt))
            rank(NCH - 1)

        @block.scalar
        def _(act):
            do = stepper(act, AC)

            def evac(n):
                need(act, PE, ("proj", n))
                src = bank[n % 4][:, :]
                if n < 7:
                    do(act.activation(pc[:, n, 1:1 + TB], src, ACT.Copy), ("evac", n), wait=False)
                elif n in (7, 9):
                    do(act.activation(ya[:, (n - 7) // 2, :], src, ACT.Sigmoid), ("evac", n), wait=False)
                elif n in (11, 12):
                    do(act.activation(xb[:, n - 11, HALO_B:], src, ACT.Copy), ("evac", n), wait=False)
                elif n in (13, 14):
                    do(act.activation(yb[:, n - 13, :], src, ACT.Gelu_apprx_tanh), ("evac", n), wait=False)
                elif n in (15, 16):
                    do(act.activation(yd[:, n - 15, :], src, ACT.Copy), ("evac", n), wait=False)
                elif n in (17, 18):
                    do(act.activation(pd[:, n - 17, HALO_D:], src, ACT.Copy), ("evac", n), wait=False)

            for n in range(7):
                evac(n)
            evac(7)
            need(act, DV, ("xs", 6))
            do(act.activation(tmp[5][32:64, 0, :], pc[32:64, 6, 1:1 + TB], ACT.Copy), wait=False)
            do(act.activation(tmp[5][64:128, 0, :], pc[64:128, 6, 1:1 + TB], ACT.Sigmoid), wait=False)
            do(act.activation(tmp[5][0:32, 0, :], pc[0:32, 6, 1:1 + TB], ACT.Tanh), "lt")
            evac(9)
            need(act, DV, ("xs", 5))
            for ct in range(2):
                need(act, PE, ("lw", ct))
                do(act.activation(tmp[0][:, ct, :], bank[4 + ct][:, :], ACT.Sigmoid, bias=cvc("w0", ct)), ("sig_w", ct), wait=False)
                need(act, PE, ("la", ct))
                do(act.activation(tmp[1][:, ct, :], bank[6 + ct][:, :], ACT.Sigmoid, bias=cvc("a0", ct)), ("sig_a", ct), wait=False)
            evac(11)
            evac(12)
            need(act, DV, "csx")
            v = lambda a: flat(a).rearrange("p (a b) -> p a b", b=P)
            krv = lambda j: kr[:, :, :, j, :].rearrange("p a b c -> p (a b) c")
            do(act.activation(krv(0), v(tmp[0]), ACT.Exp, scale=-EM05), "ex", wait=False)
            do(act.activation(krv(1), v(tmp[3]), ACT.Exp, scale=-EM05), "em", wait=False)
            dv = dsc[:, :, :, :].rearrange("p a b c -> p (a b) c")
            do(act.activation(dv[:, :, 0], v(tmp[2])[:, :, P // 2 - 1], ACT.Exp, scale=-EM05), wait=True)
            do(act.activation(dv[:, :, 1], v(tmp[3])[:, :, P - 1], ACT.Exp, scale=-EM05), "dsc", wait=False)
            do(act.activation(flat(tmp[2]), flat(tmp[3]), ACT.Exp, scale=EM05), "ep", wait=False)
            for ct in range(2):
                need(act, PE, ("ss", ct))
                do(act.activation(tmp[6][:, ct, :], bank[4 + ct][:, :], ACT.Sqrt, bias=epsc[:, 1:2]), ("knorm", ct), wait=False)
            evac(13)
            evac(14)
            evac(15)
            evac(16)
            for ct in range(2):
                need(act, PE, ("lg", ct))
                need(act, DV, "rp")
                do(act.activation(pc[:, ct, 1:1 + TB], bank[4 + ct][:, :], ACT.Copy), ("g", ct), wait=False)
            evac(17)
            evac(18)
            for ct in range(2):
                need(act, PE, ("gr", ct))
                do(act.activation(tmp[3][:, ct, :], bank[4 + ct][:, :], ACT.Sigmoid, bias=cvc("b_rg", ct)), ("gr", ct))
                need(act, PE, ("gi", ct))
                do(act.activation(tmp[4][:, ct, :], bank[6 + ct][:, :], ACT.Sigmoid, bias=cvc("b_ig", ct)), ("gi", ct), wait=False)
            for w in range(2):
                for cc in range(2):
                    need(act, PE, ("tok", w, cc))
                    do(act.activation(rb[:, 4 * cc:4 * cc + 4, 0:64], bank[2 * cc][:, 0:256].rearrange("p (h k) -> p h k", k=64),
                                      ACT.Copy), wait=False)
                    do(act.activation(tk[:, cc, 0, :], bank[2 * cc][:, 256:512], ACT.Copy), wait=False)
                    do(act.activation(tk[:, cc, 1:3, :].rearrange("p a b -> p (a b)"), bank[2 * cc + 1][:, :], ACT.Copy),
                       ("tok", w, cc), wait=False)
                need(act, PE, ("av", w))
                do(act.activation(rb[:, :, 64:128], bank[0][:, :].rearrange("p (n k) -> p n k", k=64), ACT.Copy), ("av", w), wait=False)
                if w == 0:
                    for ct in range(2):
                        do(act.activation(tmp[3][:, ct, :], tmp[3][:, ct, :], ACT.Tanh, scale=chalf[:, ct:ct + 1]), ("t", ct))
                    do(act.activation(flat(tmp[5]), flat(tmp[3]), ACT.Sqrt), "sqt", wait=False)
                for lv in range(1, len(LEVELS)):
                    for cc in range(2):
                        need(act, PE, ("p", w, lv, cc))
                        do(act.activation(pm[:, 4 * cc:4 * cc + 4, :].rearrange("p a b -> p (a b)"), bank[1 + cc][:, :], ACT.Copy),
                           ("pm", w, lv, cc), wait=False)
                    if (w, lv) == (1, 2):
                        for ct in range(2):
                            need(act, DV, ("lad", ct))
                            do(act.activation(tmp[3][:, ct, :], ya[:, ct, :], ACT.Square), "lasq", wait=False)
                    if (w, lv) == (1, 3):
                        need(act, PE, "lav")
                        do(act.activation(tmp[4][:, 0, :], bank[7][:, :], ACT.Sqrt, bias=epsc[:, 0:1], scale=1.0 / 256),
                           "las", wait=False)
                    if (w, lv) == (1, 6):
                        for ct in range(2):
                            need(act, DV, ("laz", ct))
                            do(act.activation(ya[:, ct, :], ya[:, ct, :], ACT.Silu, bias=cvc("ln_a_b", ct), scale=cvc("ln_a_g", ct)),
                               "ya", wait=False)
                for cc in range(2):
                    need(act, PE, ("wg", w, cc))
                    do(act.activation(pm[:, 4 * cc:4 * cc + 4, :].rearrange("p a b -> p (a b)"), bank[1 + cc][:, :], ACT.Copy,
                                      scale=-1.0), ("wg", w, cc), wait=False)
                for cc in range(2):
                    ch = 2 * w + cc
                    need(act, PE, ("y", w, cc))
                    do(act.activation(tmp[0][:, :, ch * P:(ch + 1) * P], bank[6 + cc][:, 0:256].rearrange("p (c n) -> p c n", n=P),
                                      ACT.Copy), ("y", w, cc), wait=False)
            for ct in range(2):
                need(act, DV, ("gnd", ct))
                do(act.activation(tmp[2][:, ct, :], tmp[0][:, ct, :], ACT.Square), "gnsq", wait=False)
            for ct in range(2):
                need(act, PE, ("gnv", ct))
                do(act.activation(tmp[2][:, ct, :], bank[2 + ct][:, :], ACT.Sqrt, bias=epsc[:, 2:3], scale=1.0 / 64), ("gns", ct), wait=False)
            def std(tt):
                need(act, DV, ("var", tt))
                do(act.activation(small[:, 44:45], small[:, 41:42], ACT.Sqrt, bias=epsc[:, 0:1]), ("std", tt), wait=False)

            std(0)
            for tt in range(NCH):
                for k in range(2):
                    need(act, PE, ("u2t", tt, k))
                    do(act.activation(u2t[:, 4 * k:4 * k + 4, :].rearrange("p a b -> p (a b)"), bank[2 + k][:, :], ACT.Copy),
                       ("u2t", tt), wait=False)
                need(act, PE, ("score", tt))
                if tt:
                    need(act, DV, ("routed", tt - 1))
                do(act.activation(rt[:, 0:NE], bank[4][:, 0:NE], ACT.Sigmoid), ("score", tt), wait=False)
                if tt + 1 < NCH:
                    std(tt + 1)
                need(act, PE, ("sh", tt))
                do(act.activation(hs, bank[5][:, 0:256], ACT.Silu), ("silu", tt), wait=False)
                need(act, PE, ("hst", tt))
                do(act.activation(hst, bank[6][:, 0:256], ACT.Copy), ("hst", tt), wait=False)
                need(act, PE, ("ysh", tt))
                if tt:
                    need(act, SS, tt - 1)
                for n in range(2):
                    do(act.activation(ysh[:, n * 512:(n + 1) * 512], bank[2 + n][:, :], ACT.Copy), ("ysh", tt), wait=False)

        @block.vector
        def _(dve):
            do = stepper(dve, DV)
            v = lambda a: flat(a).rearrange("p (a b) -> p a b", b=P)
            krv = lambda j: kr[:, :, :, j, :].rearrange("p a b c -> p (a b) c")
            for c in range(DC):
                do(dve.tensor_scalar(ut[:, c, :], ut[:, c, :], sccol[:, c:c + 1], shcol[:, c:c + 1], ALU.mult, ALU.add), ("ut", c), wait=False)
            for j in (6, 0, 2, 4):
                m = 1 if j == 6 else 2
                need(dve, AC, ("evac", j + m - 1))
                if j == 6:
                    d = tmp[6][:, 0:1, :]
                else:
                    d = tmp[{0: 0, 2: 1, 4: 2}[j]][:, :, :]
                do(dve.tensor_copy(pclast[:, j:j + m], pc[:, j:j + m, TB]), wait=False)
                do(dve.tensor_tensor(d, pc[:, j:j + m, 0:TB], pc[:, j:j + m, 1:1 + TB], ALU.subtract))
                for i in range(m):
                    x = pc[:, j + i, 1:1 + TB]
                    do(dve.scalar_tensor_tensor(out=x, in0=d[:, i, :], scalar=cvc("mu_c", j + i), in1=x, op0=ALU.mult, op1=ALU.add),
                       ("xs", j + i))
            def gate_a(n):
                need(dve, PE, ("proj", n))
                need(dve, AC, ("evac", n - 1))
                do(dve.tensor_tensor(hid[:, (n - 8) // 2, HALO_A:], bank[n % 4][:, :], ya[:, (n - 8) // 2, :], ALU.mult), ("evac", n), wait=False)
            gate_a(8)
            for ct in range(2):
                do(dve.tensor_scalar(tmp[4][:, ct, :], pc[:, 2 + ct, 1:1 + TB], cvc("k_k", ct), None, ALU.mult))
                do(dve.tensor_tensor(tmp[6][:, ct, :], tmp[4][:, ct, :], tmp[4][:, ct, :], ALU.mult), "kksq")
            gate_a(10)
            for ct in range(2):
                need(dve, AC, ("sig_w", ct))
                do(dve.tensor_tensor_scan(tmp[2][:, ct, :], scan_keep[:, :], tmp[0][:, ct, :], 0.0, ALU.mult, ALU.add))
            mid = v(tmp[2])[:, :, P // 2 - 1:P // 2].to_broadcast([P, 2 * NCH, P])
            do(dve.tensor_tensor(v(tmp[3]), v(tmp[2]), mid, ALU.subtract))
            do(dve.tensor_tensor(flat(tmp[0]), flat(tmp[3]), flat(tmp[0]), ALU.subtract), "csx")
            taps = [(ct, k) for k in range(30, -1, -1) for ct in range(2)]

            tapped = []

            def tap(count):
                for _ in range(count):
                    if not taps:
                        return
                    ct, k = taps.pop(0)
                    if k < 30:
                        dve.wait_ge(DV.sem, tapped.pop(0))
                    a, x = ya[:, ct, :], hid[:, ct, k:k + TB]
                    if k == 30:
                        do(dve.tensor_scalar(a, x, cvc("conv_a", 2 * k + ct), cvc("conv_a_bias", ct), ALU.mult, ALU.add), wait=False)
                    else:
                        do(dve.scalar_tensor_tensor(out=a, in0=x, scalar=cvc("conv_a", 2 * k + ct), in1=a, op0=ALU.mult, op1=ALU.add),
                           "conv_a", wait=False)
                    tapped.append(DV.n)

            need(dve, DV, ("evac", 10))
            tap(22)
            for ct in range(2):
                need(dve, AC, ("knorm", ct))
                do(dve.reciprocal(tmp[6][:, ct, :], tmp[6][:, ct, :]))
            do(dve.tensor_tensor(flat(tmp[4]), flat(tmp[4]), flat(tmp[6]), ALU.mult))
            need(dve, AC, "ex")
            do(dve.tensor_tensor(krv(0), krv(0), v(tmp[4]), ALU.mult), "kp", wait=False)
            need(dve, AC, ("sig_a", 1))
            do(dve.tensor_tensor(flat(tmp[4]), flat(tmp[4]), flat(tmp[1]), ALU.mult))
            need(dve, AC, "ep")
            do(dve.tensor_tensor(flat(bh), flat(tmp[4]), flat(tmp[2]), ALU.mult), wait=False)
            for ct in range(2):
                k, r = pc[:, 2 + ct, 1:1 + TB], pc[:, ct, 1:1 + TB]
                do(dve.tensor_scalar(tmp[6][:, ct, :], tmp[1][:, ct, :], -1.0, cvc("k_a", ct), ALU.add, ALU.mult))
                do(dve.scalar_tensor_tensor(out=k, in0=tmp[6][:, ct, :], scalar=1.0, in1=k, op0=ALU.add, op1=ALU.mult))
                do(dve.tensor_tensor(kh[:, ct, :], k, tmp[2][:, ct, :], ALU.mult), wait=False)
                do(dve.scalar_tensor_tensor(out=tmp[6][:, ct, :], in0=r, scalar=cvc("r_k", ct), in1=k, op0=ALU.mult, op1=ALU.mult), "rkk")
            need(dve, AC, "em")
            do(dve.tensor_tensor(kr[:, :, :, 1, :].rearrange("p a b c -> p a b c"), kr[:, :, :, 1, :],
                                 pc[:, 0:2, 1:1 + TB].rearrange("p a (b c) -> p a b c", c=P), ALU.mult), "rp")
            for ct in range(2):
                need(dve, PE, ("bonus", ct))
                do(dve.tensor_tensor(tmp[1][:, ct, :], bank[6 + ct][:, :], pc[:, 4 + ct, 1:1 + TB], ALU.mult), "bonus", wait=False)
            for ct in range(2):
                need(dve, AC, ("evac", 11 + ct))
                u = tmp[2][:, ct, :]
                do(dve.tensor_scalar(u, xb[:, ct, HALO_B:], cvc("conv_b", 2 * 3 + ct), cvc("conv_b_bias", ct), ALU.mult, ALU.add))
                for k in range(3):
                    do(dve.scalar_tensor_tensor(out=u, in0=xb[:, ct, k:k + TB], scalar=cvc("conv_b", 2 * k + ct), in1=u,
                                                op0=ALU.mult, op1=ALU.add), ("u", ct))
            tap(34)
            for ct in range(2):
                need(dve, PE, ("proj", 19 + ct))
                need(dve, AC, ("evac", 17 + ct))
                x = pd[:, ct, HALO_D:]
                do(dve.tensor_tensor(x, bank[(19 + ct) % 4][:, :], x, ALU.mult), ("evac", 19 + ct))
            need(dve, AC, ("evac", 16))
            for ct in range(2):
                a = tmp[6][:, ct, :]
                do(dve.tensor_scalar(a, pd[:, ct, HALO_D:], cvc("conv_d", 4 + ct), None, ALU.mult))
                for k in range(2):
                    do(dve.scalar_tensor_tensor(out=a, in0=pd[:, ct, k:k + TB], scalar=cvc("conv_d", 2 * k + ct), in1=a,
                                                op0=ALU.mult, op1=ALU.add))
            do(dve.tensor_tensor(flat(yd), flat(yd), flat(tmp[6]), ALU.mult), "yd")
            tap(6)

            def between(w, lv):
                if (w, lv) == (0, 2):
                    need(dve, AC, ("t", 1))
                    do(dve.tensor_scalar(flat(tmp[6]), flat(tmp[3]), 1.0, None, ALU.add))
                    do(dve.reciprocal(tmp[6][:, 0, :], tmp[6][:, 0, :]), wait=False)
                if (w, lv) == (0, 3):
                    do(dve.reciprocal(tmp[6][:, 1, :], tmp[6][:, 1, :]), "recip", wait=False)
                if (w, lv) == (0, 4):
                    do(dve.tensor_tensor(flat(tmp[4]), flat(tmp[4]), flat(tmp[2]), ALU.mult), "gated", wait=False)
                    need(dve, AC, "sqt")
                    need(dve, DV, "recip")
                    do(dve.tensor_scalar(flat(tmp[3]), flat(tmp[6]), 2.0, -1.0, ALU.mult, ALU.add), "decay", wait=False)
                if (w, lv) == (0, 5):
                    do(dve.scalar_tensor_tensor(out=flat(tmp[5]), in0=flat(tmp[5]), scalar=2.0, in1=flat(tmp[6]), op0=ALU.mult, op1=ALU.mult))
                    need(dve, DV, "gated")
                    do(dve.tensor_tensor(flat(tmp[4]), flat(tmp[4]), flat(tmp[5]), ALU.mult), "input", wait=False)
                if (w, lv) in ((0, 6), (1, 1)):
                    ct = w
                    need(dve, DV, "input")
                    need(dve, DV, "decay")
                    do(dve.tensor_tensor_scan(tmp[2][:, ct, :], tmp[3][:, ct, :], tmp[4][:, ct, :], hlast[:, ct:ct + 1], ALU.mult, ALU.add))
                    do(dve.tensor_copy(hlast[:, ct:ct + 1], tmp[2][:, ct, TB - 1:TB]), wait=False)
                if (w, lv) == (1, 2):
                    need(dve, PE, "lam")
                    for ct in range(2):
                        x = ya[:, ct, :]
                        do(dve.scalar_tensor_tensor(out=x, in0=bank[7][:, :], scalar=-1.0 / 256, in1=x, op0=ALU.mult, op1=ALU.add),
                           ("lad", ct), wait=False)
                if (w, lv) == (1, 3):
                    need(dve, AC, ("evac", 14))
                    do(dve.tensor_tensor(flat(yb), flat(yb), flat(tmp[2]), ALU.mult), "yb", wait=False)
                if (w, lv) == (1, 4):
                    need(dve, AC, "las")
                    do(dve.reciprocal(tmp[4][:, 0, :], tmp[4][:, 0, :]), "rlas", wait=False)
                if (w, lv) == (1, 5):
                    need(dve, DV, "rlas")
                    for ct in range(2):
                        do(dve.tensor_tensor(ya[:, ct, :], ya[:, ct, :], tmp[4][:, 0, :], ALU.mult), ("laz", ct), wait=False)

            need(dve, PO, "zero")
            for w in range(2):
                for n in range(8):
                    need(dve, PE, ("g4", w, n))
                    do(dve.copy_predicated(gm[:, n, :], mask_u, bank[4 + n % 4][:, :]), ("gm", w, n), wait=False)
                need(dve, PO, ("em", w, 0))
                idb = ident[:, :].unsqueeze(1).to_broadcast([P, 4, P])
                for cc in range(2):
                    q = slice(4 * cc, 4 * cc + 4)
                    do(dve.tensor_tensor(xt[:, q, :], idb, em[:, q, :], ALU.subtract), ("xt", w, 0, cc), wait=False)
                    need(dve, PE, ("q", w, 0, cc))
                    do(dve.tensor_tensor(xi[:, q, :], idb, bank[3 + cc][:, :].rearrange("p (a b) -> p a b", b=P), ALU.subtract),
                       ("x", w, 0, cc), wait=False)
                for lv in range(1, len(LEVELS)):
                    between(w, lv)
                    for cc in range(2):
                        q = slice(4 * cc, 4 * cc + 4)
                        if lv < len(LEVELS) - 1:
                            need(dve, PE, ("q", w, lv, cc))
                            need(dve, DV, ("x", w, lv - 1, cc))
                            x = xi[:, q, :].rearrange("p a b -> p (a b)")
                            do(dve.tensor_tensor(x, x, bank[3 + cc][:, :], ALU.subtract), ("x", w, lv, cc), wait=False)
                        need(dve, PE, ("qt", w, lv, cc))
                        need(dve, DV, ("xt", w, lv - 1, cc))
                        x = xt[:, q, :].rearrange("p a b -> p (a b)")
                        do(dve.tensor_tensor(x, x, bank[5 + cc][:, :], ALU.subtract), ("xt", w, lv, cc), wait=False)
                need(dve, PE, ("rk", w))
                for cc in range(2):
                    ch = 2 * w + cc
                    do(dve.tensor_tensor(rk[:, 2 * cc:2 * cc + 2, :], bank[3][:, cc * 256:(cc + 1) * 256].rearrange("p (a b) -> p a b", b=P),
                                         kr[:, :, ch, 1, :], ALU.add), ("rk", w), wait=False)
                e2 = eye2[:, :].unsqueeze(1).to_broadcast([P, 4, 64])
                do(dve.tensor_tensor(phi, bank[4][:, 0:256].rearrange("p (a b) -> p a b", b=64), e2, ALU.add), ("phi", w), wait=False)
                need(dve, AC, "dsc")
                for cc in range(2):
                    ch = 2 * w + cc
                    if cc or w:
                        last = (w, cc - 1) if cc else (0, 1)
                        need(dve, PE, ("y", *last))
                        need(dve, DV, ("st", *last))
                    for ct in range(2):
                        do(dve.tensor_scalar(s_in[:, ct, :], state[:, ct, :], dsc[:, ct, ch, 0:1], None, ALU.mult), ("sin", w, cc), wait=False)
                    need(dve, PE, ("st", w, cc))
                    for ct in range(2):
                        do(dve.tensor_scalar(state[:, ct, :], bank[5][:, ct * 64:(ct + 1) * 64], dsc[:, ct, ch, 1:2], None, ALU.mult),
                           ("st", w, cc), wait=False)

            for ct in range(2):
                need(dve, PE, ("gnm", ct))
                x = tmp[0][:, ct, :]
                do(dve.scalar_tensor_tensor(out=x, in0=bank[2 + ct][:, :], scalar=-1.0 / 64, in1=x, op0=ALU.mult, op1=ALU.add), ("gnd", ct))
            def group_norm(half):
                tokens = slice(half * (TB // 2), (half + 1) * (TB // 2))
                x, r = tmp[0][:, :, tokens], tmp[2][:, :, tokens]
                do(dve.reciprocal(r, r))
                do(dve.tensor_tensor(x, x, r, ALU.mult))
                for ct in range(2):
                    do(dve.tensor_scalar(x[:, ct, :], x[:, ct, :], cvc("gn_g", ct), cvc("gn_b", ct), ALU.mult, ALU.add), wait=(ct == 1))
                do(dve.tensor_tensor(x, x, tmp[1][:, :, tokens], ALU.add))
                g = pc[:, 0:2, 1 + half * (TB // 2):1 + (half + 1) * (TB // 2)]
                do(dve.tensor_tensor(g, g, x, ALU.mult), ("yc", half))

            need(dve, AC, ("gns", 1))
            for half in range(2):
                group_norm(half)

            def residual(tt):
                x = x1[tt % 2]
                need(dve, R0 if tt % 2 == 0 else R1, tt)
                if tt >= 2:
                    need(dve, (X0, X1S)[tt % 2], tt - 2)
                for n in range(2):
                    need(dve, PE, ("out", tt, n))
                    ns = slice(n * 512, (n + 1) * 512)
                    do(dve.tensor_tensor(x[:, ns], bank[n][:, :], g1p1[:, ns], ALU.mult), ("outev", tt), wait=(n == 1))
                do(dve.scalar_tensor_tensor(out=x, in0=xr[tt % 2], scalar=ALPHA, in1=x, op0=ALU.mult, op1=ALU.add), ("res", tt))

            def normalise(tt):
                x = x1[tt % 2]
                st = small[:, 46:58]
                mv = small[:, 40:42]
                for n in range(2):
                    do(dve.bn_stats(st[:, 6 * n:6 * n + 6], x[:, n * 512:(n + 1) * 512]), wait=(n == 1))
                do(dve.bn_aggr(mv, st), ("var", tt))
                need(dve, AC, ("std", tt))
                do(dve.reciprocal(small[:, 44:45], small[:, 44:45]))
                do(dve.tensor_scalar(x, x, mv[:, 0:1], small[:, 44:45], ALU.subtract, ALU.mult))
                do(dve.tensor_tensor(x, x, ln1g[:, :], ALU.mult))
                do(dve.tensor_tensor(x, x, ln1b[:, :], ALU.add), ("x1", tt))
                if tt:
                    need(dve, ST, ("u2", tt - 1))
                    need(dve, PE, ("u2t", tt - 1, 1))
                do(dve.tensor_tensor(u2, x, sc2p1[:, :], ALU.mult))
                do(dve.tensor_tensor(u2, u2, sh2r[:, :], ALU.add), ("u2", tt))

            residual(0)
            normalise(0)
            for tt in range(NCH):
                if tt + 1 < NCH:
                    residual(tt + 1)
                    normalise(tt + 1)
                need(dve, AC, ("silu", tt))
                do(dve.tensor_tensor(hs, hs, bank[5][:, 256:512], ALU.mult), ("hs", tt), wait=False)
                need(dve, AC, ("score", tt))
                sc, bi = rt[:, 0:64], rt[:, 64:128]
                sel, g8 = rt[:, 128:192], rt[:, 192:256]
                gs, top, rep, keep = rt[:, 256:268], rt[:, 268:276], rt[:, 276:288], rt[:, 288:296]
                msk, slots, best, w8 = rt[:, 296:360], rt[:, 360:424], rt[:, 424:432], rt[:, 432:440]
                ssum, slf, idf = rt[:, 440:441], rt[:, 448:456], rt[:, 456:464]
                g3 = lambda a: a.rearrange("p (g e) -> p g e", e=8)
                do(dve.tensor_tensor(bi, sc, ebias[:, :], ALU.add))
                for g in range(NGR):
                    do(dve.max(g8[:, 8 * g:8 * g + 8], bi[:, 8 * g:8 * g + 8]), wait=(g == NGR - 1))
                do(dve.memset(gs[:, 8:12], 1.0e30), wait=False)
                do(dve.tensor_tensor(gs[:, 0:8], g3(g8)[:, :, 0], g3(g8)[:, :, 1], ALU.add))
                do(dve.max(top, gs))
                do(dve.match_replace(rep, top, gs, NEG))
                do(dve.tensor_scalar(keep, rep[:, 0:8], NEG, None, ALU.is_equal))
                kb = keep.unsqueeze(2).to_broadcast([P, NGR, 8])
                do(dve.tensor_tensor(g3(msk), g3(bi), kb, ALU.mult))
                do(dve.tensor_scalar(keep, keep, -NEG, NEG, ALU.mult, ALU.add))
                do(dve.tensor_tensor(g3(msk), g3(msk), kb, ALU.add))
                do(dve.max(best, msk))
                do(dve.match_replace(sel, best, msk, -NEG))
                do(dve.tensor_scalar(sel, sel, -NEG, None, ALU.is_equal), ("sel", tt))
                do(dve.max_index(idx8[:, :], best, msk))
                do(dve.tensor_copy(idf, idx8[:, :]))
                oh = flat(tmp[4])[:, 0:512].rearrange("p (j e) -> p j e", e=NE)
                pr = flat(tmp[4])[:, 512:1024].rearrange("p (j e) -> p j e", e=NE)
                do(dve.tensor_tensor(oh, iota_e[:, :, :], idf.unsqueeze(2).to_broadcast([P, TOPK, NE]), ALU.is_equal))
                do(dve.tensor_tensor(pr, oh, sc.unsqueeze(1).to_broadcast([P, TOPK, NE]), ALU.mult))
                do(dve.tensor_reduce(w8, pr, AX_X, ALU.add))
                do(dve.tensor_reduce(ssum, w8, AX_X, ALU.add))
                do(dve.reciprocal(ssum, ssum))
                need(dve, PE, ("rank", tt))
                do(dve.scalar_tensor_tensor(out=slots, in0=iota_e[:, 0, :], scalar=float(CAP), in1=bank[7][:, 0:NE],
                                            op0=ALU.mult, op1=ALU.add))
                do(dve.tensor_tensor(cum_sel[:, :], cum_sel[:, :], sel, ALU.add), ("cum", tt), wait=False)
                do(dve.tensor_tensor(pr, oh, slots.unsqueeze(1).to_broadcast([P, TOPK, NE]), ALU.mult))
                do(dve.tensor_reduce(slf, pr, AX_X, ALU.add))
                dve.wait_ge(lists_written, it * (16 * TOPK * NCH) + 16 * TOPK * (tt + 1))
                do(dve.tensor_copy(slot[:, :], slf), wait=False)
                do(dve.tensor_scalar(tw[:, :, 1].bitcast(F32), w8, ssum, ROUTED_SCALE, ALU.mult, ALU.mult), ("routed", tt), wait=False)

        @block.gpsimd
        def _(pool):
            do = stepper(pool, PO)
            write_entries(pool)
            need(pool, PE, ("proj", NPT - 1))
            need(pool, DV, ("ut", DC - 1))
            do(pool.memset(gm, 0.0), "zero")
            for w in range(2):
                need(pool, DV, ("gm", w, 7))
                for lv in range(len(LEVELS)):
                    if lv:
                        need(pool, PE, ("p", w, lv - 1, 1) if lv > 1 else ("q", w, 0, 1))
                    if lv == 1:
                        need(pool, DV, ("xt", w, 0, 1))
                    do(pool.tensor_tensor(em, gm[:, :, 0:P], levm[:, lv, :].unsqueeze(1).to_broadcast([P, 8, P]), ALU.mult),
                       ("em", w, lv), wait=False)
            need(pool, DV, "conv_a")
            do(pool.tensor_copy(hid[:, :, 0:HALO_A], hid[:, :, TB:TB + HALO_A]), wait=False)
            do(pool.tensor_copy(xb[:, :, 0:HALO_B], xb[:, :, TB:TB + HALO_B]), wait=False)
            do(pool.tensor_copy(pd[:, :, 0:HALO_D], pd[:, :, TB:TB + HALO_D]), wait=False)
            do(pool.tensor_copy(pc[:, :, 0], pclast[:, :]), wait=False)
            for tt in range(NCH):
                need(pool, DV, ("routed", tt))
                do(pool.tensor_copy(tw[:, :, 0], tok_id[:, bass.ds(it * NCH + tt, 1)].to_broadcast([P, TOPK])))
                if tt + 1 < NCH:
                    write_entries(pool)
      nc.all_engine_barrier(sems_to_clear=span)


    mix.close()

    PE, AC, DV, PO, XL, WE, WO, PL, R0, R1, SL, ST, SS, X0, X1S = stage("tables")
    moe = ExitStack()
    NEED, SPLIT_A, SPLIT_B = range(3)
    NTAB = NBLK + 2
    tab = sb(moe, "tab", [1, NTAB, 3], I32)
    turn_e = sb(moe, "turn_e", [1, NE], I32)
    used = sb(moe, "used", [1, 4], I32)
    LST = NBLK + 5
    list_tok = sb(moe, "list_tok", [P, LST], I32)
    list_w = sb(moe, "list_w", [P, NTAB])
    small_t = ExitStack()
    nb = sb(small_t, "nb", [NE, 8])
    nbi = sb(small_t, "nbi", [NE, 2], I32)
    iob = sb(small_t, "iob", [NE, NTAB])
    ioe = sb(small_t, "ioe", [NE, 1])
    cmp = sb(small_t, "cmp", [NE, NTAB])
    hot = sb(small_t, "hot", [NE, NE])
    r = [sb(small_t, f"row{i}", [1, NTAB]) for i in range(6)]
    urow = sb(small_t, "urow", [1, 2])
    GROUPS = [(0, P), (P, NTAB - P)]
    lidx = sb(small_t, "lidx", [P, 2], I32)
    by_block = sb(small_t, "by_block", [P, 2, P, 2], I32)
    tok_f = sb(small_t, "tok_f", [P, 2, P])
    lists_read = top.enter_context(nc.semaphore("lists_read"))
    with nc.Block() as block:
        @block.tensor
        def _(pe):
            def mark(mm, key):
                mm.then_inc(PE.sem, PE.mark(key))
            mark(pe.matmul(bank[0][0:NE, 0:1], cum_sel[:, :], ones[:, 0:1], start=True, stop=True), "count")
            need(pe, DV, "has")
            mark(pe.matmul(bank[1][0:NE, 0:1], maskf[0:NE, P:P + NE], nb[:, 0:1], start=True, stop=True), "end")
            mark(pe.matmul(bank[2][0:NE, 0:1], maskf[0:NE, 0:NE], nb[:, 2:3], start=True, stop=True), "turn")
            mark(pe.matmul(bank[5][0:1, 0:1], nb[:, 0:1], ones[0:NE, 0:1], start=True, stop=True), "blocks")
            mark(pe.matmul(bank[5][0:1, 8:9], nb[:, 2:3], ones[0:NE, 0:1], start=True, stop=True), "turns")
            need(pe, DV, "hot")
            mark(pe.matmul(bank[7][0:1, 0:NE], ioe[:, :], hot[:, :], start=True, stop=True), "turn_e")
            mark(pe.matmul(bank[3][0:1, 0:NTAB], ones[0:NE, 0:1], cmp[:, :], start=True, stop=True), "e")
            mark(pe.matmul(bank[4][0:1, 0:NTAB], nb[:, 0:1], cmp[:, :], start=True, stop=True), "s")
            mark(pe.matmul(bank[6][0:1, 0:NTAB], nb[:, 2:3], cmp[:, :], start=True, stop=True), "o")
            need(pe, DV, "row")
            for g, (o, w) in enumerate(GROUPS):
                mm = pe.matmul(bank[0][0:w, g:g + 1], r[1][:, o:o + w], ones[0:1, 0:1], start=True, stop=True)
            mark(mm, "row")
            need(pe, DV, "tok_f")
            for g, (o, w) in enumerate(GROUPS):
                pe.transpose(bank[1][:, o:o + w], tok_f[0:w, g, :], ident[0:w, 0:w])
                mm = pe.transpose(bank[2][:, o:o + w], by_block[0:w, g, :, 1].bitcast(F32), ident[0:w, 0:w])
            mark(mm, "lists")

        @block.gpsimd
        def _(pool):
            do = stepper(pool, PO)
            do(pool.iota(iob[:, :], pattern=[[1, NTAB]], base=0, channel_multiplier=0, allow_small_or_imprecise_dtypes=True))
            do(pool.iota(ioe[:, :], pattern=[[1, 1]], base=0, channel_multiplier=1, allow_small_or_imprecise_dtypes=True), "iota")
            do(pool.memset(list_tok[:, NTAB:LST], 0), "past")
            write_entries(pool)
            need(pool, DV, "lidx")
            pool.wait_ge(lists_written, 16 * TOPK * (NTB * NCH + 1))
            blocks = LISTS.rearrange("(r n) c -> r (n c)", n=P)
            for g, (o, w) in enumerate(GROUPS):
                pool.indirect_dma_start(out=by_block[0:w, g, :, :].rearrange("p n c -> p (n c)"), out_offset=None, in_=blocks,
                                        in_offset=bass.IndirectOffsetOnAxis(ap=lidx[0:w, g:g + 1], axis=0)).then_inc(lists_read, 16)

        @block.vector
        def _(dve):
            do = stepper(dve, DV)
            need(dve, PE, "count")
            do(dve.tensor_scalar(nbi[:, 0:1], bank[0][0:NE, 0:1], float(P - 1), None, ALU.add))
            do(dve.tensor_scalar(nbi[:, 1:2], nbi[:, 0:1], 7, None, ALU.arith_shift_right))
            do(dve.tensor_copy(nb[:, 0:1], nbi[:, 1:2]))
            do(dve.tensor_scalar(nb[:, 2:3], nb[:, 0:1], 1.0, None, ALU.min), "has")
            need(dve, PE, "end")
            do(dve.tensor_copy(nb[:, 1:2], bank[1][0:NE, 0:1]))
            need(dve, PO, "iota")
            do(dve.tensor_scalar(cmp[:, :], iob[:, :], nb[:, 1:2], None, ALU.is_ge), "cmp")
            need(dve, PE, "turn")
            do(dve.tensor_copy(nb[:, 3:4], bank[2][0:NE, 0:1]))
            do(dve.tensor_scalar(hot[:, :], iob[:, 0:NE], nb[:, 3:4], nb[:, 2:3], ALU.is_equal, ALU.mult), "hot")
            need(dve, PE, "turns")
            do(dve.tensor_copy(urow[:, 0:1], bank[5][0:1, 0:1]))
            do(dve.tensor_copy(urow[:, 1:2], bank[5][0:1, 8:9]))
            do(dve.tensor_copy(used[:, 0:2], urow[:, :]))
            need(dve, PE, "o")
            do(dve.tensor_tensor(r[0][:, :], iob[0:1, :], bank[4][0:1, 0:NTAB], ALU.subtract))
            do(dve.tensor_scalar(r[1][:, :], bank[3][0:1, 0:NTAB], float(CAP // P), None, ALU.mult))
            do(dve.tensor_tensor(r[1][:, :], r[0][:, :], r[1][:, :], ALU.add))
            do(dve.tensor_scalar(r[1][:, :], r[1][:, :], float(NE * CAP // P), None, ALU.min), "row")
            need(dve, PE, "row")
            for g, (o, w) in enumerate(GROUPS):
                do(dve.tensor_copy(lidx[0:w, g:g + 1], bank[0][0:w, g:g + 1]), "lidx")
            do(dve.tensor_scalar(urow[:, 1:2], urow[:, 1:2], -1.0, None, ALU.add))
            do(dve.tensor_scalar(r[2][:, :], bank[6][0:1, 0:NTAB], urow[:, 1:2], None, ALU.min))
            do(dve.tensor_scalar(r[5][:, :], r[2][:, :], urow[:, 1:2], None, ALU.is_lt))
            do(dve.tensor_scalar(r[2][:, :], r[2][:, :], 1.0, None, ALU.add))
            do(dve.tensor_copy(tab[:, :, NEED], r[2][:, :]))
            do(dve.tensor_tensor(r[5][:, :], r[5][:, :], r[2][:, :], ALU.mult))
            do(dve.tensor_scalar(r[4][:, :], r[0][:, :], 0.0, None, ALU.is_equal))
            do(dve.tensor_tensor(tab[:, :, SPLIT_A], r[4][:, :], r[5][:, :], ALU.mult))
            do(dve.tensor_scalar(r[0][:, :], r[0][:, :], 1.0, None, ALU.is_equal))
            do(dve.tensor_tensor(r[4][:, 0:NTAB - 1], r[4][:, 0:NTAB - 1], r[4][:, 1:NTAB], ALU.mult))
            do(dve.tensor_tensor(r[4][:, :], r[4][:, :], r[0][:, :], ALU.add))
            do(dve.tensor_tensor(tab[:, :, SPLIT_B], r[4][:, :], r[5][:, :], ALU.mult))
            need(dve, PE, "turn_e")
            do(dve.tensor_copy(turn_e[:, :], bank[7][0:1, 0:NE]))
            dve.wait_ge(lists_read, 32)
            for g, (o, w) in enumerate(GROUPS):
                do(dve.tensor_copy(tok_f[0:w, g, :], by_block[0:w, g, :, 0]), "tok_f")
            need(dve, PE, "lists")
            do(dve.tensor_copy(list_tok[:, 0:NTAB], bank[1][:, 0:NTAB]), wait=False)
            do(dve.tensor_copy(list_w[:, :], bank[2][:, 0:NTAB]))
    nc.all_engine_barrier(sems_to_clear=span)
    small_t.close()

    raw13 = sb(moe, "raw13", [P, 2, DC * 512])
    raw2 = sb(moe, "raw2", [P, 2, 2 * D])
    w13p = [sb(moe, f"w13_{n}", [P, 2 * DC, 512], F32R) for n in ("high", "low")]
    w2p = [sb(moe, f"w2_{n}", [P, 2 * 2, D], F32R) for n in ("high", "low")]
    xg = [sb(moe, f"xg{i}", [P, D]) for i in range(2)]
    xt_p = [[sb(moe, f"xt{i}_{n}", [P, DC, P], F32R) for n in ("high", "low")] for i in range(2)]
    hm = [sb(moe, f"hm{i}", [P, DE]) for i in range(2)]
    ht_p = [[sb(moe, f"ht{i}_{n}", [P, DE], F32R) for n in ("high", "low")] for i in range(2)]
    yo = [sb(moe, f"yo{i}", [P, D]) for i in range(2)]
    gidx = [sb(moe, f"gidx{i}", [P, 2], I32) for i in range(2)]
    sidx = [sb(moe, f"sidx{i}", [P, 2], I32) for i in range(2)]
    zero = sb(moe, "zero", [P, 1], I32)
    PARTS = ((0, 0), (0, 1), (1, 0))

    def sem(name):
        return top.enter_context(nc.semaphore(name))

    w13_loaded = [sem("w13_even_loaded"), sem("w13_odd_loaded")]
    w2_loaded = [sem("w2_even_loaded"), sem("w2_odd_loaded")]
    loads_done = sem("loads_done")
    w13_high = sem("w13_high")
    w13_low = sem("w13_low")
    w2_high = sem("w2_high")
    w2_low = sem("w2_low")
    idx_ready = sem("idx_ready")
    x_gathered = [sem("x0_gathered"), sem("x1_gathered")]
    x_turned = sem("x_turned")
    xt_high = sem("xt_high")
    xt_low = sem("xt_low")
    h_ready = sem("h_ready")
    gate_ready = sem("gate_ready")
    hm_ready = sem("hm_ready")
    h_turned = sem("h_turned")
    ht_high = sem("ht_high")
    ht_low = sem("ht_low")
    y_ready = sem("y_ready")
    yo_d = sem("yo_d")
    yo_a = sem("yo_a")
    y_added = [sem("y0_added"), sem("y1_added")]
    yo_free = sem("yo_free")
    NPAIR = NBLK // 2
    PIECES = 4
    HALVES = (range(0, 2), range(2, 4))

    HB = (4, 7)
    with nc.Block() as block:
        @block.sync
        def _(sp):
            w13v = t["w13"].rearrange("e (p c) n -> e p (c n)", c=DC)
            w2v = t["w2"].rearrange("e (p c) n -> e p (c n)", c=2)
            turns = sp.value_load(used[0:1, 1:2], min_val=1, max_val=NE)

            def load13(o, q):
                e = sp.value_load(turn_e[0:1, bass.ds(o, 1)], min_val=0, max_val=NE - 1)
                sp.dma_start(raw13[:, q, :], w13v[bass.ds(e, 1)].rearrange("e p n -> p (e n)")).then_inc(w13_loaded[q], 16)
                return e

            def load2(e, q):
                sp.dma_start(raw2[:, q, :], w2v[bass.ds(e, 1)].rearrange("e p n -> p (e n)")).then_inc(w2_loaded[q], 16)

            for q in range(2):
                load2(load13(q, q), q)
            with sp.Fori(1, NE // 2) as i:
                with sp.If(turns > i * 2):
                    for q in range(2):
                        sp.wait_ge(w13_low, i * 2 + q - 1)
                        e = load13(i * 2 + q, q)
                        sp.wait_ge(w2_low, i * 2 + q - 1)
                        load2(e, q)
            pairs = sp.snap((turns + 1) // 2)
            for q in range(2):
                sp.wait_ge(w13_loaded[q], pairs * 16)
                sp.wait_ge(w2_loaded[q], pairs * 16)
            sp.sem_inc(loads_done, 1)
            sp.wait_ge(loads_done, 1)
            sp.drain()

        @block.tensor
        def _(pe):
            pe.sem_inc(y_ready, 1)
            pe.sem_inc(h_ready, 1)
            n = pe.value_load(used[0:1, 0:1], min_val=1, max_val=NBLK)

            def turn_x(q):
                v = xg[q][:, :].rearrange("p (n c) -> p n c", c=DC)
                for k in range(DC):
                    mm = pe.transpose(bank[k // 4][:, (k % 4) * P:(k % 4 + 1) * P], v[:, :, k], ident[:, :])
                    if k % 4 == 3:
                        mm.then_inc(x_turned, 1)

            def turn_h(b, q):
                pe.wait_ge(hm_ready, b + 1)
                v = hm[q][:, :].rearrange("p (n c) -> p n c", c=2)
                for k in range(2):
                    mm = pe.transpose(bank[HB[q]][:, k * P:(k + 1) * P], v[:, :, k], ident[:, :])
                mm.then_inc(h_turned, 1)

            def up(b, q):
                turn = pe.value_load(tab[0:1, bass.ds(b, 1), NEED], min_val=1, max_val=NE)
                par = pe.snap((turn + 1) % 2)
                pe.wait_ge(w13_low, turn)
                pe.wait_ge(xt_low, b * 2 + 2)
                for k in range(DC):
                    for m, (xp, wp) in enumerate(PARTS):
                        mm = pe.matmul(bank[2 + q][:, :], xt_p[q][xp][:, k, :],
                                       w13p[wp][:, bass.ds(par * DC + k, 1), :].rearrange("p a n -> p (a n)"),
                                       start=(k == 0 and m == 0), stop=(k == DC - 1 and m == 2))
                mm.then_inc(h_ready, 1)

            def down(b, q):
                turn = pe.value_load(tab[0:1, bass.ds(b, 1), NEED], min_val=1, max_val=NE)
                par = pe.snap((turn + 1) % 2)
                pe.wait_ge(w2_low, turn)
                pe.wait_ge(ht_low, b + 1)
                pe.wait_ge(yo_d, b + 1)
                pe.wait_ge(yo_a, b + 1)
                for h in range(2):
                    for k in range(2):
                        for m, (xp, wp) in enumerate(PARTS):
                            mm = pe.matmul(bank[5 + h][:, :], ht_p[q][xp][:, k * P:(k + 1) * P],
                                           w2p[wp][:, bass.ds(par * 2 + k, 1), h * 512:(h + 1) * 512].rearrange("p a n -> p (a n)"),
                                           start=(k == 0 and m == 0), stop=(k == 1 and m == 2))
                mm.then_inc(y_ready, 1)

            for b in range(2):
                pe.wait_ge(x_gathered[b], 16)
                if b:
                    pe.wait_ge(xt_low, 2)
                turn_x(b)
            up(0, 0)
            pe.wait_ge(x_gathered[0], 32)
            pe.wait_ge(xt_low, 4)
            turn_x(0)
            turn_h(0, 0)
            with pe.Fori(0, NPAIR) as i:
                with pe.If(n > i * 2):
                    for s in range(2):
                        b, q = i * 2 + s + 1, 1 - s
                        up(b, q)
                        pe.wait_ge(x_gathered[q], i * 16 + 32 + 16 * s)
                        pe.wait_ge(xt_low, b * 2 + 4)
                        turn_x(q)
                        down(b - 1, s)
                        turn_h(b, q)

        @block.scalar
        def _(act):
            act.sem_inc(yo_a, 1)
            n = act.value_load(used[0:1, 0:1], min_val=1, max_val=NBLK)
            def split13(par, pieces):
                w = DC // PIECES
                for k in pieces:
                    act.activation(w13p[0][:, bass.ds(par * DC + k * w, w), :].rearrange("p a n -> p (a n)"),
                                   raw13[:, bass.ds(par, 1), k * w * 512:(k + 1) * w * 512].rearrange("p a n -> p (a n)"),
                                   ACT.Copy).then_inc(w13_high, 1)

            def split2(par):
                for k in range(2):
                    act.activation(w2p[0][:, bass.ds(par * 2 + k, 1), :].rearrange("p a n -> p (a n)"),
                                   raw2[:, bass.ds(par, 1), k * D:(k + 1) * D].rearrange("p a n -> p (a n)"),
                                   ACT.Copy).then_inc(w2_high, 1)

            def copy_x(b, q):
                for h in range(2):
                    act.wait_ge(x_turned, b * 2 + 1 + h)
                    act.activation(xt_p[q][0][:, 4 * h:4 * h + 4, :].rearrange("p a b -> p (a b)"), bank[h][:, :],
                                   ACT.Copy).then_inc(xt_high, 1)

            def next_turn(b, when, loaded, done, split, *pieces):
                turn = act.value_load(tab[0:1, bass.ds(b, 1), when], min_val=0, max_val=NE)
                with act.If(turn > 0):
                    act.wait_ge(loaded[0], act.snap((turn // 2 + 1) * 16))
                    act.wait_ge(loaded[1], act.snap(((turn + 1) // 2) * 16))
                    act.wait_ge(done, b + 1)
                    par = act.snap(turn % 2)
                    split(par, *pieces)

            def gate(b, q):
                act.wait_ge(h_ready, b + 2)
                act.activation(hm[q][:, :], bank[2 + q][:, 0:DE], ACT.Silu).then_inc(gate_ready, 1)

            act.wait_ge(w13_loaded[0], 16)
            split13(0, range(PIECES))
            act.wait_ge(w2_loaded[0], 16)
            split2(0)
            for b in range(2):
                copy_x(b, b)
            next_turn(0, SPLIT_A, w13_loaded, h_ready, split13, HALVES[0])
            gate(0, 0)
            next_turn(0, SPLIT_B, w13_loaded, h_ready, split13, HALVES[1])
            copy_x(2, 0)
            with act.Fori(0, NPAIR) as i:
                with act.If(n > i * 2):
                    for s in range(2):
                        b, q = i * 2 + s + 1, 1 - s
                        act.wait_ge(h_turned, b)
                        act.activation(ht_p[s][0][:, :], bank[HB[s]][:, 0:DE], ACT.Copy).then_inc(ht_high, 1)
                        next_turn(b, SPLIT_A, w13_loaded, h_ready, split13, HALVES[0])
                        gate(b, q)
                        next_turn(b, SPLIT_B, w13_loaded, h_ready, split13, HALVES[1])
                        copy_x(b + 2, q)
                        act.wait_ge(y_ready, b + 1)
                        act.wait_ge(yo_free, b)
                        act.activation(yo[s][:, 512:1024], bank[6][:, :], ACT.Copy,
                                       scale=list_w[:, bass.ds(b - 1, 1)]).then_inc(yo_a, 1)
                        next_turn(b - 1, SPLIT_B, w2_loaded, y_ready, split2)

        @block.vector
        def _(dve):
            dve.sem_inc(yo_d, 1)
            n = dve.value_load(used[0:1, 0:1], min_val=1, max_val=NBLK)

            def split13(par, turn, pieces):
                w = DC // PIECES
                for k in pieces:
                    dve.wait_ge(w13_high, turn * PIECES + k + 1)
                    at = bass.ds(par * DC + k * w, w)
                    low = dve.tensor_tensor(w13p[1][:, at, :].rearrange("p a n -> p (a n)"),
                                            raw13[:, bass.ds(par, 1), k * w * 512:(k + 1) * w * 512].rearrange("p a n -> p (a n)"),
                                            w13p[0][:, at, :].rearrange("p a n -> p (a n)").bitcast(F32), ALU.subtract)
                if k == PIECES - 1:
                    low.then_inc(w13_low, 1)

            def split2(par, turn):
                for k in range(2):
                    dve.wait_ge(w2_high, turn * 2 + k + 1)
                    at = bass.ds(par * 2 + k, 1)
                    low = dve.tensor_tensor(w2p[1][:, at, :].rearrange("p a n -> p (a n)"),
                                            raw2[:, bass.ds(par, 1), k * D:(k + 1) * D].rearrange("p a n -> p (a n)"),
                                            w2p[0][:, at, :].rearrange("p a n -> p (a n)").bitcast(F32), ALU.subtract)
                low.then_inc(w2_low, 1)

            def copy_x(b, q):
                for h in range(2):
                    dve.wait_ge(xt_high, b * 2 + 1 + h)
                    dve.tensor_tensor(xt_p[q][1][:, 4 * h:4 * h + 4, :].rearrange("p a b -> p (a b)"), bank[h][:, :],
                                      xt_p[q][0][:, 4 * h:4 * h + 4, :].rearrange("p a b -> p (a b)").bitcast(F32),
                                      ALU.subtract).then_inc(xt_low, 1)

            def next_turn(b, when, split, *pieces):
                turn = dve.value_load(tab[0:1, bass.ds(b, 1), when], min_val=0, max_val=NE)
                with dve.If(turn > 0):
                    par = dve.snap(turn % 2)
                    split(par, turn, *pieces)

            def times_up(b, q):
                dve.wait_ge(gate_ready, b + 1)
                dve.tensor_tensor(hm[q][:, :], hm[q][:, :], bank[2 + q][:, DE:2 * DE], ALU.mult).then_inc(hm_ready, 1)

            split13(0, 0, range(PIECES))
            split2(0, 0)
            for b in range(2):
                copy_x(b, b)
            next_turn(0, SPLIT_A, split13, HALVES[0])
            times_up(0, 0)
            next_turn(0, SPLIT_B, split13, HALVES[1])
            copy_x(2, 0)
            with dve.Fori(0, NPAIR) as i:
                with dve.If(n > i * 2):
                    for s in range(2):
                        b, q = i * 2 + s + 1, 1 - s
                        dve.wait_ge(ht_high, b)
                        dve.tensor_tensor(ht_p[s][1][:, :], bank[HB[s]][:, 0:DE], ht_p[s][0][:, :].bitcast(F32),
                                          ALU.subtract).then_inc(ht_low, 1)
                        next_turn(b, SPLIT_A, split13, HALVES[0])
                        times_up(b, q)
                        next_turn(b, SPLIT_B, split13, HALVES[1])
                        copy_x(b + 2, q)
                        dve.wait_ge(y_ready, b + 1)
                        dve.wait_ge(yo_free, b)
                        dve.tensor_scalar(yo[s][:, 0:512], bank[5][:, :], list_w[:, bass.ds(b - 1, 1)], None,
                                          ALU.mult).then_inc(yo_d, 1)
                        next_turn(b - 1, SPLIT_B, split2)

        @block.gpsimd
        def _(pool):
            pool.sem_inc(yo_free, 2)
            n = pool.value_load(used[0:1, 0:1], min_val=1, max_val=NBLK)
            pool.memset(zero[:, :], 0).then_inc(idx_ready, 1)
            pool.wait_ge(idx_ready, 1)
            pool.sem_clear(idx_ready)

            def places(dst, b):
                pool.tensor_copy(dst[:, 1:2], list_tok[:, bass.ds(b, 1)]).then_inc(idx_ready, 1)
                pool.wait_ge(idx_ready, 1)

            def gather(q):
                pool.tensor_tensor(gidx[q][:, 0:1], gidx[q][:, 1:2], zero[:, :], ALU.add).then_inc(idx_ready, 1)
                pool.wait_ge(idx_ready, 2)
                pool.indirect_dma_start(out=xg[q][:, :], out_offset=None, in_=U2[:, :],
                                        in_offset=bass.IndirectOffsetOnAxis(ap=gidx[q][:, 0:1], axis=0)).then_inc(x_gathered[q], 16)
                pool.sem_clear(idx_ready)

            for b in range(5):
                places(gidx[b % 2], b)
                if b >= 2:
                    pool.wait_ge(x_turned, 2 * b - 2)
                    pool.wait_ge(x_gathered[b % 2], 16 * (b // 2))
                gather(b % 2)
            with pool.Fori(0, NPAIR) as i:
                with pool.If(n > i * 2):
                    for q in range(2):
                        b = i * 2 + q
                        places(sidx[q], b)
                        pool.wait_ge(yo_d, b + 2)
                        pool.wait_ge(yo_a, b + 2)
                        pool.tensor_tensor(sidx[q][:, 0:1], sidx[q][:, 1:2], zero[:, :], ALU.add).then_inc(idx_ready, 1)
                        pool.wait_ge(idx_ready, 2)
                        pool.indirect_dma_start(out=YACC[:, :], out_offset=bass.IndirectOffsetOnAxis(ap=sidx[q][:, 0:1], axis=0),
                                                in_=yo[q][:, :], in_offset=None, compute_op=ALU.add).then_inc(y_added[q], 16)
                        pool.sem_clear(idx_ready)
                        places(gidx[1 - q], b + 5)
                        pool.wait_ge(x_turned, b * 2 + 8)
                        pool.wait_ge(x_gathered[1 - q], i * 16 + 32 + 16 * q)
                        gather(1 - q)
                        pool.wait_ge(y_added[q], (i + 1) * 16)
                        pool.sem_inc(yo_free, 1)
            pairs = pool.snap((n + 1) // 2)
            for q in range(2):
                pool.wait_ge(y_added[q], pairs * 16)
                pool.wait_ge(x_gathered[q], pairs * 16 + (48, 32)[q])
            pool.tensor_tensor(zero[:, :], gidx[0][:, 1:2], gidx[0][:, 1:2], ALU.subtract).then_inc(idx_ready, 1)
            pool.wait_ge(idx_ready, 1)
    moe.close()

    fin = ExitStack()
    NT = SEQ // P
    NB4 = 4
    xa = sb(fin, "xa", [P, NB4, D])
    yy = sb(fin, "yy", [P, NB4, D])
    ln2g = sb(fin, "ln2g", [P, D])
    ln2b = sb(fin, "ln2b", [P, D])
    fs = sb(fin, "fs", [P, NB4, 18])
    ln_loaded = sem("ln_loaded")
    rows_in = [sem(f"rows_in{q}") for q in range(NB4)]
    tile_stats = sem("tile_stats")
    tile_std = sem("tile_std")
    tile_shift = sem("tile_shift")
    tile_normed = sem("tile_normed")
    tile_scaled = sem("tile_scaled")
    tile_done = sem("tile_done")
    rows_out = [sem(f"rows_out{q}") for q in range(NB4)]
    own = sem("final_steps")
    with nc.Block() as block:
        def tile_rows(b):
            return bass.ds(b * P, P)

        @block.sync
        def _(sp):
            def load(b, q):
                sp.dma_start(xa[:, q, :], X1[tile_rows(b), :]).then_inc(rows_in[q], 16)
                sp.dma_start(yy[:, q, :], YACC[tile_rows(b), :]).then_inc(rows_in[q], 16)

            for q in range(NB4):
                load(q, q)
                if q == 0:
                    sp.dma_start(ln2g[:, :], t["ln2_g"][0, :].partition_broadcast(P)).then_inc(ln_loaded, 16)
                    sp.dma_start(ln2b[:, :], t["ln2_b"][0, :].partition_broadcast(P)).then_inc(ln_loaded, 16)

            def finish(i, q):
                b = i * NB4 + q
                sp.wait_ge(tile_done, b + 1)
                sp.dma_start(t["out"][tile_rows(b), :], xa[:, q, :]).then_inc(rows_out[q], 16)
                if isinstance(i, int) and (b == 0 or b + NB4 > NT):
                    return
                before = (q - 1) % NB4
                sp.wait_ge(rows_out[before], (i if q == 0 else i + 1) * 16)
                load(b + NB4 - 1, before)

            for q in range(NB4):
                finish(0, q)
            with sp.Fori(1, NT // NB4 - 1) as i:
                for q in range(NB4):
                    finish(i, q)
            for q in range(NB4):
                finish(NT // NB4 - 1, q)
            for q in range(NB4):
                sp.wait_ge(rows_out[q], 16 * NT // NB4)
            sp.drain()

        @block.scalar
        def _(act):
            with act.Fori(0, NT // NB4) as i:
                for q in range(NB4):
                    b = i * NB4 + q
                    act.wait_ge(tile_stats, b + 1)
                    act.activation(fs[:, q, 14:15], fs[:, q, 13:14], ACT.Sqrt, bias=epsc[:, 0:1]).then_inc(tile_std, 1)
                    act.wait_ge(tile_shift, b + 1)
                    act.activation(xa[:, q, :], xa[:, q, :], ACT.Identity, bias=fs[:, q, 16:17],
                                   scale=fs[:, q, 15:16]).then_inc(tile_normed, 1)

        @block.gpsimd
        def _(pool):
            pool.wait_ge(ln_loaded, 32)
            with pool.Fori(0, NT // NB4) as i:
                for q in range(NB4):
                    pool.wait_ge(tile_normed, i * NB4 + q + 1)
                    pool.tensor_tensor(yy[:, q, :], xa[:, q, :], ln2g[:, :], ALU.mult).then_inc(tile_scaled, 1)
                    pool.wait_ge(tile_scaled, i * NB4 + q + 1)
                    pool.tensor_tensor(xa[:, q, :], yy[:, q, :], ln2b[:, :], ALU.add).then_inc(tile_done, 1)

        @block.vector
        def _(dve):
            with dve.Fori(0, NT // NB4) as i:
                for q in range(NB4):
                    b = i * NB4 + q
                    x, y = xa[:, q, :], yy[:, q, :]
                    st, mv, sd, rs, nm = fs[:, q, 0:12], fs[:, q, 12:14], fs[:, q, 14:15], fs[:, q, 15:16], fs[:, q, 16:17]
                    n = [0]

                    def do(ins, wait=True):
                        ins.then_inc(own, 1)
                        n[0] += 1
                        if wait:
                            dve.wait_ge(own, n[0])
                    dve.wait_ge(rows_in[q], i * 32 + 32)
                    do(dve.tensor_tensor(y, y, g2p1[:, :], ALU.mult))
                    do(dve.scalar_tensor_tensor(out=x, in0=x, scalar=ALPHA, in1=y, op0=ALU.mult, op1=ALU.add))
                    do(dve.bn_stats(st[:, 0:6], x[:, 0:512]), wait=False)
                    do(dve.bn_stats(st[:, 6:12], x[:, 512:1024]))
                    dve.bn_aggr(mv, st).then_inc(tile_stats, 1)
                    dve.wait_ge(tile_std, b + 1)
                    do(dve.reciprocal(rs, sd))
                    dve.scalar_tensor_tensor(out=nm, in0=mv[:, 0:1], scalar=-1.0, in1=rs, op0=ALU.mult, op1=ALU.mult)\
                        .then_inc(tile_shift, 1)
                    dve.sem_clear(own)
    fin.close()
    top.close()


_CHANNEL = [n for n in CV]
_TILES = [8, 9, 10, 11, 12, 13, 14, 2, 0, 3, 1, 4, 5, 6, 7, 15, 16, 17, 18, 19, 20]


def kernel(**inputs):
    import numpy as _np
    import concourse.bacc as _bacc
    from concourse import mybir as _mybir
    from concourse.bass_utils import run_bass_kernel_spmd as _run

    x = {k: _np.asarray(v) for k, v in inputs.items()}
    arrays = {
        "x": x["x"][0],
        "xt": x["x"][0].T.reshape(P, DC, SEQ),
        "c": x["c"],
        "w_in": x["w_in"][0].reshape(P, DC, NPT, P)[:, :, _TILES].reshape(P, DC, NGRP, GRP * P).transpose(0, 2, 1, 3),
        "chan": _np.concatenate([x[n][0].reshape(-1, P) for n in _CHANNEL]).T,
        "lora": _np.concatenate([x[n][0] for n in ("w_w2", "w_a2", "w_g2")]),
    }
    for n in ("w_mod", "w_out", "w_rg", "w_ig", "w_router", "w13", "w2", "ws13", "ws2"):
        arrays[n] = x[n][0]
    for n in ("b_mod", "e_bias", "ln1_g", "ln1_b", "ln2_g", "ln2_b"):
        arrays[n] = x[n]
    arrays = {f"in_{k}": _np.ascontiguousarray(v) for k, v in arrays.items()}
    for Count.final in (False, True):
        nc = _bacc.Bacc("TRN2", target_bir_lowering=False, num_devices=1)
        t = {k[3:]: nc.dram_tensor(k, a.shape, _mybir.dt.from_np(a.dtype), kind="ExternalInput").ap() for k, a in arrays.items()}
        t["out"] = nc.dram_tensor("out_rows", (SEQ, D), F32, kind="ExternalOutput").ap()
        build(nc, t)
    r = _run(nc, [arrays], core_ids=[0])
    return r.results[0]["out_rows"].reshape(x["x"].shape)
```
